# Optimizing a Trainium2 kernel written in Bass

```python
import jax, jax.numpy as jnp
from jax import lax
import numpy as np

D_MODEL = 1024
BATCH = 1
SEQ = 512
DEPTH = 1
DEC_BATCH = 8
DEC_SEQ = 4
PAST_LEN = 4096
PAGE_SIZE = 128

W_MIX = 512
N_BRANCH = 4
RG_BLOCKS = 8
RG_BLOCK = W_MIX // RG_BLOCKS
RG_CONV = 4
RG_C = 8.0
CONF_CONV = 31
POOL_WINDOWS = (2, 4, 8, 16)
POOL_GROUPS = len(POOL_WINDOWS)
POOL_GW = W_MIX // POOL_GROUPS
POOL_BUF = max(POOL_WINDOWS) - 1
SC_CONV = 3
D_FF = -(-8 * D_MODEL // (3 * 256)) * 256
IN_COLS = 8 * W_MIX + N_BRANCH * D_MODEL
ALPHA = (2 * DEPTH) ** 0.25
BETA = (8 * DEPTH) ** -0.25
LN_EPS = 1e-5

kernel_name = "hybrid_rglru_conformer_pool_shortconv_decode_step"

def layer_norm(x, g, b):
    xf = x.astype(jnp.float32)
    mu = jnp.mean(xf, axis=-1, keepdims=True)
    var = jnp.mean(jnp.square(xf - mu), axis=-1, keepdims=True)
    y = (xf - mu) * lax.rsqrt(var + LN_EPS) * g.astype(jnp.float32) + b.astype(jnp.float32)
    return y.astype(x.dtype)

def causal_dwconv(buf, x, w):
    xp = jnp.concatenate([buf.astype(x.dtype), x], axis=1)
    y = lax.conv_general_dilated(xp, w[:, None, :].astype(x.dtype), window_strides=(1,), padding="VALID",
                                 dimension_numbers=("NWC", "WIO", "NWC"), feature_group_count=x.shape[-1])
    return y, xp[:, -(w.shape[0] - 1):]

def rg_lru(x, h0, w_a, b_a, w_x, b_x, lam):
    bsz, t = x.shape[0], x.shape[1]
    xb = x.reshape(bsz, t, RG_BLOCKS, RG_BLOCK)
    r = jax.nn.sigmoid(jnp.einsum('btnc,ncd->btnd', xb, w_a).reshape(bsz, t, W_MIX) + b_a)
    i = jax.nn.sigmoid(jnp.einsum('btnc,ncd->btnd', xb, w_x).reshape(bsz, t, W_MIX) + b_x)
    log_a = -RG_C * r.astype(jnp.float32) * jax.nn.softplus(-lam.astype(jnp.float32))
    a = jnp.exp(log_a)
    mult = jnp.sqrt(-jnp.expm1(2.0 * log_a))
    b = mult * (i * x).astype(jnp.float32)
    b = b.at[:, 0].add(a[:, 0] * h0.astype(jnp.float32))

    def combine(left, right):
        return (left[0] * right[0], right[0] * left[1] + right[1])

    _, h = lax.associative_scan(combine, (a, b), axis=1)
    return h.astype(x.dtype), h[:, -1].astype(x.dtype)

def pool_mixer(buf, c, start, pool_w, pool_scale):
    bsz, t = c.shape[0], c.shape[1]
    p = jnp.concatenate([buf.astype(c.dtype), c], axis=1).astype(jnp.float32)
    cs = jnp.concatenate([jnp.zeros_like(p[:, :1]), jnp.cumsum(p, axis=1)], axis=1)
    pos = start + jnp.arange(t)
    outs = []
    for g, w in enumerate(POOL_WINDOWS):
        sl = slice(g * POOL_GW, (g + 1) * POOL_GW)
        hi = cs[:, POOL_BUF + 1:POOL_BUF + 1 + t, sl]
        lo = cs[:, POOL_BUF + 1 - w:POOL_BUF + 1 - w + t, sl]
        cnt = jnp.minimum(w, pos + 1).astype(jnp.float32)[None, :, None]
        outs.append((hi - lo) / cnt - p[:, POOL_BUF:, sl])
    m = jnp.concatenate(outs, axis=-1).astype(c.dtype).reshape(bsz, t, POOL_GROUPS, POOL_GW)
    y = jnp.einsum('btgc,gcd->btgd', m, pool_w).reshape(bsz, t, W_MIX) * pool_scale
    return y, p[:, -POOL_BUF:].astype(c.dtype)

def run_layer(x, h0, rg_buf, cf_buf, pool_buf, sc_buf, start,
              w_in, rg_conv_w, rg_conv_b, rg_w_a, rg_b_a, rg_w_x, rg_b_x, rg_lambda,
              cf_conv_w, cf_conv_b, cf_ln_g, cf_ln_b, pool_w, pool_scale, sc_conv_w,
              w_branch, w_out, ln1_g, ln1_b, w_ff_gate, w_ff_up, w_ff_down, ln2_g, ln2_b):
    z = x @ w_in
    a_x, a_gate, b_val, b_gate, c_in, d_b, d_c, d_h, gates = jnp.split(
        z, [W_MIX * k for k in range(1, 9)], axis=-1)
    a_conv, rg_buf_new = causal_dwconv(rg_buf, a_x, rg_conv_w)
    a_h, h_new = rg_lru(a_conv + rg_conv_b, h0, rg_w_a, rg_b_a, rg_w_x, rg_b_x, rg_lambda)
    y_a = a_h * jax.nn.gelu(a_gate)
    glu = b_val * jax.nn.sigmoid(b_gate)
    b_conv, cf_buf_new = causal_dwconv(cf_buf, glu, cf_conv_w)
    y_b = jax.nn.silu(layer_norm(b_conv + cf_conv_b, cf_ln_g, cf_ln_b))
    y_c, pool_buf_new = pool_mixer(pool_buf, c_in, start, pool_w, pool_scale)
    sc_conv, sc_buf_new = causal_dwconv(sc_buf, d_c * d_h, sc_conv_w)
    y_d = d_b * sc_conv
    gate_parts = jnp.split(gates, N_BRANCH, axis=-1)
    branches = (y_a, y_b, y_c, y_d)
    merged = jax.nn.sigmoid(gate_parts[0]) * (branches[0] @ w_branch[0])
    for n in range(1, N_BRANCH):
        merged = merged + jax.nn.sigmoid(gate_parts[n]) * (branches[n] @ w_branch[n])
    x = layer_norm(ALPHA * x + merged @ w_out, ln1_g, ln1_b)
    f = (jax.nn.silu(x @ w_ff_gate) * (x @ w_ff_up)) @ w_ff_down
    x = layer_norm(ALPHA * x + f, ln2_g, ln2_b)
    return x, h_new, rg_buf_new, cf_buf_new, pool_buf_new, sc_buf_new

def setup_inputs(seed: int = 0) -> dict:
    key = jax.random.key(seed)
    ks = iter(jax.random.split(key, 40))
    nrm = lambda shape, s: jax.random.normal(next(ks), shape, jnp.float32) * s
    u = jax.random.uniform(next(ks), (DEPTH, W_MIX), jnp.float32, 0.9, 0.999)
    a_base = u ** (1.0 / RG_C)
    rg_lambda = jnp.log(a_base) - jnp.log1p(-a_base)
    return {
        "x_prompt": nrm((BATCH, SEQ, D_MODEL), 1.0),
        "x_sample": nrm((DEC_BATCH, DEC_SEQ, D_MODEL), 1.0),
        "state_rglru_h": nrm((DEPTH, DEC_BATCH, W_MIX), 0.5),
        "state_rglru_conv": nrm((DEPTH, DEC_BATCH, RG_CONV - 1, W_MIX), 1.0),
        "state_conformer_conv": nrm((DEPTH, DEC_BATCH, CONF_CONV - 1, W_MIX), 0.5),
        "state_pool": nrm((DEPTH, DEC_BATCH, POOL_BUF, W_MIX), 1.0),
        "state_shortconv": nrm((DEPTH, DEC_BATCH, SC_CONV - 1, W_MIX), 1.0),
        "w_in": nrm((DEPTH, D_MODEL, IN_COLS), D_MODEL ** -0.5),
        "rg_conv_w": nrm((DEPTH, RG_CONV, W_MIX), RG_CONV ** -0.5),
        "rg_conv_b": nrm((DEPTH, W_MIX), 0.01),
        "rg_w_a": nrm((DEPTH, RG_BLOCKS, RG_BLOCK, RG_BLOCK), RG_BLOCK ** -0.5),
        "rg_b_a": nrm((DEPTH, W_MIX), 0.01),
        "rg_w_x": nrm((DEPTH, RG_BLOCKS, RG_BLOCK, RG_BLOCK), RG_BLOCK ** -0.5),
        "rg_b_x": nrm((DEPTH, W_MIX), 0.01),
        "rg_lambda": rg_lambda,
        "cf_conv_w": nrm((DEPTH, CONF_CONV, W_MIX), CONF_CONV ** -0.5),
        "cf_conv_b": nrm((DEPTH, W_MIX), 0.01),
        "cf_ln_g": 1.0 + nrm((DEPTH, W_MIX), 0.02),
        "cf_ln_b": nrm((DEPTH, W_MIX), 0.02),
        "pool_w": nrm((DEPTH, POOL_GROUPS, POOL_GW, POOL_GW), POOL_GW ** -0.5),
        "pool_scale": 1.0 + nrm((DEPTH, W_MIX), 0.1),
        "sc_conv_w": nrm((DEPTH, SC_CONV, W_MIX), SC_CONV ** -0.5),
        "w_branch": nrm((DEPTH, N_BRANCH, W_MIX, D_MODEL), BETA * W_MIX ** -0.5),
        "w_out": nrm((DEPTH, D_MODEL, D_MODEL), BETA * D_MODEL ** -0.5),
        "ln1_g": 1.0 + nrm((DEPTH, D_MODEL), 0.02),
        "ln1_b": nrm((DEPTH, D_MODEL), 0.02),
        "w_ff_gate": nrm((DEPTH, D_MODEL, D_FF), D_MODEL ** -0.5),
        "w_ff_up": nrm((DEPTH, D_MODEL, D_FF), D_MODEL ** -0.5),
        "w_ff_down": nrm((DEPTH, D_FF, D_MODEL), BETA * D_FF ** -0.5),
        "ln2_g": 1.0 + nrm((DEPTH, D_MODEL), 0.02),
        "ln2_b": nrm((DEPTH, D_MODEL), 0.02),
    }

def reference(x_prompt, x_sample, state_rglru_h, state_rglru_conv, state_conformer_conv, state_pool,
              state_shortconv, w_in, rg_conv_w, rg_conv_b, rg_w_a, rg_b_a, rg_w_x, rg_b_x, rg_lambda,
              cf_conv_w, cf_conv_b, cf_ln_g, cf_ln_b, pool_w, pool_scale, sc_conv_w, w_branch, w_out,
              ln1_g, ln1_b, w_ff_gate, w_ff_up, w_ff_down, ln2_g, ln2_b):
    weights = (w_in, rg_conv_w, rg_conv_b, rg_w_a, rg_b_a, rg_w_x, rg_b_x, rg_lambda,
               cf_conv_w, cf_conv_b, cf_ln_g, cf_ln_b, pool_w, pool_scale, sc_conv_w,
               w_branch, w_out, ln1_g, ln1_b, w_ff_gate, w_ff_up, w_ff_down, ln2_g, ln2_b)
    bp = x_prompt.shape[0]
    dt = x_prompt.dtype
    yp, ys = x_prompt, x_sample
    p_new = [[] for _ in range(5)]
    s_new = [[] for _ in range(5)]
    for l in range(DEPTH):
        wl = [w[l] for w in weights]
        zero_states = (jnp.zeros((bp, W_MIX), dt),
                       jnp.zeros((bp, RG_CONV - 1, W_MIX), dt),
                       jnp.zeros((bp, CONF_CONV - 1, W_MIX), dt),
                       jnp.zeros((bp, POOL_BUF, W_MIX), dt),
                       jnp.zeros((bp, SC_CONV - 1, W_MIX), dt))
        outp = run_layer(yp, *zero_states, 0, *wl)
        outs = run_layer(ys, state_rglru_h[l], state_rglru_conv[l], state_conformer_conv[l],
                         state_pool[l], state_shortconv[l], PAST_LEN, *wl)
        yp, ys = outp[0], outs[0]
        for k in range(5):
            p_new[k].append(outp[k + 1])
            s_new[k].append(outs[k + 1])
    p_h, p_rgc, p_cf, p_pool, p_sc = [jnp.stack(v, axis=0) for v in p_new]
    s_h, s_rgc, s_cf, s_pool, s_sc = [jnp.stack(v, axis=0) for v in s_new]
    return (yp, ys, p_h, p_rgc, p_cf, p_pool, p_sc, s_h, s_rgc, s_cf, s_pool, s_sc)


_drawn_inputs = setup_inputs


def setup_inputs(seed=0):
    import zlib

    import numpy as np

    out = dict(_drawn_inputs(seed))
    spreads = {}
    factors = {'rg_b_a': 26.544,
     'rg_b_x': 8.0,
     'cf_conv_b': 8.0,
     'cf_ln_g': 31.464,
     'cf_ln_b': 31.41,
     'pool_scale': 4.102,
     'ln1_g': 2.74,
     'ln1_b': 2.691,
     'ln2_g': 8.537,
     'ln2_b': 8.088}
    for name, (base, spread) in spreads.items():
        noise = np.random.default_rng([zlib.crc32(name.encode()), seed]).standard_normal(out[name].shape)
        drawn = base * np.exp(spread * noise) if base else spread * noise
        out[name] = __import__('jax').numpy.asarray(drawn.astype(out[name].dtype))
    for name, factor in factors.items():
        out[name] = (out[name] * factor).astype(out[name].dtype)
    return out
```

```python
from contextlib import ExitStack

import concourse.bass as bass
from concourse import mybir

F32 = mybir.dt.float32
F32R = mybir.dt.float32r
ALU = mybir.AluOpType
ACT = mybir.ActivationFunctionType
ds = bass.ds

P = 128
D = 1024
W = 512
SEQ = 512
B, T = 8, 4
NT = SEQ + B * T
HALF = NT // 2
FF = 2816
KD, KW, KF = D // P, W // P, FF // P
RING = 4
RG_TAPS, CF_TAPS, SC_TAPS, POOL_BUF = 4, 31, 3, 15
ALPHA = 2.0 ** 0.25
EPS = 1e-5

A_X, A_GATE, B_VAL, B_GATE, C_IN, D_B, D_C, D_H = range(8)
IN_ORDER = (B_VAL, B_GATE, D_C, D_H, D_B, C_IN, A_X, A_GATE)
GATE_COL = 8 * W
BRANCH_ORDER = (3, 2, 0, 1)

U_MIX = KW * 8
U_OUT = U_MIX + 4 * 2 * KD
U_FF = U_OUT + KD
U_DOWN = U_FF + 2 * KF
DOWN_SPLIT = (8, 8, KF - 16)
U_END = U_DOWN + 3 * KD

M_CONV, M_SC, M_H = 0, B * (RG_TAPS - 1), B * (RG_TAPS - 1) + B * (SC_TAPS - 1)
V_RGW = M_H + B
V_RGB, V_BA, V_BX, V_LAM = V_RGW + 4, V_RGW + 5, V_RGW + 6, V_RGW + 7
V_CFW = V_RGW + 8
V_CFB = V_CFW + CF_TAPS
V_CFG, V_CFLB, V_PSC = V_CFB + 1, V_CFB + 2, V_CFB + 3
V_SCW = V_CFB + 4
M_ROWS = V_SCW + SC_TAPS
CONF_TAPS_1, CONF_TAPS_2 = 14, 26


class Chain:

    def __init__(self, eng, sem):
        self.eng, self.sem, self.base, self.local = eng, sem, 0, 0
        self.start = 0

    def link(self, ins):
        ins.then_inc(self.sem, 1)
        self.local += 1
        return self.base + self.local

    def after(self, value):
        self.eng.wait_ge(self.sem, value)

    def enter(self, i, per):
        self.start += self.local if isinstance(self.base, int) else 0
        self.base, self.local, self.per = i * per + self.start, 0, per

    def leave(self, count):
        assert self.local == self.per, (self.local, self.per)
        self.start += self.per * count
        self.base, self.local = self.start, 0

    def flush(self):
        self.start += self.local
        self.base, self.local = self.start, 0


def build(nc, i_, o_):
    with ExitStack() as ctx:
        def sem(name):
            return ctx.enter_context(nc.semaphore(name))

        CH = NT * 4
        base = (nc.sbuf_base + 63) // 64 * 64
        top = [base]

        def take(nbytes):
            at = top[0]
            top[0] += (nbytes + 31) // 32 * 32
            assert top[0] <= nc.sbuf_usable_end, (name_of[0], top[0])
            return at

        name_of = [""]

        def at(name, shape, dt, offset):
            name_of[0] = name
            return nc.alloc_sbuf_tensor_at(name, shape, dt, offset=offset)

        def new(name, shape, dt):
            n = 4
            for s in shape[1:]:
                n *= s
            name_of[0] = name
            return at(name, shape, dt, take(n))

        x_hi = new("x_hi", [P, KD, NT], F32R)
        x_lo = new("x_lo", [P, KD, NT], F32R)
        raw = [new(f"raw{s}", [P, 8, P], F32) for s in range(RING)]
        w_hi = [new(f"w_hi{s}", [P, 8, P], F32R) for s in range(RING)]
        w_lo = [new(f"w_lo{s}", [P, 8, P], F32R) for s in range(RING)]
        at_f = take(KD * CH)
        at_s = take(4 * CH)
        ident = new("ident", [P, P], F32)
        ones = new("ones", [P, P], F32)
        miscT = new("miscT", [P, KW, M_ROWS], F32)
        confT = new("confT", [P, KW, B * 30], F32)
        poolT = new("poolT", [P, KW, B * POOL_BUF], F32)
        lnT = new("lnT", [P, 32], F32)
        inv_count = new("inv_count", [P, KW, POOL_BUF], F32)
        widen = new("widen", [P, KW, 4], F32)
        spv = new("spv", [P, 8, KW], F32)
        h_last = new("h_last", [P, KW, 1 + B], F32)
        at_r = top[0]

        merged = at("merged", [P, KD, NT], F32, at_f)
        S = [at(f"scr{j}", [P, NT], F32, at_s + j * CH) for j in range(4)]

        y = [new(f"y{j}", [P, 2 * KW, NT], F32R) for j in range(3)]
        xc = new("xc", [P, KW, NT], F32)
        agate = new("agate", [P, KW, NT], F32)
        bconv = new("bconv", [P, KW, NT], F32)
        sm_hi = new("sm_hi", [P, 12, P], F32R)
        sm_lo = new("sm_lo", [P, 12, P], F32R)
        at_st = take(4 * 128 * 10 )
        at_u = take(6 * CH)
        st_s = at("st_s", [120, 3 * P], F32, at_st)
        st_p = at("st_p", [30, 4 * P], F32, at_st + 4 * 3 * P)
        st_ax = at("st_ax", [24, P], F32, at_st + 4 * 7 * P)
        st_sc = at("st_sc", [16, P], F32, at_st + 4 * 8 * P)
        sig = [at(f"sig{j}", [P, NT], F32, at_st + j * CH) for j in range(2)]
        sq_th = at("sq_th", [P, KW, NT], F32, at_u)
        pool_t = at("pool_t", [P, KW, NT], F32, at_u)
        bsq = at("bsq", [P, KW, NT], F32, at_u)
        packed = at("packed", [P, 400], F32, at_u)
        rgate = at("rgate", [P, NT], F32, at_u + 4 * CH)
        prod = at("prod", [P, NT], F32, at_u + 5 * CH)
        Y_D, Y_C, Y_A = y
        at_y = at_r
        th = at("th", [P, KW, NT], F32, at_y)
        igate = at("igate", [P, KW, NT], F32, at_y + KW * CH)
        h_rows = at("h_rows", [1 + B, W], F32, at_u + 4 * CH)
        h_hi = at("h_hi", [P, KF, NT], F32R, at_r)
        h_lo = at("h_lo", [P, KF, NT], F32R, at_r + KF * CH)
        assert at_r + 2 * KF * CH <= nc.sbuf_usable_end
        y_tok = at("y_tok", [P, SEQ // P, D], F32, at_r)
        ys_tok = at("ys_tok", [B * T, D], F32, at_r + SEQ // P * D * 4)
        x_tok = at("x_tok", [P, SEQ // P, D], F32, at_y)
        at_i = at_y + SEQ // P * D * 4
        xs_tok = at("xs_tok", [B * T, D], F32, at_i)
        misc_tok = at("misc_tok", [M_ROWS, W], F32, at_i + 4 * D)
        conf_tok = at("conf_tok", [120, 2, W], F32, at_i + 4 * D + 4 * W)
        pool_tok = at("pool_tok", [120, W], F32, at_i + 4 * D + 12 * W)
        ln_tok = at("ln_tok", [32, P], F32, at_i + 4 * D + 16 * W)
        sm_raw = at("sm_raw", [P, 12, P], F32, at_i + 4 * D + 16 * W + 4 * P)
        assert at_i + 4 * D + 16 * W + 4 * P + 48 * P <= at_y + 6 * KW * CH
        PAD_A, PAD_B, PAD_C, PAD_D = RG_TAPS - 1, CF_TAPS - 1, POOL_BUF, SC_TAPS - 1
        t2 = [at_f]

        def pad(name, n, dt=F32):
            off = t2[0]
            t2[0] += (4 * n + 31) // 32 * 32
            assert t2[0] <= at_s + 4 * CH, name
            return at(name, [P, n], dt, off)

        def padded(w):
            return w + SEQ + B * (w + T)

        ax_pad = pad("ax_pad", padded(PAD_A))
        glu_pad = pad("glu_pad", padded(PAD_B))
        cin_pad = pad("cin_pad", padded(PAD_C))
        dch_pad = pad("dch_pad", padded(PAD_D))
        b_val, b_sig, d_b, d_c = (pad(n, NT) for n in ("b_val", "b_sig", "d_b", "d_c"))
        acc = [pad(f"acc{j}", padded(PAD_C)) for j in range(2)]

        main = ctx.enter_context(nc.psum_tensor("main", [P, 4, 512], F32))
        aux = ctx.enter_context(nc.psum_tensor("aux", [P, 4, 512], F32))

        def slot(s):
            return main[:, 2 * s:2 * s + 2, 0:HALF]

        def aslot(s):
            return aux[:, 2 * s:2 * s + 2, 0:HALF]

        def halves(ap):
            return ap.rearrange("p (h n) -> p h n", h=2)

        def steps(ap):
            return ap.rearrange("p (b t) -> p b t", b=B)

        def pr(buf, w, first, n=SEQ):
            return buf[:, first:first + n]

        def sa(buf, w, first, n=T, b0=0, b1=B):
            return steps(buf[:, w + SEQ:w + SEQ + B * (w + T)])[:, b0:b1, first:first + n]

        x_landed = [sem(f"x_landed{j}") for j in range(5)]
        small_landed = sem("small_landed")
        sm_zeroed = sem("sm_zeroed")
        sm_landed = sem("sm_landed")
        sm_hi_ready, sm_lo_ready = sem("sm_hi_ready"), sem("sm_lo_ready")
        consts = sem("consts")
        ident_ready = sem("ident_ready")
        turned = sem("turned")
        x_hi_ready, x_lo_ready = sem("x_hi_ready"), sem("x_lo_ready")
        misc_ready, conf_ready = sem("misc_ready"), sem("conf_ready")
        lam_ready, z_ready = sem("lam_ready"), sem("z_ready")
        raw_landed = [sem(f"raw_landed{s}") for s in range(RING)]
        w_hi_ready, w_lo_ready = sem("w_hi_ready"), sem("w_lo_ready")
        unit_done = sem("unit_done")
        tile_out = [sem("tile_out0"), sem("tile_out1")]
        glu_made, db_used, cin_used, ax_used = map(
            sem, ("glu_made", "db_used", "cin_used", "ax_used"))
        tails_taken, tails_out, tails_stored = sem("tails_taken"), sem("tails_out"), sem("tails_stored")
        rows_packed = sem("rows_packed")
        dve = sem("dve_steps")
        act_own = sem("act_steps")
        yd_ready = sem("yd_ready")
        side_done, side_out = sem("side_done"), sem("side_out")
        yc_ready, sqrt_ready = sem("yc_ready"), sem("sqrt_ready")
        yc_split = sem("yc_split")
        ya_ready, yb_ready = sem("ya_ready"), sem("yb_ready")
        h_turned, h_copied = sem("h_turned"), sem("h_copied")
        bsq_ready, bvar_ready, bstd_ready, bnorm_ready, bsig_ready = map(
            sem, ("bsq_ready", "bvar_ready", "bstd_ready", "bnorm_ready", "bsig_ready"))
        merged_ready = sem("merged_ready")
        r_ready, rsq_ready, stat_done = sem("r_ready"), sem("rsq_ready"), sem("stat_done")
        var_ready, std_ready = sem("var_ready"), sem("std_ready")
        norm_ready, affine_ready, x1_hi_ready, x1_lo_ready = map(
            sem, ("norm_ready", "affine_ready", "x1_hi_ready", "x1_lo_ready"))
        hid_hi_ready, hid_lo_ready = map(sem, ("hid_hi_ready", "hid_lo_ready"))
        y_turned, y_copied = sem("y_turned"), sem("y_copied")
        ys_turned, ys_copied = sem("ys_turned"), sem("ys_copied")
        stored = sem("stored")

        w_in = i_["w_in"].rearrange("a (k p) n -> p (a k) n", p=P)
        w_br = i_["w_branch"].rearrange("a b (k p) n -> p (a b k) n", p=P)
        w_out = i_["w_out"].rearrange("a (k p) n -> p (a k) n", p=P)
        w_g = i_["w_ff_gate"].rearrange("a (k p) n -> p (a k) n", p=P)
        w_u = i_["w_ff_up"].rearrange("a (k p) n -> p (a k) n", p=P)
        w_d = i_["w_ff_down"].rearrange("a (k p) n -> p (a k) n", p=P)
        x_p = i_["x_prompt"].rearrange("a (j p) d -> p (a j) d", p=P)
        x_s = i_["x_sample"].rearrange("b t d -> (b t) d")
        o_x = o_["y_prompt"].rearrange("a (j p) d -> p (a j) d", p=P)
        o_s = o_["y_sample"].rearrange("b t d -> (b t) d")

        def rows2(ap):
            return ap.rearrange("a b w -> (a b) w")

        def rows3(ap):
            return ap.rearrange("a b r w -> (a b r) w")

        block = ctx.enter_context(nc.Block())

        @block.sync
        def _(sp):
            nc.disable_value_cache = True

            def unit(u, s, src):
                if not (isinstance(u, int) and u < RING):
                    sp.wait_ge(w_lo_ready, u - (RING - 1))
                sp.dma_start(raw[s][:, 0:src.shape[1], :], src).then_inc(raw_landed[s], 16)

            for j in range(SEQ // P):
                sp.dma_start(x_tok[:, j, :], x_p[:, j, :]).then_inc(x_landed[j], 16)
            sp.dma_start(xs_tok[:, :], x_s).then_inc(x_landed[4], 16)

            def in_col(idx, c):
                return w_in[:, :, ds(IN_ORDER[idx] * W + c * P, P)]

            for idx in range(RING):
                unit(idx, idx, in_col(idx, 0))
            sp.wait_ge(sm_zeroed, 1)
            for k0, name in ((0, "rg_w_a"), (KW, "rg_w_x")):
                w = i_[name].rearrange("a (c two) i j -> (a two) i c j", two=2)
                for two in range(2):
                    q = slice(64 * two, 64 * two + 64)
                    sp.dma_start(sm_raw[q, k0:k0 + KW, q], w[two]).then_inc(sm_landed, 16)
            sp.dma_start(sm_raw[:, 2 * KW:3 * KW, :],
                         i_["pool_w"].rearrange("a g i j -> i (a g) j")).then_inc(sm_landed, 16)
            with sp.Fori(1, KW - 1 + 1) as c_1:
                c = c_1 - 1
                for idx in range(RING, 8):
                    unit(c * 8 + idx, idx % RING, in_col(idx, c))
                for idx in range(RING):
                    unit(c * 8 + 8 + idx, idx % RING, in_col(idx, c + 1))
            for idx in range(RING, 8):
                unit(8 * (KW - 1) + idx, idx % RING, in_col(idx, KW - 1))
            for q, n in enumerate(BRANCH_ORDER):
                with sp.Fori(1, KD // 2 + 1) as i_1:
                    i = i_1 - 1
                    for mm in range(2):
                        u = i * 4 + (U_MIX + 16 * q + 2 * mm)
                        unit(u, 2 * mm, w_in[:, :, ds(i * (2 * P) + (GATE_COL + D * n + P * mm), P)])
                        unit(u + 1, 2 * mm + 1, w_br[:, n * KW:(n + 1) * KW, ds(i * (2 * P) + P * mm, P)])
            with sp.Fori(1, KD // RING + 1) as i_1:
                i = i_1 - 1
                for m in range(RING):
                    unit(i * RING + (U_OUT + m), m, w_out[:, :, ds(i * (RING * P) + m * P, P)])
            with sp.Fori(1, KF // 2 + 1) as i_1:
                i = i_1 - 1
                for mm in range(2):
                    u = i * 4 + (U_FF + 2 * mm)
                    unit(u, 2 * mm, w_g[:, :, ds(i * (2 * P) + P * mm, P)])
                    unit(u + 1, 2 * mm + 1, w_u[:, :, ds(i * (2 * P) + P * mm, P)])
            with sp.Fori(1, KD // 4 + 1) as i_1:
                i = i_1 - 1
                for m in range(4):
                    k = 0
                    for part, n in enumerate(DOWN_SPLIT):
                        j = 3 * m + part
                        unit(i * 12 + (U_DOWN + j), j % RING, w_d[:, k:k + n, ds(i * (4 * P) + m * P, P)])
                        k += n
            sp.wait_ge(h_copied, 1)
            sp.dma_start(rows2(o_["prompt_h"]), h_rows[0:1, :]).then_inc(stored, 16)
            sp.dma_start(rows2(o_["sample_h"]), h_rows[1:1 + B, :]).then_inc(stored, 16)
            for g in range(2):
                sp.wait_ge(y_copied, 4 * (g + 1))
                sp.wait_ge(ys_copied, g + 1)
                sp.dma_start(o_x[:, :, g * 512:g * 512 + 512], y_tok[:, :, g * 512:g * 512 + 512])\
                  .then_inc(stored, 16)
                sp.dma_start(o_s[:, g * 512:g * 512 + 512], ys_tok[:, g * 512:g * 512 + 512])\
                  .then_inc(stored, 16)
            sp.wait_ge(stored, 16 * 6)
            sp.wait_ge(tails_stored, 1 + 9 * 16 * KW)
            nc.disable_value_cache = False

        @block.gpsimd
        def _(pool):
            pool.memset(ident[:, :], 0.0).then_inc(consts, 1)
            pool.wait_ge(consts, 1)
            pool.affine_select(out=ident[:, :], in_=ident[:, :], compare_op=ALU.not_equal, fill=1.0,
                               base=0, pattern=[[-1, P]], channel_multiplier=1).then_inc(ident_ready, 1)
            pool.memset(sm_raw[:, :, :], 0.0).then_inc(sm_zeroed, 1)
            pool.memset(ones[:, :], 1.0).then_inc(consts, 1)
            pool.memset(glu_pad[:, 0:PAD_B], 0.0).then_inc(glu_made, 1)
            pool.memset(dch_pad[:, 0:PAD_D], 0.0)
            pool.memset(cin_pad[:, 0:PAD_C], 0.0).then_inc(cin_used, 1)
            pool.memset(ax_pad[:, 0:PAD_A], 0.0).then_inc(ax_used, 1)
            pool.memset(st_s[:, :], 0.0).then_inc(tails_stored, 1)
            pool.memset(widen[:, :, :], 0.0).then_inc(consts, 1)
            pool.wait_ge(consts, 3)
            for c in range(KW):
                window = 2 << c
                for j in range(c):
                    pool.memset(widen[:, c, j:j + 1], 1.0)
                pool.memset(widen[:, c, 3:4], 1.0 / window)
                for t in range(POOL_BUF):
                    pool.memset(inv_count[:, c, t:t + 1], 1.0 / min(window, t + 1))
            pool.memset(d_b[:, 0:1], 0.0).then_inc(db_used, 1)

            def lo(u, s, n):
                pool.wait_ge(w_hi_ready, u + 1)
                pool.tensor_tensor(w_lo[s][:, 0:n, :], raw[s][:, 0:n, :], w_hi[s][:, 0:n, :].bitcast(F32),
                                   ALU.subtract).then_inc(w_lo_ready, 1)

            with pool.Fori(0, 1) as i:
                for u in range(RING):
                    lo(i * RING + u, u, 8)
            pool.wait_ge(sm_hi_ready, 1)
            pool.tensor_tensor(sm_lo[:, :, :], sm_raw[:, :, :], sm_hi[:, :, :].bitcast(F32),
                               ALU.subtract).then_inc(sm_lo_ready, 1)
            with pool.Fori(1, U_MIX // RING) as i:
                for u in range(RING):
                    lo(i * RING + u, u, 8)
            with pool.Fori(0, (U_OUT - U_MIX) // RING) as i:
                for u in range(RING):
                    lo(i * RING + (U_MIX + u), u, (8, KW)[u % 2])
            with pool.Fori(0, KD // RING) as i:
                for u in range(RING):
                    lo(i * RING + (U_OUT + u), u, 8)
            for k in range(KD):
                pool.wait_ge(x1_hi_ready, k + 1)
                pool.tensor_tensor(x_lo[:, k, :], merged[:, k, :], x_hi[:, k, :].bitcast(F32),
                                   ALU.subtract).then_inc(x1_lo_ready, 1)
            with pool.Fori(0, 2 * KF // RING) as i:
                for u in range(RING):
                    lo(i * RING + (U_FF + u), u, 8)
            with pool.Fori(0, KD // 4) as i:
                for j in range(12):
                    lo(i * 12 + (U_DOWN + j), j % RING, DOWN_SPLIT[j % 3])

        @block.scalar
        def _(act):
            own = Chain(act, act_own)

            def hi(u, s):
                act.wait_ge(raw_landed[s], (u // RING) * 16 + 16 if isinstance(u, int) else u_quot(u, s))
                act.activation(w_hi[s][:, :, :], raw[s][:, :, :], ACT.Copy).then_inc(w_hi_ready, 1)

            def u_quot(u, s):
                return (u - s) * (16 // RING) + 16

            small = ((misc_tok[M_CONV:M_SC, :], rows3(i_["state_rglru_conv"])),
                     (misc_tok[M_SC:M_H, :], rows3(i_["state_shortconv"])),
                     (misc_tok[M_H:V_RGW, :], rows2(i_["state_rglru_h"])),
                     (misc_tok[V_RGW:V_RGB, :], rows2(i_["rg_conv_w"])),
                     (misc_tok[V_RGB:V_RGB + 1, :], i_["rg_conv_b"]),
                     (misc_tok[V_BA:V_BA + 1, :], i_["rg_b_a"]),
                     (misc_tok[V_BX:V_BX + 1, :], i_["rg_b_x"]),
                     (misc_tok[V_LAM:V_LAM + 1, :], i_["rg_lambda"]),
                     (misc_tok[V_CFW:V_CFB, :], rows2(i_["cf_conv_w"])),
                     (misc_tok[V_CFB:V_CFB + 1, :], i_["cf_conv_b"]),
                     (misc_tok[V_CFG:V_CFG + 1, :], i_["cf_ln_g"]),
                     (misc_tok[V_CFLB:V_CFLB + 1, :], i_["cf_ln_b"]),
                     (misc_tok[V_PSC:V_PSC + 1, :], i_["pool_scale"]),
                     (misc_tok[V_SCW:M_ROWS, :], rows2(i_["sc_conv_w"])),
                     (conf_tok[:, 0, :], rows3(i_["state_conformer_conv"])[0:120, :]),
                     (conf_tok[:, 1, :], rows3(i_["state_conformer_conv"])[120:240, :]),
                     (pool_tok[:, :], rows3(i_["state_pool"]))) + tuple(
                         (ln_tok[8 * j:8 * j + 8, :], i_[n].rearrange("a (k p) -> (a k) p", p=P))
                         for j, n in enumerate(("ln1_g", "ln1_b", "ln2_g", "ln2_b")))
            assert len(small) == N_SMALL
            for dst, src in small:
                act.dma_start(dst, src).then_inc(small_landed, 16)
            for k in range(KD):
                act.wait_ge(turned, k + 1)
                bank = (main, aux)[k // 4]
                act.activation(x_hi[:, k, 0:SEQ], bank[:, k % 4, :], ACT.Copy).then_inc(x_hi_ready, 1)
            act.wait_ge(turned, KD + 1)
            act.activation(x_hi[:, :, SEQ:NT], main[:, 0, 0:256].rearrange("p (k n) -> p k n", k=KD),
                           ACT.Copy).then_inc(x_hi_ready, 1)
            hi(0, 0)
            for g in range(2):
                act.wait_ge(turned, KD + 3 + g)
                act.activation(confT[:, 2 * g:2 * g + 2, :],
                               main[:, 2 + g, 0:480].rearrange("p (c n) -> p c n", c=2), ACT.Copy)\
                   .then_inc(conf_ready if g == 0 else tile_out[1], 1)
            act.wait_ge(turned, KD + 5)
            act.activation(poolT[:, :, :], aux[:, 0, 0:480].rearrange("p (c n) -> p c n", c=KW), ACT.Copy)\
               .then_inc(tails_out, 1)
            for u in range(1, RING):
                hi(u, u)
            act.wait_ge(lam_ready, 1)
            act.activation(spv[:, 1, :], spv[:, 0, :], ACT.Exp).then_inc(z_ready, 1)
            act.wait_ge(sm_landed, 5 * 16)
            act.activation(sm_hi[:, :, :], sm_raw[:, :, :], ACT.Copy).then_inc(sm_hi_ready, 1)

            with act.Fori(0, KW) as c:
                for idx, kind in enumerate(IN_ORDER):
                    u = c * 8 + idx
                    act.wait_ge(unit_done, u + 1)
                    ps = slot(idx % 2)
                    out_sem = tile_out[idx % 2]
                    if kind == B_VAL:
                        act.wait_ge(glu_made, c + 1)
                        act.activation(halves(b_val[:, :]), ps, ACT.Copy).then_inc(out_sem, 1)
                    elif kind == B_GATE:
                        act.activation(halves(b_sig[:, :]), ps, ACT.Sigmoid).then_inc(out_sem, 1)
                    elif kind == D_C:
                        act.activation(halves(d_c[:, :]), ps, ACT.Copy).then_inc(out_sem, 1)
                    elif kind == D_B:
                        act.wait_ge(db_used, c + 1)
                        act.activation(halves(d_b[:, :]), ps, ACT.Copy).then_inc(out_sem, 1)
                    elif kind in (C_IN, A_X):
                        buf, w, used = ((cin_pad, PAD_C, cin_used) if kind == C_IN
                                        else (ax_pad, PAD_A, ax_used))
                        act.wait_ge(used, c + 1)
                        act.wait_ge(tails_taken, c + 1)
                        a, b = ps[:, 0, :], ps[:, 1, :]
                        act.activation(buf[:, w:w + HALF], a, ACT.Copy)
                        act.activation(buf[:, w + HALF:w + SEQ], b[:, 0:SEQ - HALF], ACT.Copy)
                        act.activation(sa(buf, w, w), steps(b[:, SEQ - HALF:HALF]), ACT.Copy)\
                           .then_inc(out_sem, 1)
                    elif kind == A_GATE:
                        act.activation(halves(agate[:, c, :]), ps, ACT.Copy).then_inc(out_sem, 1)
                    hi(u + RING, idx % RING)
                act.wait_ge(ax_used, c + 2)
                for (buf, w, n0, n1) in ((glu_pad, PAD_B, 0, 240), (cin_pad, PAD_C, 240, 360),
                                         (ax_pad, PAD_A, 360, 384), (dch_pad, PAD_D, 384, 400)):
                    ins = act.activation(steps(packed[:, n0:n1]), sa(buf, w, T, w), ACT.Copy)
                ins.then_inc(rows_packed, 1)
                act.wait_ge(tails_taken, c + 2)
                act.wait_ge(tails_stored, c * (9 * 16) + 1)
                act.activation(st_s[:, :], aux[0:120, 0, 0:3 * P], ACT.Copy)
                act.activation(st_p[:, :], aux[0:30, 1, 0:4 * P], ACT.Copy)
                act.activation(st_ax[:, :], aux[0:24, 2, 0:P], ACT.Copy)
                act.activation(st_sc[:, :], aux[0:16, 2, P:2 * P], ACT.Copy).then_inc(tails_out, 1)
                act.wait_ge(tails_out, c + 2)
                cols = ds(c * P, P)
                for dst, r0, r1, src in (
                        ("sample_cf", 0, 120, st_s[:, 0:P]), ("sample_cf", 120, 240, st_s[:, P:2 * P]),
                        ("sample_pool", 0, 120, st_s[:, 2 * P:3 * P]),
                        ("prompt_rgc", 0, 3, st_p[27:30, 0:P]), ("prompt_cf", 0, 30, st_p[:, P:2 * P]),
                        ("prompt_pool", 0, 15, st_p[15:30, 2 * P:3 * P]),
                        ("prompt_sc", 0, 2, st_p[28:30, 3 * P:4 * P]),
                        ("sample_rgc", 0, 24, st_ax[:, :]), ("sample_sc", 0, 16, st_sc[:, :])):
                    act.dma_start(rows3(o_[dst])[r0:r1, cols], src).then_inc(tails_stored, 16)
            act.wait_ge(tails_stored, 1 + 9 * 16 * KW)

            def gate(u, s, mm):
                act.wait_ge(unit_done, u + 1)
                act.activation(halves(sig[mm][:, :]), slot(0), ACT.Sigmoid).then_inc(tile_out[0], 1)
                hi(u + RING, s)

            def used(u, s):
                act.wait_ge(unit_done, u + 1)
                hi(u + RING, s)

            for q in range(4):
                with act.Fori(0, KD // 2) as i:
                    u = i * 4 + (U_MIX + 16 * q)
                    gate(u, 0, 0)
                    used(u + 1, 1)
                    if q == 2:
                        act.wait_ge(bnorm_ready, i + 1)
                        act.activation(S[3][:, :], S[2][:, :], ACT.Sigmoid).then_inc(bsig_ready, 1)
                    gate(u + 2, 2, 1)
                    used(u + 3, 3)
                if q == 0:
                    for c in range(KW):
                        act.wait_ge(side_done, c + 1)
                        act.activation(halves(pool_t[:, c, :]), aslot(c % 2), ACT.Copy,
                                       scale=miscT[:, c, V_PSC:V_PSC + 1]).then_inc(side_out, 1)
                        act.wait_ge(side_out, c + 1)
                        act.activation(Y_C[:, c, :], pool_t[:, c, :], ACT.Copy).then_inc(yc_ready, 1)
                    for c in range(KW):
                        act.wait_ge(side_done, KW + 2 * c + 1)
                        if c:
                            act.wait_ge(act_own, c)
                        act.activation(halves(rgate[:, :]), aslot(0), ACT.Sigmoid,
                                       bias=miscT[:, c, V_BA:V_BA + 1]).then_inc(side_out, 1)
                        act.wait_ge(side_done, KW + 2 * c + 2)
                        act.activation(halves(igate[:, c, :]), aslot(1), ACT.Sigmoid,
                                       bias=miscT[:, c, V_BX:V_BX + 1]).then_inc(side_out, 1)
                        act.wait_ge(side_out, KW + 2 * c + 1)
                        own.link(act.activation(th[:, c, :], rgate[:, :], ACT.Tanh,
                                                scale=spv[:, 7, c:c + 1]))
                    act.wait_ge(act_own, KW)
                    act.wait_ge(yc_split, KW)
                    act.activation(sq_th[:, :, :], th[:, :, :], ACT.Sqrt, bias=1e-30)
                    act.activation(agate[:, :, :], agate[:, :, :], ACT.Gelu_apprx_tanh)\
                       .then_inc(sqrt_ready, 1)
                if q == 1:
                    act.wait_ge(ya_ready, KW)
                    act.activation(bsq[:, :, :], bconv[:, :, :], ACT.Square).then_inc(bsq_ready, 1)
                    act.wait_ge(h_turned, 1)
                    act.activation(h_rows[:, :], aux[0:1 + B, 0, :], ACT.Copy).then_inc(h_copied, 1)
                    act.wait_ge(bvar_ready, 1)
                    act.activation(S[1][:, :], S[1][:, :], ACT.Sqrt).then_inc(bstd_ready, 1)

            def residual_squares(m, n0):
                act.wait_ge(r_ready, n0 + m + 1)
                if n0 + m >= 2:
                    act.wait_ge(stat_done, n0 + m - 1)
                act.activation(S[m % 2][:, :], merged[:, m, :], ACT.Square).then_inc(rsq_ready, 1)

            def layer_norm_tail(j):
                act.wait_ge(var_ready, j + 1)
                act.activation(S[3][:, :], S[3][:, :], ACT.Sqrt).then_inc(std_ready, 1)
                for k in range(KD):
                    act.wait_ge(norm_ready, j * KD + k + 1)
                    act.activation(merged[:, k, :], merged[:, k, :], ACT.Identity,
                                   scale=lnT[:, 16 * j + k:16 * j + k + 1],
                                   bias=lnT[:, 16 * j + 8 + k:16 * j + 9 + k]).then_inc(affine_ready, 1)
                    if j == 0:
                        act.wait_ge(affine_ready, k + 1)
                        act.activation(x_hi[:, k, :], merged[:, k, :], ACT.Copy).then_inc(x1_hi_ready, 1)

            for m in range(KD):
                used(U_OUT + m, m % RING)
                residual_squares(m, 0)
            layer_norm_tail(0)

            with act.Fori(0, KF // 2) as i:
                for mm in range(2):
                    u = i * 4 + (U_FF + 2 * mm)
                    act.wait_ge(unit_done, u + 1)
                    act.activation(halves(S[mm][:, :]), slot(0), ACT.Silu).then_inc(tile_out[0], 1)
                    hi(u + RING, 2 * mm)
                    used(u + 1, 2 * mm + 1)
                    act.wait_ge(tile_out[1], i * 2 + (U_FF // 2 + mm + 2))
                    act.activation(h_hi[:, i * 2 + mm, :], S[2 + mm][:, :], ACT.Copy).then_inc(hid_hi_ready, 1)
            for m in range(KD):
                for part in range(3):
                    u = U_DOWN + 3 * m + part
                    if u + RING < U_END:
                        used(u, u % RING)
                residual_squares(m, KD)
            layer_norm_tail(1)
            for k in range(KD):
                act.wait_ge(y_turned, k + 1)
                act.activation(y_tok[:, :, k * P:k * P + P],
                               main[:, k % 4, :].rearrange("p (j n) -> p j n", j=4), ACT.Copy)\
                   .then_inc(y_copied, 1)

        @block.tensor
        def _(pe):
            def passes(ps, pairs, last):
                n = len(pairs)
                for k, (wh, wl, xh, xl) in enumerate(pairs):
                    for j, (w, x) in enumerate(((wl, xh), (wh, xl), (wh, xh))):
                        for h in range(2):
                            mm = pe.matmul(ps[:, h, :], w, x[:, h * HALF:(h + 1) * HALF],
                                           start=(k == 0 and j == 0), stop=(last and k == n - 1 and j == 2))
                return mm

            def unit(u, s, xs, ps_slot, first=True, last=True, n0=0, ready=None):
                pe.wait_ge(w_lo_ready, u + 1)
                n = len(xs)
                for k, (xh, xl) in enumerate(xs):
                    if ready:
                        pe.wait_ge(ready, k + 1)
                    for j, (w, x) in enumerate(((w_lo, xh), (w_hi, xl), (w_hi, xh))):
                        for h in range(2):
                            mm = pe.matmul(slot(ps_slot)[:, h, :], w[s][:, k, :],
                                           x[:, h * HALF:(h + 1) * HALF],
                                           start=(first and k == 0 and j == 0),
                                           stop=(last and k == n - 1 and j == 2))
                mm.then_inc(unit_done, 1)

            pe.wait_ge(ident_ready, 1)
            for j in range(SEQ // P):
                pe.wait_ge(x_landed[j], 16)
            for k in range(KD):
                bank = (main, aux)[k // 4]
                for j in range(SEQ // P):
                    mm = pe.transpose(bank[:, k % 4, j * P:j * P + P], x_tok[:, j, k * P:k * P + P],
                                      ident[:, :])
                mm.then_inc(turned, 1)
            pe.wait_ge(x_landed[4], 16)
            pe.wait_ge(x_lo_ready, 1)
            for k in range(KD):
                mm = pe.transpose(main[:, 0, k * 32:k * 32 + 32], xs_tok[:, k * P:k * P + P],
                                  ident[0:32, 0:32])
            mm.then_inc(turned, 1)
            pe.wait_ge(small_landed, 16 * N_SMALL)
            pe.wait_ge(x_lo_ready, 2)
            for c in range(KW):
                pe.transpose(main[:, 1, c * M_ROWS:(c + 1) * M_ROWS], misc_tok[:, c * P:c * P + P],
                             ident[0:M_ROWS, 0:M_ROWS])
            pe.transpose(main[:, 1, KW * M_ROWS:KW * M_ROWS + 32], ln_tok[:, :], ident[0:32, 0:32])\
              .then_inc(turned, 1)
            for g in range(2):
                pe.wait_ge(x_lo_ready, 3 + g)
                for c in range(2):
                    for half in range(2):
                        mm = pe.transpose(main[:, 2 + g, c * 240 + half * 120:c * 240 + half * 120 + 120],
                                          conf_tok[:, half, (2 * g + c) * P:(2 * g + c + 1) * P],
                                          ident[0:120, 0:120])
                mm.then_inc(turned, 1)
            pe.wait_ge(x_lo_ready, 5)
            for c in range(KW):
                mm = pe.transpose(aux[:, 0, c * 120:c * 120 + 120], pool_tok[:, c * P:c * P + P],
                                  ident[0:120, 0:120])
            mm.then_inc(turned, 1)
            pe.wait_ge(x_lo_ready, KD + 1)
            pe.wait_ge(misc_ready, 1)
            pe.wait_ge(tails_out, 1)
            pe.transpose(aux[:, 1, 0:P], ident[:, :], ident[:, :]).then_inc(tails_taken, 1)

            x_in = [(x_hi[:, k, :], x_lo[:, k, :]) for k in range(KD)]
            with pe.Fori(0, KW) as c:
                for idx in range(8):
                    u = c * 8 + idx
                    pe.wait_ge(tile_out[idx % 2], c * 4 + (idx // 2 + 1))
                    unit(u, idx % RING, x_in, idx % 2)
                pe.wait_ge(ax_used, c + 2)
                pe.wait_ge(tails_out, c + 1)
                for j, (buf, w) in enumerate(((ax_pad, PAD_A), (glu_pad, PAD_B), (cin_pad, PAD_C),
                                              (dch_pad, PAD_D))):
                    pe.transpose(aux[0:30, 1, j * P:j * P + P], buf[:, w + SEQ - 30:w + SEQ], ident[:, :])
                pe.wait_ge(rows_packed, c + 1)
                for j in range(3):
                    pe.transpose(aux[0:120, 0, j * P:j * P + P], packed[:, 120 * j:120 * j + 120], ident[:, :])
                pe.transpose(aux[0:24, 2, 0:P], packed[:, 360:384], ident[:, :])
                pe.transpose(aux[0:16, 2, P:2 * P], packed[:, 384:400], ident[:, :])\
                  .then_inc(tails_taken, 1)

            for q in range(4):
                yq = (Y_D, Y_C, Y_A, Y_D)[q]
                xs = [(yq[:, k, :], yq[:, KW + k, :]) for k in range(KW)]
                if q == 1:
                    pe.wait_ge(sm_lo_ready, 1)
                    for j in range(3 * KW):
                        if j < KW:
                            c, t, src = j, 2 * KW + j, Y_C
                        else:
                            c = (j - KW) // 2
                            t, src = ((j - KW) % 2) * KW + c, Y_A
                        if j >= 2:
                            pe.wait_ge(side_out, j - 1)
                        passes(aslot(j % 2), [(sm_hi[:, t, :], sm_lo[:, t, :], src[:, c, :],
                                               src[:, KW + c, :])], True).then_inc(side_done, 1)
                    pe.wait_ge(yc_split, KW)
                if q == 2:
                    pe.wait_ge(ya_ready, KW)
                    for c in range(KW):
                        mm = pe.transpose(aux[0:1 + B, 0, c * P:c * P + P], h_last[:, c, :], ident[:, :])
                    mm.then_inc(h_turned, 1)
                    pe.wait_ge(bsq_ready, 1)
                    pe.wait_ge(h_copied, 1)
                    for s, src in ((0, bconv), (1, bsq)):
                        for c in range(KW):
                            for h in range(2):
                                mm = pe.matmul(aslot(s)[:, h, :], ones[:, :],
                                               src[:, c, h * HALF:(h + 1) * HALF],
                                               start=(c == 0), stop=(c == KW - 1))
                        mm.then_inc(side_done, 1)
                if q == 0:
                    pe.wait_ge(yd_ready, KW)
                if q == 3:
                    pe.wait_ge(yb_ready, KW)
                with pe.Fori(0, KD // 2) as i:
                    for mm_ in range(2):
                        u = i * 4 + (U_MIX + 16 * q + 2 * mm_)
                        t2_ = i * 2 + ((U_MIX + 16 * q) // 2 + mm_ + 1)
                        pe.wait_ge(tile_out[0], t2_)
                        unit(u, 2 * mm_, x_in, 0)
                        pe.wait_ge(tile_out[1], t2_)
                        unit(u + 1, 2 * mm_ + 1, xs, 1)

            def sums(m, n0):
                pe.wait_ge(rsq_ready, n0 + m + 1)
                for s, src in ((0, merged[:, m, :]), (1, S[m % 2][:, :])):
                    for h in range(2):
                        mm = pe.matmul(aslot(s)[:, h, :], ones[:, :], src[:, h * HALF:(h + 1) * HALF],
                                       start=(m == 0), stop=(m == KD - 1))
                mm.then_inc(stat_done, 1)

            pe.wait_ge(merged_ready, KD)
            xs = [(Y_C[:, k, :], Y_A[:, k, :]) for k in range(KD)]
            for m in range(KD):
                u = U_OUT + m
                pe.wait_ge(tile_out[m % 2], u // 2 + 1)
                unit(u, u % RING, xs, m % 2)
                if m >= 1:
                    sums(m - 1, 0)
            sums(KD - 1, 0)

            pe.wait_ge(tile_out[0], U_FF // 2 + 1)
            unit(U_FF, 0, x_in, 0, ready=x1_lo_ready)
            pe.wait_ge(tile_out[1], U_FF // 2 + 1)
            unit(U_FF + 1, 1, x_in, 1)
            with pe.Fori(0, KF // 2 - 1) as i:
                for j in range(2):
                    t2_ = i * 2 + (U_FF // 2 + 2 + j)
                    pe.wait_ge(tile_out[0], t2_)
                    unit(i * 4 + (U_FF + 2 + 2 * j), (2 + 2 * j) % RING, x_in, 0)
                    pe.wait_ge(tile_out[1], t2_)
                    unit(i * 4 + (U_FF + 3 + 2 * j), (3 + 2 * j) % RING, x_in, 1)
            pe.wait_ge(tile_out[0], U_DOWN // 2)
            unit(U_DOWN - 2, 2, x_in, 0)
            pe.wait_ge(tile_out[1], U_DOWN // 2)
            unit(U_DOWN - 1, 3, x_in, 1)

            pe.wait_ge(hid_lo_ready, KF - 1)
            for m in range(KD):
                pe.wait_ge(tile_out[m % 2], U_DOWN // 2 + m // 2 + 1)
                k = 0
                for part, n in enumerate(DOWN_SPLIT):
                    u = U_DOWN + 3 * m + part
                    if m == 0 and part == 2:
                        pe.wait_ge(hid_lo_ready, KF)
                    unit(u, u % RING, [(h_hi[:, k + j, :], h_lo[:, k + j, :]) for j in range(n)], m % 2,
                         first=(part == 0), last=(part == 2))
                    k += n
                if m >= 1:
                    sums(m - 1, KD)
            sums(KD - 1, KD)
            for k in range(KD):
                pe.wait_ge(affine_ready, KD + k + 1)
                if k == 0:
                    pe.wait_ge(tile_out[0], U_DOWN // 2 + KD // 2 + 1)
                    pe.wait_ge(tile_out[1], U_DOWN // 2 + KD // 2 + 1)
                if k >= 4:
                    pe.wait_ge(y_copied, k - 3)
                for j in range(SEQ // P):
                    mm = pe.transpose(main[:, k % 4, j * P:j * P + P], merged[:, k, j * P:j * P + P],
                                      ident[:, :])
                mm.then_inc(y_turned, 1)
                mm = pe.transpose(aux[0:32, k // 4, (k % 4) * P:(k % 4) * P + P], merged[:, k, SEQ:NT],
                                  ident[:, :])
                if k % 4 == 3:
                    mm.then_inc(ys_turned, 1)

        @block.vector
        def _(ve):
            ch = Chain(ve, dve)
            link, after = ch.link, ch.after

            def vec(c, j):
                return miscT[:, c, j:j + 1]

            for k in range(KD):
                ve.wait_ge(x_hi_ready, k + 1)
                bank = (main, aux)[k // 4]
                ve.tensor_tensor(x_lo[:, k, 0:SEQ], bank[:, k % 4, :], x_hi[:, k, 0:SEQ].bitcast(F32),
                                 ALU.subtract).then_inc(x_lo_ready, 1)
            ve.wait_ge(x_hi_ready, KD + 1)
            ve.tensor_tensor(x_lo[:, :, SEQ:NT], main[:, 0, 0:256].rearrange("p (k n) -> p k n", k=KD),
                             x_hi[:, :, SEQ:NT].bitcast(F32), ALU.subtract).then_inc(x_lo_ready, 1)
            ve.wait_ge(turned, KD + 2)
            ve.tensor_copy(miscT[:, :, :], main[:, 1, 0:KW * M_ROWS].rearrange("p (c n) -> p c n", c=KW))\
              .then_inc(misc_ready, 1)
            ve.tensor_copy(lnT[:, :], main[:, 1, KW * M_ROWS:KW * M_ROWS + 32]).then_inc(tile_out[0], 1)
            ve.wait_ge(misc_ready, 1)
            lam = miscT[:, :, V_LAM:V_LAM + 1].rearrange("p c o -> p (c o)")
            after(link(ve.tensor_scalar(spv[:, 2, :], lam, -1.0, None, ALU.mult)))
            ve.tensor_tensor(spv[:, 0, :], lam, spv[:, 2, :], ALU.min).then_inc(lam_ready, 1)
            after(link(ve.tensor_scalar(spv[:, 3, :], spv[:, 2, :], 0.0, None, ALU.max)))
            ve.wait_ge(z_ready, 1)
            after(link(ve.tensor_scalar(spv[:, 4, :], spv[:, 1, :], 2.0, None, ALU.add)))
            after(link(ve.reciprocal(spv[:, 4, :], spv[:, 4, :])))
            after(link(ve.tensor_tensor(spv[:, 4, :], spv[:, 4, :], spv[:, 1, :], ALU.mult)))
            after(link(ve.tensor_tensor(spv[:, 5, :], spv[:, 4, :], spv[:, 4, :], ALU.mult)))
            after(link(ve.tensor_scalar(spv[:, 6, :], spv[:, 5, :], 1.0 / 17, None, ALU.mult)))
            for n in (15, 13, 11, 9, 7, 5, 3):
                after(link(ve.scalar_tensor_tensor(spv[:, 6, :], spv[:, 6, :], 1.0 / n, spv[:, 5, :],
                                                   ALU.add, ALU.mult)))
            after(link(ve.scalar_tensor_tensor(spv[:, 6, :], spv[:, 6, :], 1.0, spv[:, 4, :],
                                               ALU.add, ALU.mult)))
            after(link(ve.scalar_tensor_tensor(spv[:, 6, :], spv[:, 6, :], 2.0, spv[:, 3, :],
                                               ALU.mult, ALU.add)))
            after(link(ve.tensor_scalar(spv[:, 7, :], spv[:, 6, :], 4.0, None, ALU.mult)))
            ve.wait_ge(conf_ready, 1)
            ve.wait_ge(db_used, 1)

            def filter_taps(taps, src, w, out, out_s, weight, bias, state):
                for t in taps:
                    pin, sin = pr(src, w, t), sa(src, w, t)
                    if t == 0:
                        if bias is None:
                            state[0] = link(ve.tensor_scalar(out, pin, weight(0), None, ALU.mult))
                            state[1] = link(ve.tensor_scalar(out_s, sin, weight(0), None, ALU.mult))
                        else:
                            state[0] = link(ve.tensor_scalar(out, pin, weight(0), bias, ALU.mult, ALU.add))
                            state[1] = link(ve.tensor_scalar(out_s, sin, weight(0), bias, ALU.mult, ALU.add))
                    else:
                        after(state[0])
                        state[0] = link(ve.scalar_tensor_tensor(out, pin, weight(t), out, ALU.mult, ALU.add))
                        after(state[1])
                        state[1] = link(ve.scalar_tensor_tensor(out_s, sin, weight(t), out_s,
                                                                ALU.mult, ALU.add))

            def split(src, hi_ap, lo_ap):
                after(link(ve.tensor_copy(hi_ap, src)))
                return ve.tensor_tensor(lo_ap, src, hi_ap.bitcast(F32), ALU.subtract)

            with ve.Fori(0, KW) as c:
                ch.enter(c, PER_IN)
                ve.wait_ge(tails_taken, c + 1)
                link(ve.tensor_copy(sa(glu_pad, PAD_B, 0, PAD_B), steps(confT[:, c, :])))
                ve.wait_ge(tile_out[1], c * 4 + 2)
                ve.wait_ge(tile_out[0], c * 4 + 2)
                link(ve.tensor_tensor(glu_pad[:, PAD_B:PAD_B + SEQ], b_val[:, 0:SEQ], b_sig[:, 0:SEQ],
                                      ALU.mult))
                ve.tensor_tensor(sa(glu_pad, PAD_B, PAD_B), steps(b_val[:, SEQ:NT]), steps(b_sig[:, SEQ:NT]),
                                 ALU.mult).then_inc(glu_made, 1)
                ve.wait_ge(glu_made, c + 2)
                st_b = [None, None]
                conv_b = (glu_pad, PAD_B, bconv[:, c, 0:SEQ], steps(bconv[:, c, SEQ:NT]),
                          lambda t: vec(c, V_CFW + t), vec(c, V_CFB), st_b)
                filter_taps(range(0, CONF_TAPS_1), *conv_b)

                link(ve.tensor_copy(sa(dch_pad, PAD_D, 0, PAD_D), steps(miscT[:, c, M_SC:M_H])))
                ve.wait_ge(tile_out[0], c * 4 + 3)
                ve.wait_ge(unit_done, c * 8 + 4)
                dh = slot(1)
                link(ve.tensor_tensor(dch_pad[:, PAD_D:PAD_D + HALF], dh[:, 0, :], d_c[:, 0:HALF], ALU.mult))
                link(ve.tensor_tensor(dch_pad[:, PAD_D + HALF:PAD_D + SEQ], dh[:, 1, 0:SEQ - HALF],
                                      d_c[:, HALF:SEQ], ALU.mult))
                ve.tensor_tensor(sa(dch_pad, PAD_D, PAD_D), steps(dh[:, 1, SEQ - HALF:HALF]),
                                 steps(d_c[:, SEQ:NT]), ALU.mult).then_inc(tile_out[1], 1)
                ve.wait_ge(tile_out[1], c * 4 + 3)
                st_d = [None, None]
                filter_taps(range(SC_TAPS), dch_pad, PAD_D, acc[0][:, 0:SEQ], steps(acc[0][:, SEQ:NT]),
                            lambda t: vec(c, V_SCW + t), None, st_d)
                ve.wait_ge(tile_out[0], c * 4 + 4)
                after(st_d[1])
                ve.tensor_tensor(acc[1][:, 0:NT], acc[0][:, 0:NT], d_b[:, :], ALU.mult).then_inc(db_used, 1)
                ve.wait_ge(db_used, c + 2)
                split(acc[1][:, 0:NT], Y_D[:, c, :], Y_D[:, c + KW, :]).then_inc(yd_ready, 1)

                filter_taps(range(CONF_TAPS_1, CONF_TAPS_2), *conv_b)

                link(ve.tensor_copy(sa(cin_pad, PAD_C, 0, PAD_C), steps(poolT[:, c, :])))
                ve.wait_ge(tile_out[1], c * 4 + 4)
                n = SEQ + PAD_C
                ve.wait_ge(yd_ready, c + 1)
                src = (cin_pad[:, 0:n], sa(cin_pad, PAD_C, 0, PAD_C + T))
                after(ch.base + ch.local)
                lost = 0
                for step in range(4):
                    dst_buf = acc[step % 2]
                    dst = (dst_buf[:, 0:n], sa(dst_buf, PAD_C, 0, PAD_C + T))
                    sh = 1 << step
                    lost += sh
                    for part in range(2):
                        if part == 0:
                            o, a, b_ = (dst[0][:, lost:n], src[0][:, lost:n], src[0][:, lost - sh:n - sh])
                        else:
                            m_ = PAD_C + T
                            o, a, b_ = (dst[1][:, :, lost:m_], src[1][:, :, lost:m_],
                                        src[1][:, :, lost - sh:m_ - sh])
                        by = 1.0 if step == 0 else widen[:, c, step - 1:step]
                        v = link(ve.scalar_tensor_tensor(o, b_, by, a, ALU.mult, ALU.add))
                    after(v)
                    src = dst
                win = acc[1]
                m0 = acc[0]
                link(ve.scalar_tensor_tensor(m0[:, 0:SEQ], win[:, PAD_C:PAD_C + SEQ], widen[:, c, 3:4],
                                             cin_pad[:, PAD_C:PAD_C + SEQ], ALU.mult, ALU.subtract))
                v = link(ve.scalar_tensor_tensor(steps(m0[:, SEQ:NT]), sa(win, PAD_C, PAD_C), widen[:, c, 3:4],
                                                 sa(cin_pad, PAD_C, PAD_C), ALU.mult, ALU.subtract))
                after(v)
                after(link(ve.tensor_tensor(m0[:, 0:POOL_BUF], win[:, PAD_C:2 * PAD_C], inv_count[:, c, :],
                                            ALU.mult)))
                ve.tensor_tensor(m0[:, 0:POOL_BUF], m0[:, 0:POOL_BUF], cin_pad[:, PAD_C:2 * PAD_C],
                                 ALU.subtract).then_inc(cin_used, 1)
                ve.wait_ge(cin_used, c + 2)
                after(link(split(m0[:, 0:NT], Y_C[:, c, :], Y_C[:, c + KW, :])))

                link(ve.tensor_copy(sa(ax_pad, PAD_A, 0, PAD_A), steps(miscT[:, c, M_CONV:M_SC])))
                ve.wait_ge(tile_out[0], c * 4 + 5)
                after(ch.base + ch.local)
                st_a = [None, None]
                filter_taps(range(RG_TAPS), ax_pad, PAD_A, xc[:, c, 0:SEQ], steps(xc[:, c, SEQ:NT]),
                            lambda t: vec(c, V_RGW + t), vec(c, V_RGB), st_a)
                after(st_a[1])
                after(link(ve.tensor_copy(Y_A[:, c, :], xc[:, c, :])))
                ve.tensor_tensor(Y_A[:, c + KW, :], xc[:, c, :], Y_A[:, c, :].bitcast(F32), ALU.subtract)\
                  .then_inc(ax_used, 1)
                filter_taps(range(CONF_TAPS_2, CF_TAPS), *conv_b)
                after(st_b[1])
            ch.leave(KW)

            def product(q, i, mm):
                u = i * 4 + (U_MIX + 16 * q + 2 * mm)
                ve.wait_ge(tile_out[0], i * 2 + ((U_MIX + 16 * q) // 2 + mm + 2))
                ve.wait_ge(unit_done, u + 2)
                m = i * 2 + mm
                if q == 0:
                    ve.tensor_tensor(halves(merged[:, m, :]), slot(1), halves(sig[mm][:, :]), ALU.mult)\
                      .then_inc(tile_out[1], 1)
                    return
                ve.tensor_tensor(halves(prod[:, :]), slot(1), halves(sig[mm][:, :]), ALU.mult)\
                  .then_inc(tile_out[1], 1)
                ve.wait_ge(tile_out[1], i * 2 + ((U_MIX + 16 * q) // 2 + mm + 2))
                v = link(ve.tensor_tensor(merged[:, m, :], merged[:, m, :], prod[:, :], ALU.add))
                after(v)
                if q == 3:
                    split(merged[:, m, :], Y_C[:, m, :], Y_A[:, m, :]).then_inc(merged_ready, 1)

            def recurrence(c):
                s_d, s_a, s_b, s_x = S
                after(link(ve.tensor_scalar(s_d[:, :], th[:, c, :], 1.0, None, ALU.add)))
                after(link(ve.reciprocal(s_d[:, :], s_d[:, :])))
                link(ve.tensor_scalar(s_a[:, :], s_d[:, :], 2.0, -1.0, ALU.mult, ALU.add))
                link(ve.tensor_tensor(s_b[:, :], sq_th[:, c, :], s_d[:, :], ALU.mult))
                after(link(ve.scalar_tensor_tensor(s_x[:, :], igate[:, c, :], 2.0, xc[:, c, :],
                                                   ALU.mult, ALU.mult)))
                after(link(ve.tensor_tensor(s_b[:, :], s_b[:, :], s_x[:, :], ALU.mult)))
                a0 = steps(s_a[:, SEQ:NT])[:, :, 0:1].rearrange("p b o -> p (b o)")
                b0 = steps(s_b[:, SEQ:NT])[:, :, 0:1].rearrange("p b o -> p (b o)")
                after(link(ve.tensor_tensor(s_x[:, 0:B], a0, miscT[:, c, M_H:M_H + B], ALU.mult)))
                link(ve.tensor_tensor(b0, b0, s_x[:, 0:B], ALU.add))
                after(link(ve.tensor_scalar(a0, a0, 0.0, None, ALU.mult)))
                after(link(ve.tensor_tensor_scan(s_x[:, :], s_a[:, :], s_b[:, :], 0.0, ALU.mult, ALU.add)))
                link(ve.tensor_copy(h_last[:, c, 0:1], s_x[:, SEQ - 1:SEQ]))
                link(ve.tensor_copy(h_last[:, c, 1:1 + B],
                                    steps(s_x[:, SEQ:NT])[:, :, T - 1:T].rearrange("p b o -> p (b o)")))
                after(link(ve.tensor_tensor(s_b[:, :], s_x[:, :], agate[:, c, :], ALU.mult)))
                split(s_b[:, :], Y_A[:, c, :], Y_A[:, c + KW, :]).then_inc(ya_ready, 1)
                ve.wait_ge(ya_ready, c + 1)

            def statistics(n, mean, var, sem_out):
                link(ve.tensor_scalar(halves(mean[:, :]), aslot(0), 1.0 / n, None, ALU.mult))
                after(ch.base + ch.local)
                after(link(ve.tensor_tensor(prod2[:, :], mean[:, :], mean[:, :], ALU.mult)))
                after(link(ve.scalar_tensor_tensor(halves(var[:, :]), aslot(1), 1.0 / n, halves(prod2[:, :]),
                                                   ALU.mult, ALU.subtract)))
                ve.tensor_scalar(var[:, :], var[:, :], 0.0, EPS, ALU.max, ALU.add).then_inc(sem_out, 1)

            prod2 = S[3]
            for q in range(4):
                if q == 1:
                    for c in range(KW):
                        ve.wait_ge(yc_ready, c + 1)
                        ve.tensor_tensor(Y_C[:, c + KW, :], pool_t[:, c, :], Y_C[:, c, :].bitcast(F32),
                                         ALU.subtract).then_inc(yc_split, 1)
                if q == 2:
                    ve.wait_ge(side_done, 3 * KW + 2)
                    statistics(W, S[0], S[1], bvar_ready)
                    ve.wait_ge(bstd_ready, 1)
                    after(link(ve.reciprocal(S[1][:, :], S[1][:, :])))
                ch.flush()
                with ve.Fori(0, KD // 2) as i:
                    ch.enter(i, (0, 2 + PER_REC, 2 + PER_B, 4)[q])
                    if q == 2:
                        t = bconv[:, i, :]
                        after(link(ve.tensor_tensor(t, t, S[0][:, :], ALU.subtract)))
                        after(link(ve.tensor_tensor(t, t, S[1][:, :], ALU.mult)))
                        ve.tensor_scalar(S[2][:, :], t, vec(i, V_CFG), vec(i, V_CFLB), ALU.mult, ALU.add)\
                          .then_inc(bnorm_ready, 1)
                    product(q, i, 0)
                    product(q, i, 1)
                    if q == 1:
                        ve.wait_ge(sqrt_ready, 1)
                        recurrence(i)
                    if q == 2:
                        ve.wait_ge(bsig_ready, i + 1)
                        after(link(ve.tensor_tensor(bconv[:, i, :], S[2][:, :], S[3][:, :], ALU.mult)))
                        split(bconv[:, i, :], Y_D[:, i, :], Y_D[:, i + KW, :]).then_inc(yb_ready, 1)
                ch.leave(KD // 2)

            def residual(m, u_done, t_val, n0):
                ve.wait_ge(unit_done, u_done)
                ve.scalar_tensor_tensor(halves(S[2][:, :]), halves(x_lo[:, m, :].bitcast(F32)), ALPHA,
                                        slot(m % 2), ALU.mult, ALU.add).then_inc(tile_out[m % 2], 1)
                ve.wait_ge(tile_out[m % 2], t_val)
                ve.scalar_tensor_tensor(merged[:, m, :], x_hi[:, m, :].bitcast(F32), ALPHA, S[2][:, :],
                                        ALU.mult, ALU.add).then_inc(r_ready, 1)
                ve.wait_ge(r_ready, n0 + m + 1)

            def layer_norm(j):
                ve.wait_ge(stat_done, KD * (j + 1))
                link(ve.tensor_scalar(halves(S[2][:, :]), aslot(0), 1.0 / D, None, ALU.mult))
                after(ch.base + ch.local)
                after(link(ve.tensor_tensor(S[1][:, :], S[2][:, :], S[2][:, :], ALU.mult)))
                after(link(ve.scalar_tensor_tensor(halves(S[3][:, :]), aslot(1), 1.0 / D, halves(S[1][:, :]),
                                                   ALU.mult, ALU.subtract)))
                ve.tensor_scalar(S[3][:, :], S[3][:, :], 0.0, EPS, ALU.max, ALU.add).then_inc(var_ready, 1)
                ve.wait_ge(std_ready, j + 1)
                after(link(ve.reciprocal(S[3][:, :], S[3][:, :])))
                for k in range(KD):
                    after(link(ve.tensor_tensor(merged[:, k, :], merged[:, k, :], S[2][:, :], ALU.subtract)))
                    ve.tensor_tensor(merged[:, k, :], merged[:, k, :], S[3][:, :], ALU.mult)\
                      .then_inc(norm_ready, 1)

            for m in range(KD):
                residual(m, U_OUT + m + 1, (U_OUT + m) // 2 + 2, 0)
            layer_norm(0)
            ve.wait_ge(norm_ready, KD)
            ch.flush()

            with ve.Fori(0, KF // 2) as i:
                for mm in range(2):
                    f = i * 2 + mm
                    ve.wait_ge(tile_out[0], i * 2 + (U_FF // 2 + mm + 2))
                    ve.wait_ge(unit_done, i * 4 + (U_FF + 2 * mm + 2))
                    ve.tensor_tensor(halves(S[2 + mm][:, :]), slot(1), halves(S[mm][:, :]), ALU.mult)\
                      .then_inc(tile_out[1], 1)
                    ve.wait_ge(tile_out[1], i * 2 + (U_FF // 2 + mm + 2))
                    ve.wait_ge(hid_hi_ready, f + 1)
                    ve.tensor_tensor(h_lo[:, f, :], S[2 + mm][:, :], h_hi[:, f, :].bitcast(F32), ALU.subtract)\
                      .then_inc(hid_lo_ready, 1)
                    ve.wait_ge(hid_lo_ready, f + 1)

            for m in range(KD):
                residual(m, U_DOWN + 3 * m + 3, U_DOWN // 2 + m // 2 + 2, KD)
            layer_norm(1)
            for g in range(2):
                ve.wait_ge(ys_turned, g + 1)
                ve.tensor_copy(ys_tok[:, g * 512:g * 512 + 512], aux[0:32, g, :]).then_inc(ys_copied, 1)


N_SMALL = 21
PER_IN = 98
PER_REC = 14
PER_B = 4

_INS = ["x_prompt", "x_sample", "state_rglru_h", "state_rglru_conv", "state_conformer_conv", "state_pool",
        "state_shortconv", "w_in", "rg_conv_w", "rg_conv_b", "rg_w_a", "rg_b_a", "rg_w_x", "rg_b_x",
        "rg_lambda", "cf_conv_w", "cf_conv_b", "cf_ln_g", "cf_ln_b", "pool_w", "pool_scale", "sc_conv_w",
        "w_branch", "w_out", "ln1_g", "ln1_b", "w_ff_gate", "w_ff_up", "w_ff_down", "ln2_g", "ln2_b"]
_OUTS = [("y_prompt", (1, SEQ, D)), ("y_sample", (B, T, D)),
         ("prompt_h", (1, 1, W)), ("prompt_rgc", (1, 1, 3, W)), ("prompt_cf", (1, 1, 30, W)),
         ("prompt_pool", (1, 1, 15, W)), ("prompt_sc", (1, 1, 2, W)),
         ("sample_h", (1, B, W)), ("sample_rgc", (1, B, 3, W)), ("sample_cf", (1, B, 30, W)),
         ("sample_pool", (1, B, 15, W)), ("sample_sc", (1, B, 2, W))]


def kernel(**inputs):
    import numpy as _np
    import concourse.bacc as _bacc
    from concourse.bass_utils import run_bass_kernel_spmd as _run

    nc = _bacc.Bacc("TRN2", target_bir_lowering=False, num_devices=1, dynamic_dma_scratch_size=1024)
    arrays, ins, outs = {}, {}, {}
    for name in _INS:
        a = _np.ascontiguousarray(inputs[name])
        arrays[f"in_{name}"] = a
        ins[name] = nc.dram_tensor(f"in_{name}", a.shape, mybir.dt.from_np(a.dtype), kind="ExternalInput").ap()
    for name, shape in _OUTS:
        outs[name] = nc.dram_tensor(f"out_{name}", shape, F32, kind="ExternalOutput").ap()
    build(nc, ins, outs)
    r = _run(nc, [arrays], core_ids=[0])
    return tuple(r.results[0][f"out_{name}"] for name, _ in _OUTS)
```

```python
from contextlib import ExitStack

import concourse.bass as bass
from concourse import mybir

F32 = mybir.dt.float32
F32R = mybir.dt.float32r
ALU = mybir.AluOpType
ACT = mybir.ActivationFunctionType
ds = bass.ds

P = 128
D = 1024
W = 512
SEQ = 512
B, T = 8, 4
NT = SEQ + B * T
HALF = NT // 2
FF = 2816
KD, KW, KF = D // P, W // P, FF // P
RING = 4
RG_TAPS, CF_TAPS, SC_TAPS, POOL_BUF = 4, 31, 3, 15
ALPHA = 2.0 ** 0.25
EPS = 1e-5

A_X, A_GATE, B_VAL, B_GATE, C_IN, D_B, D_C, D_H = range(8)
IN_ORDER = (B_VAL, B_GATE, D_C, D_H, D_B, C_IN, A_X, A_GATE)
GATE_COL = 8 * W
BRANCH_ORDER = (3, 2, 0, 1)

U_MIX = KW * 8
U_OUT = U_MIX + 4 * 2 * KD
U_FF = U_OUT + KD
U_DOWN = U_FF + 2 * KF
DOWN_SPLIT = (8, 8, KF - 16)
U_END = U_DOWN + 3 * KD

M_CONV, M_SC, M_H = 0, B * (RG_TAPS - 1), B * (RG_TAPS - 1) + B * (SC_TAPS - 1)
V_RGW = M_H + B
V_RGB, V_BA, V_BX, V_LAM = V_RGW + 4, V_RGW + 5, V_RGW + 6, V_RGW + 7
V_CFW = V_RGW + 8
V_CFB = V_CFW + CF_TAPS
V_CFG, V_CFLB, V_PSC = V_CFB + 1, V_CFB + 2, V_CFB + 3
V_SCW = V_CFB + 4
M_ROWS = V_SCW + SC_TAPS
CONF_TAPS_1, CONF_TAPS_2 = 14, 26


class Chain:

    def __init__(self, eng, sem):
        self.eng, self.sem, self.base, self.local = eng, sem, 0, 0
        self.start = 0

    def link(self, ins):
        ins.then_inc(self.sem, 1)
        self.local += 1
        return self.base + self.local

    def after(self, value):
        self.eng.wait_ge(self.sem, value)

    def enter(self, i, per):
        self.start += self.local if isinstance(self.base, int) else 0
        self.base, self.local, self.per = i * per + self.start, 0, per

    def leave(self, count):
        assert self.local == self.per, (self.local, self.per)
        self.start += self.per * count
        self.base, self.local = self.start, 0

    def flush(self):
        self.start += self.local
        self.base, self.local = self.start, 0


def build(nc, i_, o_):
    with ExitStack() as ctx:
        def sem(name):
            return ctx.enter_context(nc.semaphore(name))

        CH = NT * 4
        base = (nc.sbuf_base + 63) // 64 * 64
        top = [base]

        def take(nbytes):
            at = top[0]
            top[0] += (nbytes + 31) // 32 * 32
            assert top[0] <= nc.sbuf_usable_end, (name_of[0], top[0], nc.sbuf_usable_end)
            return at

        name_of = [""]

        def at(name, shape, dt, offset):
            name_of[0] = name
            return nc.alloc_sbuf_tensor_at(name, shape, dt, offset=offset)

        def new(name, shape, dt):
            n = 4
            for s in shape[1:]:
                n *= s
            name_of[0] = name
            return at(name, shape, dt, take(n))

        x_hi = new("x_hi", [P, KD, NT], F32R)
        x_lo = new("x_lo", [P, KD, NT], F32R)
        raw = [new(f"raw{s}", [P, 8, P], F32) for s in range(RING)]
        w_hi = [new(f"w_hi{s}", [P, 8, P], F32R) for s in range(RING)]
        w_lo = [new(f"w_lo{s}", [P, 8, P], F32R) for s in range(RING)]
        at_f = take(KD * CH)
        at_s = take(4 * CH)
        ident = new("ident", [P, P], F32)
        ones = new("ones", [P, P], F32)
        miscT = new("miscT", [P, KW, M_ROWS], F32)
        at_v = top[0]
        confT = new("confT", [P, KW, B * 30], F32)
        poolT = new("poolT", [P, KW, B * POOL_BUF], F32)
        lnT = new("lnT", [P, 32], F32)
        inv_count = new("inv_count", [P, KW, POOL_BUF], F32)
        widen = new("widen", [P, KW, 4], F32)
        spv = new("spv", [P, 8, KW], F32)
        bn = new("bn", [P, SEQ // P + 1, KD, 6], F32)
        bn_mv = new("bn_mv", [P, SEQ // P + 1, 2], F32)
        bn_rs = new("bn_rs", [P, SEQ // P + 1, 2], F32)
        h_last = new("h_last", [P, KW, 1 + B], F32)
        at_r = top[0]

        merged = at("merged", [P, KD, NT], F32, at_f)
        S = [at(f"scr{j}", [P, NT], F32, at_s + j * CH) for j in range(4)]

        y = [new(f"y{j}", [P, 2 * KW, NT], F32R) for j in range(3)]
        xc = new("xc", [P, KW, NT], F32)
        agate = new("agate", [P, KW, NT], F32)
        bconv = new("bconv", [P, KW, NT], F32)
        sm_hi = new("sm_hi", [P, 12, P], F32R)
        sm_lo = new("sm_lo", [P, 12, P], F32R)
        at_sig = take(2 * CH)
        at_u = take(5 * CH)
        at_st = at_u + 4 * 400
        st_s = at("st_s", [120, 3 * P], F32, at_st)
        st_p = at("st_p", [30, 4 * P], F32, at_st + 4 * 3 * P)
        st_ax = at("st_ax", [24, P], F32, at_st + 4 * 7 * P)
        st_sc = at("st_sc", [16, P], F32, at_st + 4 * 8 * P)
        sig = [at(f"sig{j}", [P, NT], F32, at_sig + j * CH) for j in range(2)]
        sq_th = at("sq_th", [P, KW, NT], F32, at_u)
        pool_t = at("pool_t", [P, KW, NT], F32, at_u)
        bsq = at("bsq", [P, KW, NT], F32, at_s)
        at_sm = at_r + 6 * KW * CH + 3 * KW * CH
        b_mean, b_std, b_tmp = (at(n, [P, NT], F32, at_sm + j * CH)
                                for j, n in enumerate(("b_mean", "b_std", "b_tmp")))
        packed = at("packed", [P, 400], F32, at_u)
        rgate = at("rgate", [P, NT], F32, at_u + 4 * CH)
        prod = at("prod", [P, NT], F32, at_sm + 3 * CH)
        Y_D, Y_C, Y_A = y
        at_y = at_r
        th = at("th", [P, KW, NT], F32, at_y)
        igate = at("igate", [P, KW, NT], F32, at_y + KW * CH)
        h_rows = at("h_rows", [1 + B, W], F32, at_u + 4 * CH)
        h_hi = at("h_hi", [P, KF, NT], F32R, at_r)
        h_lo = at("h_lo", [P, KF, NT], F32R, at_r + KF * CH)
        assert at_r + 2 * KF * CH <= nc.sbuf_usable_end
        NTILE = SEQ // P
        r_tok = at("r_tok", [P, NTILE, D], F32, at_f)
        at_t = at_r + 2 * KF * CH
        rs_tok = at("rs_tok", [B * T, D], F32, at_t)
        g_row = at("g_row", [P, D], F32, at_t + 4 * D)
        b_row = at("b_row", [P, D], F32, at_v)
        assert 4 * D <= 4 * KW * B * (30 + POOL_BUF) and at_t + 8 * D <= nc.sbuf_usable_end
        x_tok = at("x_tok", [P, SEQ // P, D], F32, at_y)
        at_i = at_y + SEQ // P * D * 4
        xs_tok = at("xs_tok", [B * T, D], F32, at_i)
        misc_tok = at("misc_tok", [M_ROWS, W], F32, at_i + 4 * D)
        conf_tok = at("conf_tok", [120, 2, W], F32, at_i + 4 * D + 4 * W)
        pool_tok = at("pool_tok", [120, W], F32, at_i + 4 * D + 12 * W)
        ln_tok = at("ln_tok", [32, P], F32, at_i + 4 * D + 16 * W)
        sm_raw = at("sm_raw", [P, 12, P], F32, at_i + 4 * D + 16 * W + 4 * P)
        assert at_i + 4 * D + 16 * W + 4 * P + 48 * P <= at_y + 6 * KW * CH
        PAD_A, PAD_B, PAD_C, PAD_D = RG_TAPS - 1, CF_TAPS - 1, POOL_BUF, SC_TAPS - 1
        t2 = [at_f]

        def pad(name, n, dt=F32):
            off = t2[0]
            t2[0] += (4 * n + 31) // 32 * 32
            assert t2[0] <= at_s + 4 * CH, name
            return at(name, [P, n], dt, off)

        def padded(w):
            return w + SEQ + B * (w + T)

        ax_pad = pad("ax_pad", padded(PAD_A))
        glu_pad = pad("glu_pad", padded(PAD_B))
        cin_pad = pad("cin_pad", padded(PAD_C))
        dch_pad = pad("dch_pad", padded(PAD_D))
        b_val, b_sig, d_b, d_c = (pad(n, NT) for n in ("b_val", "b_sig", "d_b", "d_c"))
        acc = [pad(f"acc{j}", padded(PAD_C)) for j in range(2)]

        main = ctx.enter_context(nc.psum_tensor("main", [P, 4, 512], F32))
        aux = ctx.enter_context(nc.psum_tensor("aux", [P, 4, 512], F32))

        def slot(s):
            return main[:, 2 * s:2 * s + 2, 0:HALF]

        def aslot(s):
            return aux[:, 2 * s:2 * s + 2, 0:HALF]

        def halves(ap):
            return ap.rearrange("p (h n) -> p h n", h=2)

        def steps(ap):
            return ap.rearrange("p (b t) -> p b t", b=B)

        def pr(buf, w, first, n=SEQ):
            return buf[:, first:first + n]

        def sa(buf, w, first, n=T, b0=0, b1=B):
            return steps(buf[:, w + SEQ:w + SEQ + B * (w + T)])[:, b0:b1, first:first + n]

        x_landed = [sem(f"x_landed{j}") for j in range(5)]
        small_landed = sem("small_landed")
        sm_zeroed = sem("sm_zeroed")
        sm_landed = sem("sm_landed")
        sm_hi_ready, sm_lo_ready = sem("sm_hi_ready"), sem("sm_lo_ready")
        consts = sem("consts")
        ident_ready = sem("ident_ready")
        turned = sem("turned")
        x_hi_ready, x_lo_ready = sem("x_hi_ready"), sem("x_lo_ready")
        misc_ready, conf_ready = sem("misc_ready"), sem("conf_ready")
        lam_ready, z_ready = sem("lam_ready"), sem("z_ready")
        raw_landed = [sem(f"raw_landed{s}") for s in range(RING)]
        w_hi_ready, w_lo_ready = sem("w_hi_ready"), sem("w_lo_ready")
        unit_done = sem("unit_done")
        tile_out = [sem("tile_out0"), sem("tile_out1")]
        glu_made, db_used, cin_used, ax_used = map(
            sem, ("glu_made", "db_used", "cin_used", "ax_used"))
        tails_taken, tails_out, tails_stored = sem("tails_taken"), sem("tails_out"), sem("tails_stored")
        rows_packed = sem("rows_packed")
        dve = sem("dve_steps")
        act_own = sem("act_steps")
        yd_ready = sem("yd_ready")
        side_done, side_out = sem("side_done"), sem("side_out")
        yc_ready, sqrt_ready = sem("yc_ready"), sem("sqrt_ready")
        yc_split = sem("yc_split")
        ya_ready, yb_ready = sem("ya_ready"), sem("yb_ready")
        h_turned, h_copied = sem("h_turned"), sem("h_copied")
        bsq_ready, bvar_ready, bstd_ready, bnorm_ready, bsig_ready = map(
            sem, ("bsq_ready", "bvar_ready", "bstd_ready", "bnorm_ready", "bsig_ready"))
        merged_ready = sem("merged_ready")
        r_ready, rsq_ready, stat_done = sem("r_ready"), sem("rsq_ready"), sem("stat_done")
        var_ready, std_ready = sem("var_ready"), sem("std_ready")
        norm_ready, affine_ready, x1_hi_ready, x1_lo_ready = map(
            sem, ("norm_ready", "affine_ready", "x1_hi_ready", "x1_lo_ready"))
        hid_hi_ready, hid_lo_ready = map(sem, ("hid_hi_ready", "hid_lo_ready"))
        rows_turned, rows_out = sem("rows_turned"), sem("rows_out")
        row_vecs, bn_zero = sem("row_vecs"), sem("bn_zero")
        bn_var, bn_std, bn_scale = sem("bn_var"), sem("bn_std"), sem("bn_scale")
        row_normed, rows_ready, pool_rows = sem("row_normed"), sem("rows_ready"), sem("pool_rows")
        stored = sem("stored")

        w_in = i_["w_in"].rearrange("a (k p) n -> p (a k) n", p=P)
        w_br = i_["w_branch"].rearrange("a b (k p) n -> p (a b k) n", p=P)
        w_out = i_["w_out"].rearrange("a (k p) n -> p (a k) n", p=P)
        w_g = i_["w_ff_gate"].rearrange("a (k p) n -> p (a k) n", p=P)
        w_u = i_["w_ff_up"].rearrange("a (k p) n -> p (a k) n", p=P)
        w_d = i_["w_ff_down"].rearrange("a (k p) n -> p (a k) n", p=P)
        x_p = i_["x_prompt"].rearrange("a (j p) d -> p (a j) d", p=P)
        x_s = i_["x_sample"].rearrange("b t d -> (b t) d")
        o_x = o_["y_prompt"].rearrange("a (j p) d -> p (a j) d", p=P)
        o_s = o_["y_sample"].rearrange("b t d -> (b t) d")

        def rows2(ap):
            return ap.rearrange("a b w -> (a b) w")

        def rows3(ap):
            return ap.rearrange("a b r w -> (a b r) w")

        block = ctx.enter_context(nc.Block())

        @block.sync
        def _(sp):
            nc.disable_value_cache = True

            def unit(u, s, src):
                if not (isinstance(u, int) and u < RING):
                    sp.wait_ge(w_lo_ready, u - (RING - 1))
                sp.dma_start(raw[s][:, 0:src.shape[1], :], src).then_inc(raw_landed[s], 16)

            for j in range(SEQ // P):
                sp.dma_start(x_tok[:, j, :], x_p[:, j, :]).then_inc(x_landed[j], 16)
            sp.dma_start(xs_tok[:, :], x_s).then_inc(x_landed[4], 16)

            def in_col(idx, c):
                return w_in[:, :, ds(IN_ORDER[idx] * W + c * P, P)]

            for idx in range(RING):
                unit(idx, idx, in_col(idx, 0))
            sp.wait_ge(sm_zeroed, 1)
            for k0, name in ((0, "rg_w_a"), (KW, "rg_w_x")):
                w = i_[name].rearrange("a (c two) i j -> (a two) i c j", two=2)
                for two in range(2):
                    q = slice(64 * two, 64 * two + 64)
                    sp.dma_start(sm_raw[q, k0:k0 + KW, q], w[two]).then_inc(sm_landed, 16)
            sp.dma_start(sm_raw[:, 2 * KW:3 * KW, :],
                         i_["pool_w"].rearrange("a g i j -> i (a g) j")).then_inc(sm_landed, 16)
            with sp.Fori(1, KW - 1 + 1) as c_1:
                c = c_1 - 1
                for idx in range(RING, 8):
                    unit(c * 8 + idx, idx % RING, in_col(idx, c))
                for idx in range(RING):
                    unit(c * 8 + 8 + idx, idx % RING, in_col(idx, c + 1))
            for idx in range(RING, 8):
                unit(8 * (KW - 1) + idx, idx % RING, in_col(idx, KW - 1))
            for q, n in enumerate(BRANCH_ORDER):
                with sp.Fori(1, KD // 2 + 1) as i_1:
                    i = i_1 - 1
                    for mm in range(2):
                        u = i * 4 + (U_MIX + 16 * q + 2 * mm)
                        unit(u, 2 * mm, w_in[:, :, ds(i * (2 * P) + (GATE_COL + D * n + P * mm), P)])
                        unit(u + 1, 2 * mm + 1, w_br[:, n * KW:(n + 1) * KW, ds(i * (2 * P) + P * mm, P)])
            sp.wait_ge(h_copied, 1)
            sp.dma_start(rows2(o_["prompt_h"]), h_rows[0:1, :]).then_inc(stored, 16)
            sp.dma_start(rows2(o_["sample_h"]), h_rows[1:1 + B, :]).then_inc(stored, 16)
            with sp.Fori(1, KD // RING + 1) as i_1:
                i = i_1 - 1
                for m in range(RING):
                    unit(i * RING + (U_OUT + m), m, w_out[:, :, ds(i * (RING * P) + m * P, P)])
            with sp.Fori(1, KF // 2 + 1) as i_1:
                i = i_1 - 1
                for mm in range(2):
                    u = i * 4 + (U_FF + 2 * mm)
                    unit(u, 2 * mm, w_g[:, :, ds(i * (2 * P) + P * mm, P)])
                    unit(u + 1, 2 * mm + 1, w_u[:, :, ds(i * (2 * P) + P * mm, P)])
            sp.wait_ge(stored, 2 * 16)
            for dst, name in ((g_row, "ln2_g"), (b_row, "ln2_b")):
                sp.dma_start(dst[:, :], i_[name].to_broadcast([P, D])).then_inc(row_vecs, 16)
            with sp.Fori(1, KD // 4 + 1) as i_1:
                i = i_1 - 1
                for m in range(4):
                    k = 0
                    for part, n in enumerate(DOWN_SPLIT):
                        j = 3 * m + part
                        unit(i * 12 + (U_DOWN + j), j % RING, w_d[:, k:k + n, ds(i * (4 * P) + m * P, P)])
                        k += n
            for n, (rdy, cnt, dst, src) in enumerate((
                    (rows_ready, 1, o_x[:, 0, :], r_tok[:, 0, :]), (rows_ready, 2, o_x[:, 1, :], r_tok[:, 1, :]),
                    (pool_rows, 2, o_x[:, 3, :], r_tok[:, 3, :]), (rows_ready, 3, o_x[:, 2, :], r_tok[:, 2, :]),
                    (rows_ready, 4, o_s, rs_tok[:, :]))):
                sp.wait_ge(rdy, cnt)
                sp.dma_start(dst, src).then_inc(stored, 16)
            sp.wait_ge(stored, 16 * 7)
            sp.wait_ge(tails_stored, 1 + 9 * 16 * KW)
            nc.disable_value_cache = False

        @block.gpsimd
        def _(pool):
            pool.memset(ident[:, :], 0.0).then_inc(consts, 1)
            pool.wait_ge(consts, 1)
            pool.affine_select(out=ident[:, :], in_=ident[:, :], compare_op=ALU.not_equal, fill=1.0,
                               base=0, pattern=[[-1, P]], channel_multiplier=1).then_inc(ident_ready, 1)
            pool.memset(sm_raw[:, :, :], 0.0).then_inc(sm_zeroed, 1)
            pool.memset(ones[:, :], 1.0).then_inc(consts, 1)
            pool.memset(glu_pad[:, 0:PAD_B], 0.0).then_inc(glu_made, 1)
            pool.memset(dch_pad[:, 0:PAD_D], 0.0)
            pool.memset(cin_pad[:, 0:PAD_C], 0.0).then_inc(cin_used, 1)
            pool.memset(ax_pad[:, 0:PAD_A], 0.0).then_inc(ax_used, 1)
            pool.memset(st_s[:, :], 0.0).then_inc(tails_stored, 1)
            pool.memset(bn_mv[:, :, :], 1.0).then_inc(bn_zero, 1)
            pool.memset(widen[:, :, :], 0.0).then_inc(consts, 1)
            pool.wait_ge(consts, 3)
            for c in range(KW):
                window = 2 << c
                for j in range(c):
                    pool.memset(widen[:, c, j:j + 1], 1.0)
                pool.memset(widen[:, c, 3:4], 1.0 / window)
                for t in range(POOL_BUF):
                    pool.memset(inv_count[:, c, t:t + 1], 1.0 / min(window, t + 1))
            pool.memset(d_b[:, 0:1], 0.0).then_inc(db_used, 1)

            def lo(u, s, n):
                pool.wait_ge(w_hi_ready, u + 1)
                pool.tensor_tensor(w_lo[s][:, 0:n, :], raw[s][:, 0:n, :], w_hi[s][:, 0:n, :].bitcast(F32),
                                   ALU.subtract).then_inc(w_lo_ready, 1)

            with pool.Fori(0, 1) as i:
                for u in range(RING):
                    lo(i * RING + u, u, 8)
            pool.wait_ge(sm_hi_ready, 1)
            pool.tensor_tensor(sm_lo[:, :, :], sm_raw[:, :, :], sm_hi[:, :, :].bitcast(F32),
                               ALU.subtract).then_inc(sm_lo_ready, 1)
            with pool.Fori(1, U_MIX // RING) as i:
                for u in range(RING):
                    lo(i * RING + u, u, 8)
            with pool.Fori(0, (U_OUT - U_MIX) // RING) as i:
                for u in range(RING):
                    lo(i * RING + (U_MIX + u), u, (8, KW)[u % 2])
            with pool.Fori(0, KD // RING) as i:
                for u in range(RING):
                    lo(i * RING + (U_OUT + u), u, 8)
            for k in range(KD):
                pool.wait_ge(x1_hi_ready, k + 1)
                pool.tensor_tensor(x_lo[:, k, :], merged[:, k, :], x_hi[:, k, :].bitcast(F32),
                                   ALU.subtract).then_inc(x1_lo_ready, 1)
            with pool.Fori(0, 2 * KF // RING) as i:
                for u in range(RING):
                    lo(i * RING + (U_FF + u), u, 8)
            with pool.Fori(0, KD // 4) as i:
                for j in range(12):
                    lo(i * 12 + (U_DOWN + j), j % RING, DOWN_SPLIT[j % 3])
            pool.wait_ge(row_vecs, 32)
            pool.wait_ge(row_normed, 1)
            pool.tensor_tensor(r_tok[:, 3, :], r_tok[:, 3, :], g_row[:, :], ALU.mult).then_inc(pool_rows, 1)
            pool.wait_ge(pool_rows, 1)
            pool.tensor_tensor(r_tok[:, 3, :], r_tok[:, 3, :], b_row[:, :], ALU.add).then_inc(pool_rows, 1)

        @block.scalar
        def _(act):
            own = Chain(act, act_own)

            def hi(u, s):
                act.wait_ge(raw_landed[s], (u // RING) * 16 + 16 if isinstance(u, int) else u_quot(u, s))
                act.activation(w_hi[s][:, :, :], raw[s][:, :, :], ACT.Copy).then_inc(w_hi_ready, 1)

            def u_quot(u, s):
                return (u - s) * (16 // RING) + 16

            small = ((misc_tok[M_CONV:M_SC, :], rows3(i_["state_rglru_conv"])),
                     (misc_tok[M_SC:M_H, :], rows3(i_["state_shortconv"])),
                     (misc_tok[M_H:V_RGW, :], rows2(i_["state_rglru_h"])),
                     (misc_tok[V_RGW:V_RGB, :], rows2(i_["rg_conv_w"])),
                     (misc_tok[V_RGB:V_RGB + 1, :], i_["rg_conv_b"]),
                     (misc_tok[V_BA:V_BA + 1, :], i_["rg_b_a"]),
                     (misc_tok[V_BX:V_BX + 1, :], i_["rg_b_x"]),
                     (misc_tok[V_LAM:V_LAM + 1, :], i_["rg_lambda"]),
                     (misc_tok[V_CFW:V_CFB, :], rows2(i_["cf_conv_w"])),
                     (misc_tok[V_CFB:V_CFB + 1, :], i_["cf_conv_b"]),
                     (misc_tok[V_CFG:V_CFG + 1, :], i_["cf_ln_g"]),
                     (misc_tok[V_CFLB:V_CFLB + 1, :], i_["cf_ln_b"]),
                     (misc_tok[V_PSC:V_PSC + 1, :], i_["pool_scale"]),
                     (misc_tok[V_SCW:M_ROWS, :], rows2(i_["sc_conv_w"])),
                     (conf_tok[:, 0, :], rows3(i_["state_conformer_conv"])[0:120, :]),
                     (conf_tok[:, 1, :], rows3(i_["state_conformer_conv"])[120:240, :]),
                     (pool_tok[:, :], rows3(i_["state_pool"]))) + tuple(
                         (ln_tok[8 * j:8 * j + 8, :], i_[n].rearrange("a (k p) -> (a k) p", p=P))
                         for j, n in enumerate(("ln1_g", "ln1_b", "ln2_g", "ln2_b")))
            assert len(small) == N_SMALL
            for dst, src in small:
                act.dma_start(dst, src).then_inc(small_landed, 16)
            for k in range(KD):
                act.wait_ge(turned, k + 1)
                bank = (main, aux)[k // 4]
                act.activation(x_hi[:, k, 0:SEQ], bank[:, k % 4, :], ACT.Copy).then_inc(x_hi_ready, 1)
            act.wait_ge(turned, KD + 1)
            act.activation(x_hi[:, :, SEQ:NT], main[:, 0, 0:256].rearrange("p (k n) -> p k n", k=KD),
                           ACT.Copy).then_inc(x_hi_ready, 1)
            hi(0, 0)
            for g in range(2):
                act.wait_ge(turned, KD + 3 + g)
                act.activation(confT[:, 2 * g:2 * g + 2, :],
                               main[:, 2 + g, 0:480].rearrange("p (c n) -> p c n", c=2), ACT.Copy)\
                   .then_inc(conf_ready if g == 0 else tile_out[1], 1)
            act.wait_ge(turned, KD + 5)
            act.activation(poolT[:, :, :], aux[:, 0, 0:480].rearrange("p (c n) -> p c n", c=KW), ACT.Copy)\
               .then_inc(tails_out, 1)
            for u in range(1, RING):
                hi(u, u)
            act.wait_ge(lam_ready, 1)
            act.activation(spv[:, 1, :], spv[:, 0, :], ACT.Exp).then_inc(z_ready, 1)
            act.wait_ge(sm_landed, 5 * 16)
            act.activation(sm_hi[:, :, :], sm_raw[:, :, :], ACT.Copy).then_inc(sm_hi_ready, 1)

            def in_tile(idx, c):
                kind = IN_ORDER[idx]
                u = c * 8 + idx
                act.wait_ge(unit_done, u + 1)
                ps = slot(idx % 2)
                out_sem = tile_out[idx % 2]
                if kind == B_VAL:
                    act.wait_ge(glu_made, c + 1)
                    act.activation(halves(b_val[:, :]), ps, ACT.Copy).then_inc(out_sem, 1)
                elif kind == B_GATE:
                    act.activation(halves(b_sig[:, :]), ps, ACT.Sigmoid).then_inc(out_sem, 1)
                elif kind == D_C:
                    act.activation(halves(d_c[:, :]), ps, ACT.Copy).then_inc(out_sem, 1)
                elif kind == D_B:
                    act.wait_ge(db_used, c + 1)
                    act.activation(halves(d_b[:, :]), ps, ACT.Copy).then_inc(out_sem, 1)
                elif kind in (C_IN, A_X):
                    buf, w, used = ((cin_pad, PAD_C, cin_used) if kind == C_IN
                                    else (ax_pad, PAD_A, ax_used))
                    act.wait_ge(used, c + 1)
                    act.wait_ge(tails_taken, c + 1)
                    a, b = ps[:, 0, :], ps[:, 1, :]
                    act.activation(buf[:, w:w + HALF], a, ACT.Copy)
                    act.activation(buf[:, w + HALF:w + SEQ], b[:, 0:SEQ - HALF], ACT.Copy)
                    act.activation(sa(buf, w, w), steps(b[:, SEQ - HALF:HALF]), ACT.Copy)\
                       .then_inc(out_sem, 1)
                elif kind == A_GATE:
                    act.activation(halves(agate[:, c, :]), ps, ACT.Copy).then_inc(out_sem, 1)
                hi(u + RING, idx % RING)

            def pack_tails(c):
                act.wait_ge(ax_used, c + 2)
                for (buf, w, n0, n1) in ((glu_pad, PAD_B, 0, 240), (cin_pad, PAD_C, 240, 360),
                                         (ax_pad, PAD_A, 360, 384), (dch_pad, PAD_D, 384, 400)):
                    ins = act.activation(steps(packed[:, n0:n1]), sa(buf, w, T, w), ACT.Copy)
                ins.then_inc(rows_packed, 1)

            def store_tails(c):
                act.wait_ge(tails_taken, c + 2)
                act.wait_ge(tails_stored, c * (9 * 16) + 1)
                act.activation(st_s[:, :], aux[0:120, 0, 0:3 * P], ACT.Copy)
                act.activation(st_p[:, :], aux[0:30, 1, 0:4 * P], ACT.Copy)
                act.activation(st_ax[:, :], aux[0:24, 2, 0:P], ACT.Copy)
                act.activation(st_sc[:, :], aux[0:16, 2, P:2 * P], ACT.Copy).then_inc(tails_out, 1)
                act.wait_ge(tails_out, c + 2)
                cols = ds(c * P, P)
                for dst, r0, r1, src in (
                        ("sample_cf", 0, 120, st_s[:, 0:P]), ("sample_cf", 120, 240, st_s[:, P:2 * P]),
                        ("sample_pool", 0, 120, st_s[:, 2 * P:3 * P]),
                        ("prompt_rgc", 0, 3, st_p[27:30, 0:P]), ("prompt_cf", 0, 30, st_p[:, P:2 * P]),
                        ("prompt_pool", 0, 15, st_p[15:30, 2 * P:3 * P]),
                        ("prompt_sc", 0, 2, st_p[28:30, 3 * P:4 * P]),
                        ("sample_rgc", 0, 24, st_ax[:, :]), ("sample_sc", 0, 16, st_sc[:, :])):
                    act.dma_start(rows3(o_[dst])[r0:r1, cols], src).then_inc(tails_stored, 16)

            for idx in range(2):
                in_tile(idx, 0)
            with act.Fori(0, KW - 1) as c:
                for idx in range(2, 8):
                    in_tile(idx, c)
                in_tile(0, c + 1)
                pack_tails(c)
                in_tile(1, c + 1)
                store_tails(c)
            for idx in range(2, 8):
                in_tile(idx, KW - 1)

            def gate(u, s, mm):
                act.wait_ge(unit_done, u + 1)
                act.activation(halves(sig[mm][:, :]), slot(0), ACT.Sigmoid).then_inc(tile_out[0], 1)
                hi(u + RING, s)

            def used(u, s):
                act.wait_ge(unit_done, u + 1)
                hi(u + RING, s)

            def pairs(q, i, tails=False):
                u = i * 4 + (U_MIX + 16 * q)
                gate(u, 0, 0)
                if tails:
                    pack_tails(KW - 1)
                used(u + 1, 1)
                if tails:
                    store_tails(KW - 1)
                if q == 2:
                    act.wait_ge(bnorm_ready, i + 1)
                    act.activation(S[3][:, :], S[2][:, :], ACT.Sigmoid).then_inc(bsig_ready, 1)
                gate(u + 2, 2, 1)
                used(u + 3, 3)

            for q in range(4):
                if q == 0:
                    pairs(0, 0, tails=True)
                with act.Fori(1 if q == 0 else 0, KD // 2) as i:
                    pairs(q, i)
                if q == 0:
                    act.wait_ge(tails_stored, 1 + 9 * 16 * KW)
                    act.wait_ge(tile_out[1], (U_MIX + 16) // 2 + 1)
                    act.activation(bsq[:, :, :], bconv[:, :, :], ACT.Square).then_inc(bsq_ready, 1)
                    for c in range(KW):
                        act.wait_ge(side_done, c + 1)
                        act.activation(halves(pool_t[:, c, :]), aslot(c % 2), ACT.Copy,
                                       scale=miscT[:, c, V_PSC:V_PSC + 1]).then_inc(side_out, 1)
                        act.wait_ge(side_out, c + 1)
                        act.activation(Y_C[:, c, :], pool_t[:, c, :], ACT.Copy).then_inc(yc_ready, 1)
                    for c in range(KW):
                        act.wait_ge(side_done, KW + 2 * c + 1)
                        if c:
                            act.wait_ge(act_own, c)
                        act.activation(halves(rgate[:, :]), aslot(0), ACT.Sigmoid,
                                       bias=miscT[:, c, V_BA:V_BA + 1]).then_inc(side_out, 1)
                        act.wait_ge(side_done, KW + 2 * c + 2)
                        act.activation(halves(igate[:, c, :]), aslot(1), ACT.Sigmoid,
                                       bias=miscT[:, c, V_BX:V_BX + 1]).then_inc(side_out, 1)
                        act.wait_ge(side_out, KW + 2 * c + 1)
                        own.link(act.activation(th[:, c, :], rgate[:, :], ACT.Tanh,
                                                scale=spv[:, 7, c:c + 1]))
                    act.wait_ge(act_own, KW)
                    act.wait_ge(yc_split, KW)
                    act.activation(sq_th[:, :, :], th[:, :, :], ACT.Sqrt, bias=1e-30)
                    act.activation(agate[:, :, :], agate[:, :, :], ACT.Gelu_apprx_tanh)\
                       .then_inc(sqrt_ready, 1)
                    act.wait_ge(bvar_ready, 1)
                    act.activation(b_std[:, :], b_std[:, :], ACT.Sqrt).then_inc(bstd_ready, 1)
                if q == 2:
                    act.wait_ge(h_turned, 1)
                    act.activation(h_rows[:, :], aux[0:1 + B, 0, :], ACT.Copy).then_inc(h_copied, 1)

            def residual_squares(m, n0=0):
                act.wait_ge(r_ready, n0 + m + 1)
                if n0 + m >= 2:
                    act.wait_ge(stat_done, n0 + m - 1)
                act.activation(S[m % 2][:, :], merged[:, m, :], ACT.Square).then_inc(rsq_ready, 1)

            def layer_norm_tail(j):
                act.wait_ge(var_ready, j + 1)
                act.activation(S[3][:, :], S[3][:, :], ACT.Sqrt).then_inc(std_ready, 1)
                for k in range(KD):
                    act.wait_ge(norm_ready, j * KD + k + 1)
                    act.activation(merged[:, k, :], merged[:, k, :], ACT.Identity,
                                   scale=lnT[:, 16 * j + k:16 * j + k + 1],
                                   bias=lnT[:, 16 * j + 8 + k:16 * j + 9 + k]).then_inc(affine_ready, 1)
                    if j == 0:
                        act.wait_ge(affine_ready, k + 1)
                        act.activation(x_hi[:, k, :], merged[:, k, :], ACT.Copy).then_inc(x1_hi_ready, 1)

            for m in range(KD):
                used(U_OUT + m, m % RING)
                residual_squares(m, 0)
            layer_norm_tail(0)

            with act.Fori(0, KF // 2) as i:
                for mm in range(2):
                    u = i * 4 + (U_FF + 2 * mm)
                    act.wait_ge(unit_done, u + 1)
                    act.activation(halves(S[mm][:, :]), slot(0), ACT.Silu).then_inc(tile_out[0], 1)
                    hi(u + RING, 2 * mm)
                    used(u + 1, 2 * mm + 1)
                    act.wait_ge(tile_out[1], i * 2 + (U_FF // 2 + mm + 2))
                    act.activation(h_hi[:, i * 2 + mm, :], S[2 + mm][:, :], ACT.Copy).then_inc(hid_hi_ready, 1)
            def rows(m):
                act.wait_ge(rows_turned, m + 1)
                act.activation(r_tok[:, :, m * P:m * P + P],
                               aux[:, m % 2, :].rearrange("p (j n) -> p j n", j=NTILE), ACT.Copy)
                act.activation(rs_tok[:, m * P:m * P + P], aux[0:B * T, 2 + m % 2, 0:P], ACT.Copy)\
                   .then_inc(rows_out, 1)

            for m in range(KD):
                for part in range(3):
                    u = U_DOWN + 3 * m + part
                    if u + RING < U_END:
                        used(u, u % RING)
                if m >= 1:
                    rows(m - 1)
            rows(KD - 1)
            act.wait_ge(bn_var, 1)
            act.activation(bn_rs[:, :, 0:1], bn_mv[:, :, 1:2], ACT.Sqrt, bias=EPS).then_inc(bn_std, 1)
            act.wait_ge(bn_scale, 1)
            for j in (3, 0, 1, 2, 4):
                n = P if j < NTILE else B * T
                t = r_tok[:, j, :] if j < NTILE else rs_tok[:, :]
                act.activation(t, t, ACT.Identity, scale=bn_rs[0:n, j, 0:1], bias=bn_rs[0:n, j, 1:2])\
                   .then_inc(row_normed, 1)

        @block.tensor
        def _(pe):
            def passes(ps, pairs, last):
                n = len(pairs)
                for k, (wh, wl, xh, xl) in enumerate(pairs):
                    for j, (w, x) in enumerate(((wl, xh), (wh, xl), (wh, xh))):
                        for h in range(2):
                            mm = pe.matmul(ps[:, h, :], w, x[:, h * HALF:(h + 1) * HALF],
                                           start=(k == 0 and j == 0), stop=(last and k == n - 1 and j == 2))
                return mm

            def unit(u, s, xs, ps_slot, first=True, last=True, n0=0, ready=None):
                pe.wait_ge(w_lo_ready, u + 1)
                n = len(xs)
                for k, (xh, xl) in enumerate(xs):
                    if ready:
                        pe.wait_ge(ready, k + 1)
                    for j, (w, x) in enumerate(((w_lo, xh), (w_hi, xl), (w_hi, xh))):
                        for h in range(2):
                            mm = pe.matmul(slot(ps_slot)[:, h, :], w[s][:, k, :],
                                           x[:, h * HALF:(h + 1) * HALF],
                                           start=(first and k == 0 and j == 0),
                                           stop=(last and k == n - 1 and j == 2))
                mm.then_inc(unit_done, 1)

            pe.wait_ge(ident_ready, 1)
            for j in range(SEQ // P):
                pe.wait_ge(x_landed[j], 16)
            for k in range(KD):
                bank = (main, aux)[k // 4]
                for j in range(SEQ // P):
                    mm = pe.transpose(bank[:, k % 4, j * P:j * P + P], x_tok[:, j, k * P:k * P + P],
                                      ident[:, :])
                mm.then_inc(turned, 1)
            pe.wait_ge(x_landed[4], 16)
            pe.wait_ge(x_lo_ready, 1)
            for k in range(KD):
                mm = pe.transpose(main[:, 0, k * 32:k * 32 + 32], xs_tok[:, k * P:k * P + P],
                                  ident[0:32, 0:32])
            mm.then_inc(turned, 1)
            pe.wait_ge(small_landed, 16 * N_SMALL)
            pe.wait_ge(x_lo_ready, 2)
            for c in range(KW):
                pe.transpose(main[:, 1, c * M_ROWS:(c + 1) * M_ROWS], misc_tok[:, c * P:c * P + P],
                             ident[0:M_ROWS, 0:M_ROWS])
            pe.transpose(main[:, 1, KW * M_ROWS:KW * M_ROWS + 32], ln_tok[:, :], ident[0:32, 0:32])\
              .then_inc(turned, 1)
            for g in range(2):
                pe.wait_ge(x_lo_ready, 3 + g)
                for c in range(2):
                    for half in range(2):
                        mm = pe.transpose(main[:, 2 + g, c * 240 + half * 120:c * 240 + half * 120 + 120],
                                          conf_tok[:, half, (2 * g + c) * P:(2 * g + c + 1) * P],
                                          ident[0:120, 0:120])
                mm.then_inc(turned, 1)
            pe.wait_ge(x_lo_ready, 5)
            for c in range(KW):
                mm = pe.transpose(aux[:, 0, c * 120:c * 120 + 120], pool_tok[:, c * P:c * P + P],
                                  ident[0:120, 0:120])
            mm.then_inc(turned, 1)
            pe.wait_ge(x_lo_ready, KD + 1)
            pe.wait_ge(misc_ready, 1)
            pe.wait_ge(tails_out, 1)
            pe.transpose(aux[:, 1, 0:P], ident[:, :], ident[:, :]).then_inc(tails_taken, 1)

            x_in = [(x_hi[:, k, :], x_lo[:, k, :]) for k in range(KD)]
            def in_tile(idx, c):
                pe.wait_ge(tile_out[idx % 2], c * 4 + (idx // 2 + 1))
                unit(c * 8 + idx, idx % RING, x_in, idx % 2)

            def turn_tails(c):
                pe.wait_ge(ax_used, c + 2)
                pe.wait_ge(tails_out, c + 1)
                for j, (buf, w) in enumerate(((ax_pad, PAD_A), (glu_pad, PAD_B), (cin_pad, PAD_C),
                                              (dch_pad, PAD_D))):
                    pe.transpose(aux[0:30, 1, j * P:j * P + P], buf[:, w + SEQ - 30:w + SEQ], ident[:, :])
                pe.wait_ge(rows_packed, c + 1)
                for j in range(3):
                    pe.transpose(aux[0:120, 0, j * P:j * P + P], packed[:, 120 * j:120 * j + 120], ident[:, :])
                pe.transpose(aux[0:24, 2, 0:P], packed[:, 360:384], ident[:, :])
                pe.transpose(aux[0:16, 2, P:2 * P], packed[:, 384:400], ident[:, :])\
                  .then_inc(tails_taken, 1)

            for idx in range(2):
                in_tile(idx, 0)
            with pe.Fori(0, KW - 1) as c:
                for idx in range(2, 8):
                    in_tile(idx, c)
                for idx in range(2):
                    in_tile(idx, c + 1)
                turn_tails(c)
            for idx in range(2, 8):
                in_tile(idx, KW - 1)

            def pairs(q, i, xs, branch_ready, tails=False):
                for mm_ in range(2):
                    u = i * 4 + (U_MIX + 16 * q + 2 * mm_)
                    t2_ = i * 2 + ((U_MIX + 16 * q) // 2 + mm_ + 1)
                    pe.wait_ge(tile_out[0], t2_)
                    unit(u, 2 * mm_, x_in, 0)
                    if tails and mm_ == 0:
                        turn_tails(KW - 1)
                    pe.wait_ge(tile_out[1], t2_)
                    pe.wait_ge(branch_ready, KW)
                    unit(u + 1, 2 * mm_ + 1, xs, 1)

            for q in range(4):
                yq = (Y_D, Y_C, Y_A, Y_D)[q]
                xs = [(yq[:, k, :], yq[:, KW + k, :]) for k in range(KW)]
                if q == 1:
                    pe.wait_ge(sm_lo_ready, 1)
                    for j in range(3 * KW):
                        if j < KW:
                            c, t, src = j, 2 * KW + j, Y_C
                        else:
                            c = (j - KW) // 2
                            t, src = ((j - KW) % 2) * KW + c, Y_A
                        if j >= 2:
                            pe.wait_ge(side_out, j - 1)
                        passes(aslot(j % 2), [(sm_hi[:, t, :], sm_lo[:, t, :], src[:, c, :],
                                               src[:, KW + c, :])], True).then_inc(side_done, 1)
                    pe.wait_ge(bsq_ready, 1)
                    for s, src in ((0, bconv), (1, bsq)):
                        pe.wait_ge(side_out, 3 * KW - 1 + s)
                        for c in range(KW):
                            for h in range(2):
                                mm = pe.matmul(aslot(s)[:, h, :], ones[:, :],
                                               src[:, c, h * HALF:(h + 1) * HALF],
                                               start=(c == 0), stop=(c == KW - 1))
                        mm.then_inc(side_done, 1)
                if q == 3:
                    for c in range(KW):
                        mm = pe.transpose(aux[0:1 + B, 0, c * P:c * P + P], h_last[:, c, :], ident[:, :])
                    mm.then_inc(h_turned, 1)
                branch_ready = (yd_ready, yc_split, ya_ready, yb_ready)[q]
                if q == 0:
                    pairs(0, 0, xs, branch_ready, tails=True)
                with pe.Fori(1 if q == 0 else 0, KD // 2) as i:
                    pairs(q, i, xs, branch_ready)

            def sums(m, n0):
                pe.wait_ge(rsq_ready, n0 + m + 1)
                for s, src in ((0, merged[:, m, :]), (1, S[m % 2][:, :])):
                    for h in range(2):
                        mm = pe.matmul(aslot(s)[:, h, :], ones[:, :], src[:, h * HALF:(h + 1) * HALF],
                                       start=(m == 0), stop=(m == KD - 1))
                mm.then_inc(stat_done, 1)

            xs = [(Y_C[:, k, :], Y_A[:, k, :]) for k in range(KD)]
            for m in range(KD):
                u = U_OUT + m
                pe.wait_ge(tile_out[m % 2], u // 2 + 1)
                unit(u, u % RING, xs, m % 2, ready=merged_ready if m == 0 else None)
                if m >= 1:
                    sums(m - 1, 0)
            sums(KD - 1, 0)

            pe.wait_ge(tile_out[0], U_FF // 2 + 1)
            unit(U_FF, 0, x_in, 0, ready=x1_lo_ready)
            pe.wait_ge(tile_out[1], U_FF // 2 + 1)
            unit(U_FF + 1, 1, x_in, 1)
            with pe.Fori(0, KF // 2 - 1) as i:
                for j in range(2):
                    t2_ = i * 2 + (U_FF // 2 + 2 + j)
                    pe.wait_ge(tile_out[0], t2_)
                    unit(i * 4 + (U_FF + 2 + 2 * j), (2 + 2 * j) % RING, x_in, 0)
                    pe.wait_ge(tile_out[1], t2_)
                    unit(i * 4 + (U_FF + 3 + 2 * j), (3 + 2 * j) % RING, x_in, 1)
            pe.wait_ge(tile_out[0], U_DOWN // 2)
            unit(U_DOWN - 2, 2, x_in, 0)
            pe.wait_ge(tile_out[1], U_DOWN // 2)
            unit(U_DOWN - 1, 3, x_in, 1)

            def turn_rows(m):
                pe.wait_ge(r_ready, KD + m + 1)
                if m >= 2:
                    pe.wait_ge(rows_out, m - 1)
                r = S[m % 2]
                for j in range(NTILE):
                    pe.transpose(aux[:, m % 2, j * P:j * P + P], r[:, j * P:j * P + P], ident[:, :])
                pe.transpose(aux[0:B * T, 2 + m % 2, 0:P], r[:, SEQ:NT], ident[:, :]).then_inc(rows_turned, 1)

            pe.wait_ge(hid_lo_ready, KF - 1)
            for m in range(KD):
                pe.wait_ge(tile_out[m % 2], U_DOWN // 2 + m // 2 + 1)
                k = 0
                for part, n in enumerate(DOWN_SPLIT):
                    u = U_DOWN + 3 * m + part
                    if m == 0 and part == 2:
                        pe.wait_ge(hid_lo_ready, KF)
                    unit(u, u % RING, [(h_hi[:, k + j, :], h_lo[:, k + j, :]) for j in range(n)], m % 2,
                         first=(part == 0), last=(part == 2))
                    k += n
                if m >= 1:
                    turn_rows(m - 1)
            turn_rows(KD - 1)

        @block.vector
        def _(ve):
            ch = Chain(ve, dve)
            link, after = ch.link, ch.after

            def vec(c, j):
                return miscT[:, c, j:j + 1]

            for k in range(KD):
                ve.wait_ge(x_hi_ready, k + 1)
                bank = (main, aux)[k // 4]
                ve.tensor_tensor(x_lo[:, k, 0:SEQ], bank[:, k % 4, :], x_hi[:, k, 0:SEQ].bitcast(F32),
                                 ALU.subtract).then_inc(x_lo_ready, 1)
            ve.wait_ge(x_hi_ready, KD + 1)
            ve.tensor_tensor(x_lo[:, :, SEQ:NT], main[:, 0, 0:256].rearrange("p (k n) -> p k n", k=KD),
                             x_hi[:, :, SEQ:NT].bitcast(F32), ALU.subtract).then_inc(x_lo_ready, 1)
            ve.wait_ge(turned, KD + 2)
            ve.tensor_copy(miscT[:, :, :], main[:, 1, 0:KW * M_ROWS].rearrange("p (c n) -> p c n", c=KW))\
              .then_inc(misc_ready, 1)
            ve.tensor_copy(lnT[:, :], main[:, 1, KW * M_ROWS:KW * M_ROWS + 32]).then_inc(tile_out[0], 1)
            ve.wait_ge(misc_ready, 1)
            lam = miscT[:, :, V_LAM:V_LAM + 1].rearrange("p c o -> p (c o)")
            after(link(ve.tensor_scalar(spv[:, 2, :], lam, -1.0, None, ALU.mult)))
            ve.tensor_tensor(spv[:, 0, :], lam, spv[:, 2, :], ALU.min).then_inc(lam_ready, 1)
            after(link(ve.tensor_scalar(spv[:, 3, :], spv[:, 2, :], 0.0, None, ALU.max)))
            ve.wait_ge(z_ready, 1)
            after(link(ve.tensor_scalar(spv[:, 4, :], spv[:, 1, :], 2.0, None, ALU.add)))
            after(link(ve.reciprocal(spv[:, 4, :], spv[:, 4, :])))
            after(link(ve.tensor_tensor(spv[:, 4, :], spv[:, 4, :], spv[:, 1, :], ALU.mult)))
            after(link(ve.tensor_tensor(spv[:, 5, :], spv[:, 4, :], spv[:, 4, :], ALU.mult)))
            after(link(ve.tensor_scalar(spv[:, 6, :], spv[:, 5, :], 1.0 / 17, None, ALU.mult)))
            for n in (15, 13, 11, 9, 7, 5, 3):
                after(link(ve.scalar_tensor_tensor(spv[:, 6, :], spv[:, 6, :], 1.0 / n, spv[:, 5, :],
                                                   ALU.add, ALU.mult)))
            after(link(ve.scalar_tensor_tensor(spv[:, 6, :], spv[:, 6, :], 1.0, spv[:, 4, :],
                                               ALU.add, ALU.mult)))
            after(link(ve.scalar_tensor_tensor(spv[:, 6, :], spv[:, 6, :], 2.0, spv[:, 3, :],
                                               ALU.mult, ALU.add)))
            after(link(ve.tensor_scalar(spv[:, 7, :], spv[:, 6, :], 4.0, None, ALU.mult)))
            ve.wait_ge(conf_ready, 1)
            ve.wait_ge(db_used, 1)

            def filter_taps(taps, src, w, out, out_s, weight, bias, state):
                for t in taps:
                    pin, sin = pr(src, w, t), sa(src, w, t)
                    if t == 0:
                        if bias is None:
                            state[0] = link(ve.tensor_scalar(out, pin, weight(0), None, ALU.mult))
                            state[1] = link(ve.tensor_scalar(out_s, sin, weight(0), None, ALU.mult))
                        else:
                            state[0] = link(ve.tensor_scalar(out, pin, weight(0), bias, ALU.mult, ALU.add))
                            state[1] = link(ve.tensor_scalar(out_s, sin, weight(0), bias, ALU.mult, ALU.add))
                    else:
                        after(state[0])
                        state[0] = link(ve.scalar_tensor_tensor(out, pin, weight(t), out, ALU.mult, ALU.add))
                        after(state[1])
                        state[1] = link(ve.scalar_tensor_tensor(out_s, sin, weight(t), out_s,
                                                                ALU.mult, ALU.add))

            def split(src, hi_ap, lo_ap):
                after(link(ve.tensor_copy(hi_ap, src)))
                return ve.tensor_tensor(lo_ap, src, hi_ap.bitcast(F32), ALU.subtract)

            with ve.Fori(0, KW) as c:
                ch.enter(c, PER_IN)
                ve.wait_ge(tails_taken, c + 1)
                link(ve.tensor_copy(sa(glu_pad, PAD_B, 0, PAD_B), steps(confT[:, c, :])))
                ve.wait_ge(tile_out[1], c * 4 + 2)
                ve.wait_ge(tile_out[0], c * 4 + 2)
                link(ve.tensor_tensor(glu_pad[:, PAD_B:PAD_B + SEQ], b_val[:, 0:SEQ], b_sig[:, 0:SEQ],
                                      ALU.mult))
                ve.tensor_tensor(sa(glu_pad, PAD_B, PAD_B), steps(b_val[:, SEQ:NT]), steps(b_sig[:, SEQ:NT]),
                                 ALU.mult).then_inc(glu_made, 1)
                ve.wait_ge(glu_made, c + 2)
                st_b = [None, None]
                conv_b = (glu_pad, PAD_B, bconv[:, c, 0:SEQ], steps(bconv[:, c, SEQ:NT]),
                          lambda t: vec(c, V_CFW + t), vec(c, V_CFB), st_b)
                filter_taps(range(0, CONF_TAPS_1), *conv_b)

                link(ve.tensor_copy(sa(dch_pad, PAD_D, 0, PAD_D), steps(miscT[:, c, M_SC:M_H])))
                ve.wait_ge(tile_out[0], c * 4 + 3)
                ve.wait_ge(unit_done, c * 8 + 4)
                dh = slot(1)
                link(ve.tensor_tensor(dch_pad[:, PAD_D:PAD_D + HALF], dh[:, 0, :], d_c[:, 0:HALF], ALU.mult))
                link(ve.tensor_tensor(dch_pad[:, PAD_D + HALF:PAD_D + SEQ], dh[:, 1, 0:SEQ - HALF],
                                      d_c[:, HALF:SEQ], ALU.mult))
                ve.tensor_tensor(sa(dch_pad, PAD_D, PAD_D), steps(dh[:, 1, SEQ - HALF:HALF]),
                                 steps(d_c[:, SEQ:NT]), ALU.mult).then_inc(tile_out[1], 1)
                ve.wait_ge(tile_out[1], c * 4 + 3)
                st_d = [None, None]
                filter_taps(range(SC_TAPS), dch_pad, PAD_D, acc[0][:, 0:SEQ], steps(acc[0][:, SEQ:NT]),
                            lambda t: vec(c, V_SCW + t), None, st_d)
                ve.wait_ge(tile_out[0], c * 4 + 4)
                after(st_d[1])
                ve.tensor_tensor(acc[1][:, 0:NT], acc[0][:, 0:NT], d_b[:, :], ALU.mult).then_inc(db_used, 1)
                ve.wait_ge(db_used, c + 2)
                split(acc[1][:, 0:NT], Y_D[:, c, :], Y_D[:, c + KW, :]).then_inc(yd_ready, 1)

                filter_taps(range(CONF_TAPS_1, CONF_TAPS_2), *conv_b)

                link(ve.tensor_copy(sa(cin_pad, PAD_C, 0, PAD_C), steps(poolT[:, c, :])))
                ve.wait_ge(tile_out[1], c * 4 + 4)
                n = SEQ + PAD_C
                ve.wait_ge(yd_ready, c + 1)
                src = (cin_pad[:, 0:n], sa(cin_pad, PAD_C, 0, PAD_C + T))
                after(ch.base + ch.local)
                lost = 0
                for step in range(4):
                    dst_buf = acc[step % 2]
                    dst = (dst_buf[:, 0:n], sa(dst_buf, PAD_C, 0, PAD_C + T))
                    sh = 1 << step
                    lost += sh
                    for part in range(2):
                        if part == 0:
                            o, a, b_ = (dst[0][:, lost:n], src[0][:, lost:n], src[0][:, lost - sh:n - sh])
                        else:
                            m_ = PAD_C + T
                            o, a, b_ = (dst[1][:, :, lost:m_], src[1][:, :, lost:m_],
                                        src[1][:, :, lost - sh:m_ - sh])
                        by = 1.0 if step == 0 else widen[:, c, step - 1:step]
                        v = link(ve.scalar_tensor_tensor(o, b_, by, a, ALU.mult, ALU.add))
                    after(v)
                    src = dst
                win = acc[1]
                m0 = acc[0]
                link(ve.scalar_tensor_tensor(m0[:, 0:SEQ], win[:, PAD_C:PAD_C + SEQ], widen[:, c, 3:4],
                                             cin_pad[:, PAD_C:PAD_C + SEQ], ALU.mult, ALU.subtract))
                v = link(ve.scalar_tensor_tensor(steps(m0[:, SEQ:NT]), sa(win, PAD_C, PAD_C), widen[:, c, 3:4],
                                                 sa(cin_pad, PAD_C, PAD_C), ALU.mult, ALU.subtract))
                after(v)
                after(link(ve.tensor_tensor(m0[:, 0:POOL_BUF], win[:, PAD_C:2 * PAD_C], inv_count[:, c, :],
                                            ALU.mult)))
                ve.tensor_tensor(m0[:, 0:POOL_BUF], m0[:, 0:POOL_BUF], cin_pad[:, PAD_C:2 * PAD_C],
                                 ALU.subtract).then_inc(cin_used, 1)
                ve.wait_ge(cin_used, c + 2)
                after(link(split(m0[:, 0:NT], Y_C[:, c, :], Y_C[:, c + KW, :])))

                link(ve.tensor_copy(sa(ax_pad, PAD_A, 0, PAD_A), steps(miscT[:, c, M_CONV:M_SC])))
                ve.wait_ge(tile_out[0], c * 4 + 5)
                after(ch.base + ch.local)
                st_a = [None, None]
                filter_taps(range(RG_TAPS), ax_pad, PAD_A, xc[:, c, 0:SEQ], steps(xc[:, c, SEQ:NT]),
                            lambda t: vec(c, V_RGW + t), vec(c, V_RGB), st_a)
                after(st_a[1])
                after(link(ve.tensor_copy(Y_A[:, c, :], xc[:, c, :])))
                ve.tensor_tensor(Y_A[:, c + KW, :], xc[:, c, :], Y_A[:, c, :].bitcast(F32), ALU.subtract)\
                  .then_inc(ax_used, 1)
                filter_taps(range(CONF_TAPS_2, CF_TAPS), *conv_b)
                after(st_b[1])
            ch.leave(KW)

            def product(q, i, mm):
                u = i * 4 + (U_MIX + 16 * q + 2 * mm)
                ve.wait_ge(tile_out[0], i * 2 + ((U_MIX + 16 * q) // 2 + mm + 2))
                ve.wait_ge(unit_done, u + 2)
                m = i * 2 + mm
                if q == 0:
                    ve.tensor_tensor(halves(merged[:, m, :]), slot(1), halves(sig[mm][:, :]), ALU.mult)\
                      .then_inc(tile_out[1], 1)
                    return
                ve.tensor_tensor(halves(prod[:, :]), slot(1), halves(sig[mm][:, :]), ALU.mult)\
                  .then_inc(tile_out[1], 1)
                ve.wait_ge(tile_out[1], i * 2 + ((U_MIX + 16 * q) // 2 + mm + 2))
                v = link(ve.tensor_tensor(merged[:, m, :], merged[:, m, :], prod[:, :], ALU.add))
                after(v)
                if q == 3:
                    split(merged[:, m, :], Y_C[:, m, :], Y_A[:, m, :]).then_inc(merged_ready, 1)

            def recurrence(c):
                s_d, s_a, s_b, s_x = S
                after(link(ve.tensor_scalar(s_d[:, :], th[:, c, :], 1.0, None, ALU.add)))
                after(link(ve.reciprocal(s_d[:, :], s_d[:, :])))
                link(ve.tensor_scalar(s_a[:, :], s_d[:, :], 2.0, -1.0, ALU.mult, ALU.add))
                link(ve.tensor_tensor(s_b[:, :], sq_th[:, c, :], s_d[:, :], ALU.mult))
                after(link(ve.scalar_tensor_tensor(s_x[:, :], igate[:, c, :], 2.0, xc[:, c, :],
                                                   ALU.mult, ALU.mult)))
                after(link(ve.tensor_tensor(s_b[:, :], s_b[:, :], s_x[:, :], ALU.mult)))
                a0 = steps(s_a[:, SEQ:NT])[:, :, 0:1].rearrange("p b o -> p (b o)")
                b0 = steps(s_b[:, SEQ:NT])[:, :, 0:1].rearrange("p b o -> p (b o)")
                after(link(ve.tensor_tensor(s_x[:, 0:B], a0, miscT[:, c, M_H:M_H + B], ALU.mult)))
                link(ve.tensor_tensor(b0, b0, s_x[:, 0:B], ALU.add))
                after(link(ve.tensor_scalar(a0, a0, 0.0, None, ALU.mult)))
                after(link(ve.tensor_tensor_scan(s_x[:, :], s_a[:, :], s_b[:, :], 0.0, ALU.mult, ALU.add)))
                link(ve.tensor_copy(h_last[:, c, 0:1], s_x[:, SEQ - 1:SEQ]))
                link(ve.tensor_copy(h_last[:, c, 1:1 + B],
                                    steps(s_x[:, SEQ:NT])[:, :, T - 1:T].rearrange("p b o -> p (b o)")))
                after(link(ve.tensor_tensor(s_b[:, :], s_x[:, :], agate[:, c, :], ALU.mult)))
                split(s_b[:, :], Y_A[:, c, :], Y_A[:, c + KW, :]).then_inc(ya_ready, 1)
                ve.wait_ge(ya_ready, c + 1)

            def statistics(n, mean, var, prod2, sem_out):
                link(ve.tensor_scalar(halves(mean[:, :]), aslot(0), 1.0 / n, None, ALU.mult))
                after(ch.base + ch.local)
                after(link(ve.tensor_tensor(prod2[:, :], mean[:, :], mean[:, :], ALU.mult)))
                after(link(ve.scalar_tensor_tensor(halves(var[:, :]), aslot(1), 1.0 / n, halves(prod2[:, :]),
                                                   ALU.mult, ALU.subtract)))
                ve.tensor_scalar(var[:, :], var[:, :], 0.0, EPS, ALU.max, ALU.add).then_inc(sem_out, 1)

            for q in range(4):
                if q == 0:
                    ve.wait_ge(tails_taken, KW + 1)
                if q == 1:
                    for c in range(KW):
                        ve.wait_ge(yc_ready, c + 1)
                        ve.tensor_tensor(Y_C[:, c + KW, :], pool_t[:, c, :], Y_C[:, c, :].bitcast(F32),
                                         ALU.subtract).then_inc(yc_split, 1)
                    ve.wait_ge(side_done, 3 * KW + 2)
                    statistics(W, b_mean, b_std, b_tmp, bvar_ready)
                if q == 2:
                    ve.wait_ge(bstd_ready, 1)
                    after(link(ve.reciprocal(b_std[:, :], b_std[:, :])))
                ch.flush()
                with ve.Fori(0, KD // 2) as i:
                    ch.enter(i, (0, 2 + PER_REC, 2 + PER_B, 4)[q])
                    if q == 2:
                        t = bconv[:, i, :]
                        after(link(ve.tensor_tensor(t, t, b_mean[:, :], ALU.subtract)))
                        after(link(ve.tensor_tensor(t, t, b_std[:, :], ALU.mult)))
                        ve.tensor_scalar(S[2][:, :], t, vec(i, V_CFG), vec(i, V_CFLB), ALU.mult, ALU.add)\
                          .then_inc(bnorm_ready, 1)
                    product(q, i, 0)
                    if q == 1:
                        ve.wait_ge(sqrt_ready, 1)
                        recurrence(i)
                    product(q, i, 1)
                    if q == 2:
                        ve.wait_ge(bsig_ready, i + 1)
                        after(link(ve.tensor_tensor(bconv[:, i, :], S[2][:, :], S[3][:, :], ALU.mult)))
                        split(bconv[:, i, :], Y_D[:, i, :], Y_D[:, i + KW, :]).then_inc(yb_ready, 1)
                ch.leave(KD // 2)

            def residual(m, u_done, t_val, n0, out):
                ve.wait_ge(unit_done, u_done)
                ve.scalar_tensor_tensor(halves(S[2][:, :]), halves(x_lo[:, m, :].bitcast(F32)), ALPHA,
                                        slot(m % 2), ALU.mult, ALU.add).then_inc(tile_out[m % 2], 1)
                ve.wait_ge(tile_out[m % 2], t_val)
                ve.scalar_tensor_tensor(out, x_hi[:, m, :].bitcast(F32), ALPHA, S[2][:, :],
                                        ALU.mult, ALU.add).then_inc(r_ready, 1)
                ve.wait_ge(r_ready, n0 + m + 1)

            def layer_norm(j):
                ve.wait_ge(stat_done, KD * (j + 1))
                statistics(D, S[2], S[3], S[1], var_ready)
                ve.wait_ge(std_ready, j + 1)
                after(link(ve.reciprocal(S[3][:, :], S[3][:, :])))
                for k in range(KD):
                    after(link(ve.tensor_tensor(merged[:, k, :], merged[:, k, :], S[2][:, :], ALU.subtract)))
                    ve.tensor_tensor(merged[:, k, :], merged[:, k, :], S[3][:, :], ALU.mult)\
                      .then_inc(norm_ready, 1)

            for m in range(KD):
                residual(m, U_OUT + m + 1, (U_OUT + m) // 2 + 2, 0, merged[:, m, :])
            layer_norm(0)
            ve.wait_ge(norm_ready, KD)
            ch.flush()

            with ve.Fori(0, KF // 2) as i:
                for mm in range(2):
                    f = i * 2 + mm
                    ve.wait_ge(tile_out[0], i * 2 + (U_FF // 2 + mm + 2))
                    ve.wait_ge(unit_done, i * 4 + (U_FF + 2 * mm + 2))
                    ve.tensor_tensor(halves(S[2 + mm][:, :]), slot(1), halves(S[mm][:, :]), ALU.mult)\
                      .then_inc(tile_out[1], 1)
                    ve.wait_ge(tile_out[1], i * 2 + (U_FF // 2 + mm + 2))
                    ve.wait_ge(hid_hi_ready, f + 1)
                    ve.tensor_tensor(h_lo[:, f, :], S[2 + mm][:, :], h_hi[:, f, :].bitcast(F32), ALU.subtract)\
                      .then_inc(hid_lo_ready, 1)
                    ve.wait_ge(hid_lo_ready, f + 1)

            def row_statistics(m):
                ve.wait_ge(rows_out, m + 1)
                for j in range(NTILE):
                    link(ve.bn_stats(bn[:, j, m, :], r_tok[:, j, m * P:m * P + P]))
                link(ve.bn_stats(bn[0:B * T, NTILE, m, :], rs_tok[:, m * P:m * P + P]))

            for m in range(KD):
                if m >= 2:
                    ve.wait_ge(rows_turned, m - 1)
                residual(m, U_DOWN + 3 * m + 3, U_DOWN // 2 + m // 2 + 2, KD, S[m % 2][:, :])
                if m >= 1:
                    row_statistics(m - 1)
            row_statistics(KD - 1)
            after(ch.base + ch.local)
            ve.wait_ge(bn_zero, 1)
            for j in range(NTILE):
                ins = ve.bn_aggr(bn_mv[:, j, :], bn[:, j, :, :].rearrange("p k s -> p (k s)"))
                link(ins)
            ve.bn_aggr(bn_mv[0:B * T, NTILE, :], bn[0:B * T, NTILE, :, :].rearrange("p k s -> p (k s)"))\
              .then_inc(bn_var, 1)
            ve.wait_ge(bn_std, 1)
            after(link(ve.reciprocal(bn_rs[:, :, 0:1], bn_rs[:, :, 0:1])))
            ve.scalar_tensor_tensor(bn_rs[:, :, 1:2], bn_mv[:, :, 0:1], -1.0, bn_rs[:, :, 0:1],
                                    ALU.mult, ALU.mult).then_inc(bn_scale, 1)
            ve.wait_ge(row_vecs, 32)
            for n, j in enumerate((0, 1, 2, 4)):
                q = P if j < NTILE else B * T
                t = r_tok[:, j, :] if j < NTILE else rs_tok[:, :]
                ve.wait_ge(row_normed, n + 2)
                after(link(ve.tensor_tensor(t, t, g_row[0:q, :], ALU.mult)))
                ve.tensor_tensor(t, t, b_row[0:q, :], ALU.add).then_inc(rows_ready, 1)


N_SMALL = 21
PER_IN = 98
PER_REC = 14
PER_B = 4

_INS = ["x_prompt", "x_sample", "state_rglru_h", "state_rglru_conv", "state_conformer_conv", "state_pool",
        "state_shortconv", "w_in", "rg_conv_w", "rg_conv_b", "rg_w_a", "rg_b_a", "rg_w_x", "rg_b_x",
        "rg_lambda", "cf_conv_w", "cf_conv_b", "cf_ln_g", "cf_ln_b", "pool_w", "pool_scale", "sc_conv_w",
        "w_branch", "w_out", "ln1_g", "ln1_b", "w_ff_gate", "w_ff_up", "w_ff_down", "ln2_g", "ln2_b"]
_OUTS = [("y_prompt", (1, SEQ, D)), ("y_sample", (B, T, D)),
         ("prompt_h", (1, 1, W)), ("prompt_rgc", (1, 1, 3, W)), ("prompt_cf", (1, 1, 30, W)),
         ("prompt_pool", (1, 1, 15, W)), ("prompt_sc", (1, 1, 2, W)),
         ("sample_h", (1, B, W)), ("sample_rgc", (1, B, 3, W)), ("sample_cf", (1, B, 30, W)),
         ("sample_pool", (1, B, 15, W)), ("sample_sc", (1, B, 2, W))]


def kernel(**inputs):
    import numpy as _np
    import concourse.bacc as _bacc
    from concourse.bass_utils import run_bass_kernel_spmd as _run

    nc = _bacc.Bacc("TRN2", target_bir_lowering=False, num_devices=1, dynamic_dma_scratch_size=1024)
    arrays, ins, outs = {}, {}, {}
    for name in _INS:
        a = _np.ascontiguousarray(inputs[name])
        arrays[f"in_{name}"] = a
        ins[name] = nc.dram_tensor(f"in_{name}", a.shape, mybir.dt.from_np(a.dtype), kind="ExternalInput").ap()
    for name, shape in _OUTS:
        outs[name] = nc.dram_tensor(f"out_{name}", shape, F32, kind="ExternalOutput").ap()
    build(nc, ins, outs)
    r = _run(nc, [arrays], core_ids=[0])
    return tuple(r.results[0][f"out_{name}"] for name, _ in _OUTS)
```

```python
from contextlib import ExitStack

import concourse.bass as bass
from concourse import mybir

F32 = mybir.dt.float32
F32R = mybir.dt.float32r
ALU = mybir.AluOpType
ACT = mybir.ActivationFunctionType
ds = bass.ds

P = 128
D = 1024
W = 512
SEQ = 512
B, T = 8, 4
NT = SEQ + B * T
HALF = NT // 2
FF = 2816
KD, KW, KF = D // P, W // P, FF // P
RING = 4
RG_TAPS, CF_TAPS, SC_TAPS, POOL_BUF = 4, 31, 3, 15
ALPHA = 2.0 ** 0.25
EPS = 1e-5

A_X, A_GATE, B_VAL, B_GATE, C_IN, D_B, D_C, D_H = range(8)
IN_ORDER = (B_VAL, B_GATE, D_C, D_H, D_B, C_IN, A_X, A_GATE)
GATE_COL = 8 * W
BRANCH_ORDER = (3, 2, 0, 1)

U_MIX = KW * 8
U_OUT = U_MIX + 4 * 2 * KD
U_FF = U_OUT + KD
U_DOWN = U_FF + 2 * KF
DOWN_SPLIT = (8, 8, KF - 16)
U_END = U_DOWN + 3 * KD
T_FF = U_OUT // 2
T_DOWN = T_FF + KF

M_CONV, M_SC, M_H = 0, B * (RG_TAPS - 1), B * (RG_TAPS - 1) + B * (SC_TAPS - 1)
V_RGW = M_H + B
V_RGB, V_BA, V_BX, V_LAM = V_RGW + 4, V_RGW + 5, V_RGW + 6, V_RGW + 7
V_CFW = V_RGW + 8
V_CFB = V_CFW + CF_TAPS
V_CFG, V_CFLB, V_PSC = V_CFB + 1, V_CFB + 2, V_CFB + 3
V_SCW = V_CFB + 4
M_ROWS = V_SCW + SC_TAPS
CONF_TAPS_1, CONF_TAPS_2 = 15, 28


class Chain:

    def __init__(self, eng, sem):
        self.eng, self.sem, self.base, self.local = eng, sem, 0, 0
        self.start = 0

    def link(self, ins):
        ins.then_inc(self.sem, 1)
        self.local += 1
        return self.base + self.local

    def after(self, value):
        self.eng.wait_ge(self.sem, value)

    def enter(self, i, per):
        self.start += self.local if isinstance(self.base, int) else 0
        self.base, self.local, self.per = i * per + self.start, 0, per

    def leave(self, count):
        assert self.local == self.per, (self.local, self.per)
        self.start += self.per * count
        self.base, self.local = self.start, 0

    def flush(self):
        self.start += self.local
        self.base, self.local = self.start, 0


def build(nc, i_, o_):
    with ExitStack() as ctx:
        def sem(name):
            return ctx.enter_context(nc.semaphore(name))

        CH = NT * 4
        base = (nc.sbuf_base + 63) // 64 * 64
        top = [base]

        def take(nbytes):
            at = top[0]
            top[0] += (nbytes + 31) // 32 * 32
            assert top[0] <= nc.sbuf_usable_end, (name_of[0], top[0], nc.sbuf_usable_end)
            return at

        name_of = [""]

        def at(name, shape, dt, offset):
            name_of[0] = name
            return nc.alloc_sbuf_tensor_at(name, shape, dt, offset=offset)

        def new(name, shape, dt):
            n = 4
            for s in shape[1:]:
                n *= s
            name_of[0] = name
            return at(name, shape, dt, take(n))

        x_hi = new("x_hi", [P, KD, NT], F32R)
        x_lo = new("x_lo", [P, KD, NT], F32R)
        raw = [new(f"raw{s}", [P, 8, P], F32) for s in range(RING)]
        w_hi = [new(f"w_hi{s}", [P, 8, P], F32R) for s in range(RING)]
        w_lo = [new(f"w_lo{s}", [P, 8, P], F32R) for s in range(RING)]
        at_f = take(KD * CH)
        at_s = take(4 * CH)
        ident = new("ident", [P, P], F32)
        ones = new("ones", [P, P], F32)
        miscT = new("miscT", [P, KW, M_ROWS], F32)
        at_v = top[0]
        confT = new("confT", [P, KW, B * 30], F32)
        poolT = new("poolT", [P, KW, B * POOL_BUF], F32)
        lnT = new("lnT", [P, 32], F32)
        inv_count = new("inv_count", [P, KW, POOL_BUF], F32)
        spv = new("spv", [P, 8, KW], F32)
        bn = new("bn", [P, SEQ // P + 1, KD, 6], F32)
        bn_mv = new("bn_mv", [P, SEQ // P + 1, 2], F32)
        bn_rs = new("bn_rs", [P, SEQ // P + 1, 2], F32)
        h_last = new("h_last", [P, KW, 1 + B], F32)
        at_r = top[0]

        merged = at("merged", [P, KD, NT], F32, at_f)
        S = [at(f"scr{j}", [P, NT], F32, at_s + j * CH) for j in range(4)]

        y = [new(f"y{j}", [P, 2 * KW, NT], F32R) for j in range(3)]
        xc = new("xc", [P, KW, NT], F32)
        agate = new("agate", [P, KW, NT], F32)
        bconv = new("bconv", [P, KW, NT], F32)
        sm_hi = new("sm_hi", [P, 12, P], F32R)
        sm_lo = new("sm_lo", [P, 12, P], F32R)
        at_sig = take(2 * CH)
        at_u = take(5 * CH)
        at_st = at_u + 4 * 400
        st_s = at("st_s", [120, 3 * P], F32, at_st)
        st_p = at("st_p", [30, 4 * P], F32, at_st + 4 * 3 * P)
        st_ax = at("st_ax", [24, P], F32, at_st + 4 * 7 * P)
        st_sc = at("st_sc", [16, P], F32, at_st + 4 * 8 * P)
        sig = [at(f"sig{j}", [P, NT], F32, at_sig + j * CH) for j in range(2)]
        sq_th = at("sq_th", [P, KW, NT], F32, at_u)
        pool_t = at("pool_t", [P, KW, NT], F32, at_u)
        bsq = at("bsq", [P, KW, NT], F32, at_s)
        at_sm = at_r + 6 * KW * CH + 3 * KW * CH
        b_mean, b_std, b_tmp = (at(n, [P, NT], F32, at_sm + j * CH)
                                for j, n in enumerate(("b_mean", "b_std", "b_tmp")))
        packed = at("packed", [P, 400], F32, at_u)
        prod = at("prod", [P, NT], F32, at_sm + 3 * CH + 128)
        Y_D, Y_C, Y_A = y
        at_y = at_r
        th = at("th", [P, KW, NT], F32, at_y + 4 * KW * CH)
        igate = at("igate", [P, KW, NT], F32, at_y + 5 * KW * CH)
        h_rows = at("h_rows", [1 + B, W], F32, at_u + 4 * CH)
        wx_hi = [at(f"wx_hi{s}", [P, 8, P], F32R, at_r + 6 * KW * CH + 4096 * s) for s in range(RING)]
        wx_lo = [at(f"wx_lo{s}", [P, 8, P], F32R, at_r + 6 * KW * CH + 4096 * (RING + s)) for s in range(RING)]
        assert 2 * RING * 4096 <= 3 * KW * CH + 3 * CH + 128
        r_tmp, rsq0, rsq1, acc_r, acc_q, mean_h, std_h, tmp_h = (
            at(n, [P, HALF], F32, at_s + j * HALF * 4) for j, n in enumerate(
                ("r_tmp", "rsq0", "rsq1", "acc_r", "acc_q", "mean_h", "std_h", "tmp_h")))
        rsq = (rsq0, rsq1)
        h_hi = at("h_hi", [P, KF, NT], F32R, at_r)
        h_lo = at("h_lo", [P, KF, NT], F32R, at_r + KF * CH)
        assert at_r + 2 * KF * CH <= nc.sbuf_usable_end
        NTILE = SEQ // P
        r_tok = at("r_tok", [P, NTILE, D], F32, at_f)
        at_t = at_r + 2 * KF * CH
        rs_tok = at("rs_tok", [B * T, D], F32, at_t)
        g_row = at("g_row", [P, D], F32, at_t + 4 * D)
        b_row = at("b_row", [P, D], F32, at_v)
        assert 4 * D <= 4 * KW * B * (30 + POOL_BUF) and at_t + 8 * D <= nc.sbuf_usable_end
        x_tok = at("x_tok", [P, SEQ // P, D], F32, at_y)
        at_i = at_y + SEQ // P * D * 4
        xs_tok = at("xs_tok", [B * T, D], F32, at_i)
        misc_tok = at("misc_tok", [M_ROWS, W], F32, at_i + 4 * D)
        conf_tok = at("conf_tok", [120, 2, W], F32, at_i + 4 * D + 4 * W)
        pool_tok = at("pool_tok", [120, W], F32, at_i + 4 * D + 12 * W)
        ln_tok = at("ln_tok", [32, P], F32, at_i + 4 * D + 16 * W)
        sm_raw = at("sm_raw", [P, 12, P], F32, at_i + 4 * D + 16 * W + 4 * P)
        assert at_i + 4 * D + 16 * W + 4 * P + 48 * P <= at_y + 6 * KW * CH
        PAD_A, PAD_B, PAD_C, PAD_D = RG_TAPS - 1, CF_TAPS - 1, POOL_BUF, SC_TAPS - 1
        t2 = [at_f]

        def pad(name, n, dt=F32):
            off = t2[0]
            t2[0] += (4 * n + 31) // 32 * 32
            assert t2[0] <= at_s + 4 * CH, name
            return at(name, [P, n], dt, off)

        def padded(w):
            return w + SEQ + B * (w + T)

        ax_pad = pad("ax_pad", padded(PAD_A))
        glu_pad = pad("glu_pad", padded(PAD_B))
        cin_pad = pad("cin_pad", padded(PAD_C))
        dch_pad = pad("dch_pad", padded(PAD_D))
        b_val, b_sig, d_b, d_c = (pad(n, NT) for n in ("b_val", "b_sig", "d_b", "d_c"))
        acc = pad("acc", NT)
        win = [pad("win0", padded(PAD_C)),
               at("win1", [P, padded(PAD_C)], F32, at_st + 4 * 9 * P)]
        assert at_st + 4 * 9 * P + 4 * padded(PAD_C) <= at_u + 5 * CH

        main = ctx.enter_context(nc.psum_tensor("main", [P, 4, 512], F32))
        aux = ctx.enter_context(nc.psum_tensor("aux", [P, 4, 512], F32))

        def slot(s):
            return main[:, 2 * s:2 * s + 2, 0:HALF]

        def aslot(s):
            return aux[:, 2 * s:2 * s + 2, 0:HALF]

        def halves(ap):
            return ap.rearrange("p (h n) -> p h n", h=2)

        def steps(ap):
            return ap.rearrange("p (b t) -> p b t", b=B)

        def pr(buf, w, first, n=SEQ):
            return buf[:, first:first + n]

        def sa(buf, w, first, n=T, b0=0, b1=B):
            return steps(buf[:, w + SEQ:w + SEQ + B * (w + T)])[:, b0:b1, first:first + n]

        x_landed = [sem(f"x_landed{j}") for j in range(5)]
        small_landed = sem("small_landed")
        sm_zeroed = sem("sm_zeroed")
        sm_landed = sem("sm_landed")
        sm_hi_ready, sm_lo_ready = sem("sm_hi_ready"), sem("sm_lo_ready")
        consts = sem("consts")
        ident_ready = sem("ident_ready")
        turned = sem("turned")
        x_hi_ready, x_lo_ready = sem("x_hi_ready"), sem("x_lo_ready")
        misc_ready, conf_ready = sem("misc_ready"), sem("conf_ready")
        lam_ready, z_ready = sem("lam_ready"), sem("z_ready")
        raw_landed = [sem(f"raw_landed{s}") for s in range(RING)]
        w_hi_ready, w_lo_ready = sem("w_hi_ready"), sem("w_lo_ready")
        unit_done = sem("unit_done")
        tile_out = [sem("tile_out0"), sem("tile_out1")]
        glu_made, db_used, cin_used, ax_used = map(
            sem, ("glu_made", "db_used", "cin_used", "ax_used"))
        tails_taken, tails_out, tails_stored = sem("tails_taken"), sem("tails_out"), sem("tails_stored")
        rows_packed = sem("rows_packed")
        dve = sem("dve_steps")
        yd_ready = sem("yd_ready")
        side_done, side_out = sem("side_done"), sem("side_out")
        yc_ready, sqrt_ready = sem("yc_ready"), sem("sqrt_ready")
        yc_split, yc_made = sem("yc_split"), sem("yc_made")
        pool_own = sem("pool_steps")
        bsq_summed, th_ready = sem("bsq_summed"), sem("th_ready")
        ya_ready, yb_ready = sem("ya_ready"), sem("yb_ready")
        h_turned, h_copied = sem("h_turned"), sem("h_copied")
        bsq_ready, bvar_ready, bstd_ready, bnorm_ready, bsig_ready = map(
            sem, ("bsq_ready", "bvar_ready", "bstd_ready", "bnorm_ready", "bsig_ready"))
        merged_ready = sem("merged_ready")
        r_ready, rsq_ready, stat_done = sem("r_ready"), sem("rsq_ready"), sem("stat_done")
        half_done, half_out = sem("half_done"), sem("half_out")
        sq_summed, acc_ready, gelu_ready = sem("sq_summed"), sem("acc_ready"), sem("gelu_ready")
        var_ready, std_ready = sem("var_ready"), sem("std_ready")
        norm_ready, affine_ready, x1_hi_ready, x1_lo_ready = map(
            sem, ("norm_ready", "affine_ready", "x1_hi_ready", "x1_lo_ready"))
        hid_hi_ready, hid_lo_ready = map(sem, ("hid_hi_ready", "hid_lo_ready"))
        rows_turned, rows_out = sem("rows_turned"), sem("rows_out")
        row_vecs, bn_zero = sem("row_vecs"), sem("bn_zero")
        bn_var, bn_std, bn_scale = sem("bn_var"), sem("bn_std"), sem("bn_scale")
        row_normed, rows_ready, pool_rows = sem("row_normed"), sem("rows_ready"), sem("pool_rows")
        last_half, last_out = sem("last_half"), sem("last_out")
        stored = sem("stored")

        w_in = i_["w_in"].rearrange("a (k p) n -> p (a k) n", p=P)
        w_br = i_["w_branch"].rearrange("a b (k p) n -> p (a b k) n", p=P)
        w_out = i_["w_out"].rearrange("a (k p) n -> p (a k) n", p=P)
        w_g = i_["w_ff_gate"].rearrange("a (k p) n -> p (a k) n", p=P)
        w_u = i_["w_ff_up"].rearrange("a (k p) n -> p (a k) n", p=P)
        w_d = i_["w_ff_down"].rearrange("a (k p) n -> p (a k) n", p=P)
        x_p = i_["x_prompt"].rearrange("a (j p) d -> p (a j) d", p=P)
        x_s = i_["x_sample"].rearrange("b t d -> (b t) d")
        o_x = o_["y_prompt"].rearrange("a (j p) d -> p (a j) d", p=P)
        o_s = o_["y_sample"].rearrange("b t d -> (b t) d")

        def rows2(ap):
            return ap.rearrange("a b w -> (a b) w")

        def rows3(ap):
            return ap.rearrange("a b r w -> (a b r) w")

        block = ctx.enter_context(nc.Block())

        @block.sync
        def _(sp):
            nc.disable_value_cache = True

            def unit(u, s, src):
                if not (isinstance(u, int) and u < RING):
                    sp.wait_ge(w_lo_ready, u - (RING - 1))
                sp.dma_start(raw[s][:, 0:src.shape[1], :], src).then_inc(raw_landed[s], 16)

            def in_col(idx, c):
                return w_in[:, :, ds(IN_ORDER[idx] * W + c * P, P)]

            sp.dma_start(xs_tok[:, :], x_s).then_inc(x_landed[4], 16)
            unit(0, 0, in_col(0, 0))
            for j in range(SEQ // P):
                sp.dma_start(x_tok[:, j, :], x_p[:, j, :]).then_inc(x_landed[j], 16)
            for idx in range(1, RING - 1):
                unit(idx, idx, in_col(idx, 0))
            small = ((misc_tok[M_CONV:M_SC, :], rows3(i_["state_rglru_conv"])),
                     (misc_tok[M_SC:M_H, :], rows3(i_["state_shortconv"])),
                     (misc_tok[M_H:V_RGW, :], rows2(i_["state_rglru_h"])),
                     (misc_tok[V_RGW:V_RGB, :], rows2(i_["rg_conv_w"])),
                     (misc_tok[V_RGB:V_RGB + 1, :], i_["rg_conv_b"]),
                     (misc_tok[V_BA:V_BA + 1, :], i_["rg_b_a"]),
                     (misc_tok[V_BX:V_BX + 1, :], i_["rg_b_x"]),
                     (misc_tok[V_LAM:V_LAM + 1, :], i_["rg_lambda"]),
                     (misc_tok[V_CFW:V_CFB, :], rows2(i_["cf_conv_w"])),
                     (misc_tok[V_CFB:V_CFB + 1, :], i_["cf_conv_b"]),
                     (misc_tok[V_CFG:V_CFG + 1, :], i_["cf_ln_g"]),
                     (misc_tok[V_CFLB:V_CFLB + 1, :], i_["cf_ln_b"]),
                     (misc_tok[V_PSC:V_PSC + 1, :], i_["pool_scale"]),
                     (misc_tok[V_SCW:M_ROWS, :], rows2(i_["sc_conv_w"])),
                     (conf_tok[:, 0, :], rows3(i_["state_conformer_conv"])[0:120, :]),
                     (conf_tok[:, 1, :], rows3(i_["state_conformer_conv"])[120:240, :]),
                     (pool_tok[:, :], rows3(i_["state_pool"]))) + tuple(
                         (ln_tok[8 * j:8 * j + 8, :], i_[n].rearrange("a (k p) -> (a k) p", p=P))
                         for j, n in enumerate(("ln1_g", "ln1_b", "ln2_g", "ln2_b")))
            assert len(small) == N_SMALL
            for dst, src in small:
                sp.dma_start(dst, src).then_inc(small_landed, 16)
            unit(RING - 1, RING - 1, in_col(RING - 1, 0))
            sp.wait_ge(sm_zeroed, 1)
            for k0, name in ((0, "rg_w_a"), (KW, "rg_w_x")):
                w = i_[name].rearrange("a (c two) i j -> (a two) i c j", two=2)
                for two in range(2):
                    q = slice(64 * two, 64 * two + 64)
                    sp.dma_start(sm_raw[q, k0:k0 + KW, q], w[two]).then_inc(sm_landed, 16)
            sp.dma_start(sm_raw[:, 2 * KW:3 * KW, :],
                         i_["pool_w"].rearrange("a g i j -> i (a g) j")).then_inc(sm_landed, 16)
            with sp.Fori(1, KW - 1 + 1) as c_1:
                c = c_1 - 1
                for idx in range(RING, 8):
                    unit(c * 8 + idx, idx % RING, in_col(idx, c))
                for idx in range(RING):
                    unit(c * 8 + 8 + idx, idx % RING, in_col(idx, c + 1))
            for idx in range(RING, 8):
                unit(8 * (KW - 1) + idx, idx % RING, in_col(idx, KW - 1))
            for q, n in enumerate(BRANCH_ORDER):
                with sp.Fori(1, KD // 2 + 1) as i_1:
                    i = i_1 - 1
                    for mm in range(2):
                        u = i * 4 + (U_MIX + 16 * q + 2 * mm)
                        unit(u, 2 * mm, w_in[:, :, ds(i * (2 * P) + (GATE_COL + D * n + P * mm), P)])
                        unit(u + 1, 2 * mm + 1, w_br[:, n * KW:(n + 1) * KW, ds(i * (2 * P) + P * mm, P)])
            sp.wait_ge(h_copied, 1)
            sp.dma_start(rows2(o_["prompt_h"]), h_rows[0:1, :]).then_inc(stored, 16)
            sp.dma_start(rows2(o_["sample_h"]), h_rows[1:1 + B, :]).then_inc(stored, 16)
            with sp.Fori(1, KD // RING + 1) as i_1:
                i = i_1 - 1
                for m in range(RING):
                    unit(i * RING + (U_OUT + m), m, w_out[:, :, ds(i * (RING * P) + m * P, P)])
            with sp.Fori(1, KF // 2 + 1) as i_1:
                i = i_1 - 1
                for mm in range(2):
                    u = i * 4 + (U_FF + 2 * mm)
                    unit(u, 2 * mm, w_g[:, :, ds(i * (2 * P) + P * mm, P)])
                    unit(u + 1, 2 * mm + 1, w_u[:, :, ds(i * (2 * P) + P * mm, P)])
            sp.wait_ge(stored, 2 * 16)
            for dst, name in ((g_row, "ln2_g"), (b_row, "ln2_b")):
                sp.dma_start(dst[:, :], i_[name].to_broadcast([P, D])).then_inc(row_vecs, 16)
            with sp.Fori(1, KD // 4 + 1) as i_1:
                i = i_1 - 1
                for m in range(4):
                    k = 0
                    for part, n in enumerate(DOWN_SPLIT):
                        j = 3 * m + part
                        unit(i * 12 + (U_DOWN + j), j % RING, w_d[:, k:k + n, ds(i * (4 * P) + m * P, P)])
                        k += n
            for n, (rdy, cnt, dst, src) in enumerate((
                    (rows_ready, 1, o_x[:, 0, :], r_tok[:, 0, :]), (pool_rows, 2, o_x[:, 1, :], r_tok[:, 1, :]),
                    (rows_ready, 2, o_x[:, 2, :], r_tok[:, 2, :]),
                    (pool_rows, 4, o_x[:, 3, D // 2:D], r_tok[:, 3, D // 2:D]),
                    (rows_ready, 3, o_s, rs_tok[:, :]),
                    (rows_ready, 4, o_x[:, 3, 0:D // 2], r_tok[:, 3, 0:D // 2]))):
                sp.wait_ge(rdy, cnt)
                sp.dma_start(dst, src).then_inc(stored, 16)
            sp.wait_ge(stored, 16 * 8)
            sp.wait_ge(tails_stored, 1 + 9 * 16 * KW)
            nc.disable_value_cache = False

        @block.gpsimd
        def _(pool):
            pool.memset(ident[:, :], 0.0).then_inc(consts, 1)
            pool.wait_ge(consts, 1)
            pool.affine_select(out=ident[:, :], in_=ident[:, :], compare_op=ALU.not_equal, fill=1.0,
                               base=0, pattern=[[-1, P]], channel_multiplier=1).then_inc(ident_ready, 1)
            pool.memset(sm_raw[:, :, :], 0.0).then_inc(sm_zeroed, 1)
            pool.memset(ones[:, :], 1.0).then_inc(consts, 1)
            pool.memset(glu_pad[:, 0:PAD_B], 0.0).then_inc(glu_made, 1)
            pool.memset(dch_pad[:, 0:PAD_D], 0.0)
            pool.memset(cin_pad[:, 0:PAD_C], 0.0).then_inc(cin_used, 1)
            pool.memset(ax_pad[:, 0:PAD_A], 0.0).then_inc(ax_used, 1)
            pool.memset(st_s[:, :], 0.0).then_inc(tails_stored, 1)
            pool.memset(bn_mv[:, :, :], 1.0).then_inc(bn_zero, 1)
            for c in range(KW):
                window = 2 << c
                for t in range(POOL_BUF):
                    pool.memset(inv_count[:, c, t:t + 1], 1.0 / min(window, t + 1))
            pool.memset(d_b[:, 0:1], 0.0).then_inc(db_used, 1)

            def lo(u, s, n):
                pool.wait_ge(w_hi_ready, u + 1)
                pool.tensor_tensor(w_lo[s][:, 0:n, :], raw[s][:, 0:n, :], w_hi[s][:, 0:n, :].bitcast(F32),
                                   ALU.subtract).then_inc(w_lo_ready, 1)

            for u in range(RING):
                lo(u, u, 8)
            pool.wait_ge(sm_hi_ready, 1)
            pool.tensor_tensor(sm_lo[:, :, :], sm_raw[:, :, :], sm_hi[:, :, :].bitcast(F32),
                               ALU.subtract).then_inc(sm_lo_ready, 1)
            own = Chain(pool, pool_own)
            link, after = own.link, own.after
            n = SEQ + PAD_C

            def parts(buf):
                return buf[:, 0:n], sa(buf, PAD_C, 0, PAD_C + T)

            def window_step(c, step):
                if step == 0:
                    pool.wait_ge(tails_taken, c + 1)
                    after(link(pool.tensor_copy(sa(cin_pad, PAD_C, 0, PAD_C), steps(poolT[:, c, :]))))
                    pool.wait_ge(tile_out[1], c * 4 + 4)
                sh, lost = 1 << step, (2 << step) - 1
                src = cin_pad if step == 0 else win[(step - 1) % 2]
                (d0, d1), (s0, s1) = parts(win[step % 2]), parts(src)
                link(pool.tensor_tensor(d0[:, lost:n], s0[:, lost:n], s0[:, lost - sh:n - sh], ALU.add))
                m_ = PAD_C + T
                after(link(pool.tensor_tensor(d1[:, :, lost:m_], s1[:, :, lost:m_], s1[:, :, lost - sh:m_ - sh],
                                              ALU.add)))

            def window_mean(c):
                w, m = win[c % 2], win[(c + 1) % 2]
                by = 1.0 / (2 << c)
                link(pool.tensor_scalar(m[:, POOL_BUF:SEQ], w[:, PAD_C + POOL_BUF:PAD_C + SEQ], by, None,
                                        ALU.mult))
                link(pool.tensor_scalar(steps(m[:, SEQ:NT]), sa(w, PAD_C, PAD_C), by, None, ALU.mult))
                after(link(pool.tensor_tensor(m[:, 0:POOL_BUF], w[:, PAD_C:2 * PAD_C], inv_count[:, c, :],
                                              ALU.mult)))
                link(pool.tensor_tensor(m[:, 0:SEQ], m[:, 0:SEQ], cin_pad[:, PAD_C:PAD_C + SEQ], ALU.subtract))
                pool.tensor_tensor(steps(m[:, SEQ:NT]), steps(m[:, SEQ:NT]), sa(cin_pad, PAD_C, PAD_C),
                                   ALU.subtract).then_inc(cin_used, 1)
                pool.wait_ge(cin_used, c + 2)
                after(link(pool.tensor_copy(Y_C[:, c, :], m[:, 0:NT])))
                pool.tensor_tensor(Y_C[:, c + KW, :], m[:, 0:NT], Y_C[:, c, :].bitcast(F32), ALU.subtract)\
                    .then_inc(yc_made, 1)
                pool.wait_ge(yc_made, c + 1)

            for c in range(KW):
                for j in range(8):
                    u = RING + 8 * c + j
                    lo(u, u % RING, 8 if u < U_MIX else (8, KW)[u % 2])
                    if j == 5:
                        window_step(c, 0)
                        if c >= 1:
                            window_step(c, 1)
                    if j == 6:
                        for step in range(2, c + 1):
                            window_step(c, step)
                    if j == 7:
                        window_mean(c)
            with pool.Fori(1, 16 // RING) as i:
                for u in range(RING):
                    lo(i * RING + (U_MIX + u), u, (8, KW)[u % 2])
            pool.wait_ge(bsq_ready, 1)
            after(link(pool.tensor_tensor(bsq[:, 0, :], bsq[:, 0, :], bsq[:, 1, :], ALU.add)))
            link(pool.tensor_tensor(bsq[:, 0, :], bsq[:, 0, :], bsq[:, 2, :], ALU.add))
            after(link(pool.tensor_tensor(bsq[:, 1, :], bconv[:, 0, :], bconv[:, 1, :], ALU.add)))
            link(pool.tensor_tensor(bsq[:, 0, :], bsq[:, 0, :], bsq[:, 3, :], ALU.add))
            after(link(pool.tensor_tensor(bsq[:, 1, :], bsq[:, 1, :], bconv[:, 2, :], ALU.add)))
            pool.tensor_tensor(bsq[:, 1, :], bsq[:, 1, :], bconv[:, 3, :], ALU.add).then_inc(bsq_summed, 1)
            with pool.Fori(16 // RING, (U_OUT - U_MIX) // RING) as i:
                for u in range(RING):
                    lo(i * RING + (U_MIX + u), u, (8, KW)[u % 2])
            def lo_to(u, dst, src_hi, s):
                pool.wait_ge(w_hi_ready, u + 1)
                pool.tensor_tensor(dst[:, :, :], raw[s][:, :, :], src_hi[:, :, :].bitcast(F32),
                                   ALU.subtract).then_inc(w_lo_ready, 1)

            def add_square(h, m):
                pool.wait_ge(rsq_ready, h * KD + m + 1)
                if m == 1:
                    if h == 1:
                        pool.wait_ge(stat_done, 1)
                    pool.tensor_tensor(acc_q[:, :], rsq0[:, :], rsq1[:, :], ALU.add).then_inc(sq_summed, 1)
                else:
                    pool.tensor_tensor(acc_q[:, :], acc_q[:, :], rsq[m % 2][:, :], ALU.add)\
                        .then_inc(sq_summed, 1)
                pool.wait_ge(sq_summed, h * (KD - 2) + m)

            def x1_lo(h, k):
                cols = slice(h * HALF, (h + 1) * HALF)
                pool.wait_ge(x1_hi_ready, h * KD + k + 1)
                pool.tensor_tensor(x_lo[:, k, cols], merged[:, k, cols], x_hi[:, k, cols].bitcast(F32),
                                   ALU.subtract).then_inc(x1_lo_ready, 1)

            for u in range(RING):
                lo(U_OUT + u, u, 8)
            for m in range(KD - 1):
                if m < RING:
                    lo_to(U_OUT + RING + m, wx_lo[m], wx_hi[m], m)
                if m >= 1:
                    add_square(0, m)
            for m in range(KD - 1):
                if m >= 1:
                    add_square(1, m)
                if 2 <= m < 6:
                    x1_lo(0, 2 * m - 4)
                    x1_lo(0, 2 * m - 3)
                if m < RING - 2:
                    lo(U_FF + m, m, 8)
            for m in range(RING - 2, RING):
                lo(U_FF + m, m, 8)
            for k in range(KD):
                x1_lo(1, k)
            with pool.Fori(1, 2 * KF // RING) as i:
                for u in range(RING):
                    lo(i * RING + (U_FF + u), u, 8)
            with pool.Fori(0, KD // 4) as i:
                for j in range(12):
                    lo(i * 12 + (U_DOWN + j), j % RING, DOWN_SPLIT[j % 3])
            pool.wait_ge(row_vecs, 32)
            for n, (j, cols) in enumerate(((1, slice(0, D)), (3, slice(D // 2, D)))):
                t = r_tok[:, j, cols]
                pool.wait_ge(row_normed, n + 1)
                pool.tensor_tensor(t, t, g_row[:, cols], ALU.mult).then_inc(pool_rows, 1)
                pool.wait_ge(pool_rows, 2 * n + 1)
                pool.tensor_tensor(t, t, b_row[:, cols], ALU.add).then_inc(pool_rows, 1)

        @block.scalar
        def _(act):

            def hi(u, s):
                act.wait_ge(raw_landed[s], (u // RING) * 16 + 16 if isinstance(u, int) else u_quot(u, s))
                act.activation(w_hi[s][:, :, :], raw[s][:, :, :], ACT.Copy).then_inc(w_hi_ready, 1)

            def u_quot(u, s):
                return (u - s) * (16 // RING) + 16

            act.wait_ge(turned, 1)
            act.activation(x_hi[:, :, SEQ:NT], aux[:, 3, 0:256].rearrange("p (k n) -> p k n", k=KD),
                           ACT.Copy).then_inc(x_hi_ready, 1)
            hi(0, 0)
            for k in range(KD):
                act.wait_ge(turned, k + 2)
                bank = (main, aux)[k // 4]
                act.activation(x_hi[:, k, 0:SEQ], bank[:, k % 4, :], ACT.Copy).then_inc(x_hi_ready, 1)
            hi(1, 1)
            for g in range(2):
                act.wait_ge(turned, KD + 3 + g)
                act.activation(confT[:, 2 * g:2 * g + 2, :],
                               aux[:, 1 + g, 0:480].rearrange("p (c n) -> p c n", c=2), ACT.Copy)\
                   .then_inc(conf_ready if g == 0 else tile_out[1], 1)
            act.wait_ge(turned, KD + 5)
            act.activation(poolT[:, :, :], aux[:, 3, 0:480].rearrange("p (c n) -> p c n", c=KW), ACT.Copy)\
               .then_inc(tails_out, 1)
            for u in range(2, RING):
                hi(u, u)
            act.wait_ge(lam_ready, 1)
            act.activation(spv[:, 1, :], spv[:, 0, :], ACT.Exp).then_inc(z_ready, 1)
            act.wait_ge(sm_landed, 5 * 16)
            act.activation(sm_hi[:, :, :], sm_raw[:, :, :], ACT.Copy).then_inc(sm_hi_ready, 1)

            def in_tile(idx, c):
                kind = IN_ORDER[idx]
                u = c * 8 + idx
                act.wait_ge(unit_done, u + 1)
                ps = slot(idx % 2)
                out_sem = tile_out[idx % 2]
                if kind == B_VAL:
                    act.wait_ge(glu_made, c + 1)
                    act.activation(halves(b_val[:, :]), ps, ACT.Copy).then_inc(out_sem, 1)
                elif kind == B_GATE:
                    act.activation(halves(b_sig[:, :]), ps, ACT.Sigmoid).then_inc(out_sem, 1)
                elif kind == D_C:
                    act.activation(halves(d_c[:, :]), ps, ACT.Copy).then_inc(out_sem, 1)
                elif kind == D_B:
                    act.wait_ge(db_used, c + 1)
                    act.activation(halves(d_b[:, :]), ps, ACT.Copy).then_inc(out_sem, 1)
                elif kind in (C_IN, A_X):
                    buf, w, used = ((cin_pad, PAD_C, cin_used) if kind == C_IN
                                    else (ax_pad, PAD_A, ax_used))
                    act.wait_ge(used, c + 1)
                    act.wait_ge(tails_taken, c + 1)
                    a, b = ps[:, 0, :], ps[:, 1, :]
                    act.activation(buf[:, w:w + HALF], a, ACT.Copy)
                    act.activation(buf[:, w + HALF:w + SEQ], b[:, 0:SEQ - HALF], ACT.Copy)
                    act.activation(sa(buf, w, w), steps(b[:, SEQ - HALF:HALF]), ACT.Copy)\
                       .then_inc(out_sem, 1)
                elif kind == A_GATE:
                    act.activation(halves(agate[:, c, :]), ps, ACT.Copy).then_inc(out_sem, 1)
                hi(u + RING, idx % RING)

            def pack_tails(c):
                act.wait_ge(cin_used, c + 2)
                act.wait_ge(ax_used, c + 2)
                for (buf, w, n0, n1) in ((glu_pad, PAD_B, 0, 240), (cin_pad, PAD_C, 240, 360),
                                         (ax_pad, PAD_A, 360, 384), (dch_pad, PAD_D, 384, 400)):
                    ins = act.activation(steps(packed[:, n0:n1]), sa(buf, w, T, w), ACT.Copy)
                ins.then_inc(rows_packed, 1)

            def store_tails(c):
                act.wait_ge(tails_taken, c + 2)
                act.wait_ge(tails_stored, c * (9 * 16) + 1)
                act.activation(st_s[:, :], aux[0:120, 0, 0:3 * P], ACT.Copy)
                act.activation(st_p[:, :], aux[0:30, 1, 0:4 * P], ACT.Copy)
                act.activation(st_ax[:, :], aux[0:24, 2, 0:P], ACT.Copy)
                act.activation(st_sc[:, :], aux[0:16, 2, P:2 * P], ACT.Copy).then_inc(tails_out, 1)
                act.wait_ge(tails_out, c + 2)
                cols = ds(c * P, P)
                for dst, r0, r1, src in (
                        ("sample_cf", 0, 120, st_s[:, 0:P]), ("sample_cf", 120, 240, st_s[:, P:2 * P]),
                        ("sample_pool", 0, 120, st_s[:, 2 * P:3 * P]),
                        ("prompt_rgc", 0, 3, st_p[27:30, 0:P]), ("prompt_cf", 0, 30, st_p[:, P:2 * P]),
                        ("prompt_pool", 0, 15, st_p[15:30, 2 * P:3 * P]),
                        ("prompt_sc", 0, 2, st_p[28:30, 3 * P:4 * P]),
                        ("sample_rgc", 0, 24, st_ax[:, :]), ("sample_sc", 0, 16, st_sc[:, :])):
                    act.dma_start(rows3(o_[dst])[r0:r1, cols], src).then_inc(tails_stored, 16)

            for idx in range(2):
                in_tile(idx, 0)
            with act.Fori(0, KW - 1) as c:
                for idx in range(2, 8):
                    in_tile(idx, c)
                in_tile(0, c + 1)
                pack_tails(c)
                in_tile(1, c + 1)
                store_tails(c)
            for idx in range(2, 8):
                in_tile(idx, KW - 1)

            def gate(u, s, mm):
                act.wait_ge(unit_done, u + 1)
                act.activation(halves(sig[mm][:, :]), slot(0), ACT.Sigmoid).then_inc(tile_out[0], 1)
                hi(u + RING, s)

            def used(u, s):
                act.wait_ge(unit_done, u + 1)
                hi(u + RING, s)

            def side(j):
                if j < KW:
                    act.wait_ge(side_done, j + 1)
                    act.activation(halves(pool_t[:, j, :]), aslot(j % 2), ACT.Copy,
                                   scale=miscT[:, j, V_PSC:V_PSC + 1]).then_inc(side_out, 1)
                    act.wait_ge(side_out, j + 1)
                    act.activation(Y_C[:, j, :], pool_t[:, j, :], ACT.Copy).then_inc(yc_ready, 1)
                elif j % 2:
                    c = (j - KW) // 2
                    act.wait_ge(side_done, j + 1)
                    for s, dst, b in ((0, th, V_BA), (1, igate, V_BX)):
                        act.activation(halves(dst[:, c, :]), aslot(s), ACT.Sigmoid,
                                       bias=miscT[:, c, b:b + 1]).then_inc(side_out, 1)

            def pairs(q, i, tails=False, jobs=False, deviation=False):
                u = i * 4 + (U_MIX + 16 * q)
                gate(u, 0, 0)
                if tails:
                    pack_tails(KW - 1)
                if jobs:
                    side(4 * (i - 1))
                used(u + 1, 1)
                if jobs:
                    side(4 * (i - 1) + 1)
                if tails:
                    store_tails(KW - 1)
                if deviation:
                    act.wait_ge(bvar_ready, 1)
                    act.activation(b_std[:, :], b_std[:, :], ACT.Sqrt).then_inc(bstd_ready, 1)
                if q == 2:
                    act.wait_ge(bnorm_ready, i + 1)
                    act.activation(S[3][:, :], S[2][:, :], ACT.Sigmoid).then_inc(bsig_ready, 1)
                gate(u + 2, 2, 1)
                if jobs:
                    side(4 * (i - 1) + 2)
                used(u + 3, 3)
                if jobs:
                    side(4 * (i - 1) + 3)

            pairs(0, 0, tails=True)
            act.wait_ge(tile_out[1], U_MIX // 2 + 2)
            act.activation(bsq[:, :, :], bconv[:, :, :], ACT.Square).then_inc(bsq_ready, 1)
            act.wait_ge(tails_stored, 1 + 9 * 16 * KW)
            act.activation(agate[:, :, :], agate[:, :, :], ACT.Gelu_apprx_tanh).then_inc(gelu_ready, 1)
            for i in range(1, KD // 2):
                pairs(0, i, jobs=True)
            act.wait_ge(side_out, 3 * KW)
            for c in range(KW):
                act.activation(th[:, c, :], th[:, c, :], ACT.Tanh, scale=spv[:, 7, c:c + 1])\
                   .then_inc(th_ready, 1)
            act.wait_ge(th_ready, KW)
            act.wait_ge(yc_split, KW)
            act.activation(sq_th[:, :, :], th[:, :, :], ACT.Sqrt, bias=1e-30).then_inc(sqrt_ready, 1)
            pairs(1, 0, deviation=True)
            for q in range(1, 4):
                with act.Fori(1 if q == 1 else 0, KD // 2) as i:
                    pairs(q, i)
                if q == 2:
                    act.wait_ge(h_turned, 1)
                    act.activation(h_rows[:, :], aux[0:1 + B, 0, :], ACT.Copy).then_inc(h_copied, 1)

            def square(h, m):
                act.wait_ge(r_ready, h * KD + m + 1)
                if m >= 2:
                    act.wait_ge(sq_summed, h * (KD - 2) + max(1, m - 2))
                elif h == 1 and m == 0:
                    act.wait_ge(sq_summed, KD - 2)
                elif h == 1:
                    act.wait_ge(stat_done, 1)
                act.activation(rsq[m % 2][:, :], merged[:, m, h * HALF:(h + 1) * HALF], ACT.Square)\
                   .then_inc(rsq_ready, 1)

            def std(h):
                act.wait_ge(var_ready, h + 1)
                act.activation(std_h[:, :], std_h[:, :], ACT.Sqrt).then_inc(std_ready, 1)

            def affine(h, chunks):
                def part(buf, k):
                    return buf[:, k, h * HALF:(h + 1) * HALF]

                def x1_hi(k):
                    act.wait_ge(affine_ready, h * KD + k + 1)
                    act.activation(part(x_hi, k), part(merged, k), ACT.Copy).then_inc(x1_hi_ready, 1)

                for k in chunks:
                    act.wait_ge(norm_ready, h * KD + k + 1)
                    act.activation(part(merged, k), part(merged, k), ACT.Identity, scale=lnT[:, k:k + 1],
                                   bias=lnT[:, 8 + k:9 + k]).then_inc(affine_ready, 1)
                    if k > chunks[0]:
                        x1_hi(k - 1)
                x1_hi(chunks[-1])

            for m in range(KD):
                if m < RING:
                    act.wait_ge(raw_landed[m], ((U_OUT + RING) // RING) * 16 + 16)
                    act.activation(wx_hi[m][:, :, :], raw[m][:, :, :], ACT.Copy).then_inc(w_hi_ready, 1)
                square(0, m)
            for m in range(KD):
                if m < RING:
                    act.wait_ge(unit_done, U_OUT + m + 1)
                    hi(U_FF + m, m)
                square(1, m)
                if m == 0:
                    std(0)
                elif m <= 4:
                    affine(0, (2 * m - 2, 2 * m - 1))
            std(1)
            affine(1, range(KD))

            def ff_pair(i, mm, gate_slot):
                u = i * 4 + (U_FF + 2 * mm)
                act.wait_ge(unit_done, u + 1)
                act.activation(halves(S[mm][:, :]), gate_slot, ACT.Silu).then_inc(tile_out[0], 1)
                hi(u + RING, 2 * mm)
                used(u + 1, 2 * mm + 1)
                act.wait_ge(tile_out[1], i * 2 + (T_FF + mm + 2))
                act.activation(h_hi[:, i * 2 + mm, :], S[2 + mm][:, :], ACT.Copy).then_inc(hid_hi_ready, 1)

            for mm in range(2):
                ff_pair(0, mm, (slot, aslot)[mm](0))
            with act.Fori(1, KF // 2) as i:
                for mm in range(2):
                    ff_pair(i, mm, slot(0))

            def rows(m):
                act.wait_ge(rows_turned, m + 1)
                act.activation(r_tok[:, :, m * P:m * P + P],
                               aux[:, m % 2, :].rearrange("p (j n) -> p j n", j=NTILE), ACT.Copy)
                act.activation(rs_tok[:, m * P:m * P + P], aux[0:B * T, 2 + m % 2, 0:P], ACT.Copy)\
                   .then_inc(rows_out, 1)

            for m in range(KD):
                for part in range(3):
                    u = U_DOWN + 3 * m + part
                    if u + RING < U_END:
                        used(u, u % RING)
                if m >= 1:
                    rows(m - 1)
            act.wait_ge(rows_turned, KD)
            act.activation(r_tok[:, 0:2, D - P:D], aux[:, 1, 0:2 * P].rearrange("p (j n) -> p j n", j=2),
                           ACT.Copy).then_inc(rows_out, 1)
            for h, (j0, j1, j, cols) in enumerate(((0, 2, 1, slice(0, D)), (2, 5, 3, slice(D // 2, D)))):
                if h == 1:
                    act.wait_ge(rows_turned, KD + 1)
                    act.activation(r_tok[:, 2:4, D - P:D],
                                   aux[:, 1, 2 * P:4 * P].rearrange("p (j n) -> p j n", j=2), ACT.Copy)
                    act.activation(rs_tok[:, D - P:D], aux[0:B * T, 3, 0:P], ACT.Copy).then_inc(rows_out, 1)
                act.wait_ge(bn_var, h + 1)
                act.activation(bn_rs[:, j0:j1, 0:1], bn_mv[:, j0:j1, 1:2], ACT.Sqrt, bias=EPS)\
                   .then_inc(bn_std, 1)
                act.wait_ge(bn_scale, h + 1)
                t = r_tok[:, j, cols]
                act.activation(t, t, ACT.Identity, scale=bn_rs[:, j, 0:1], bias=bn_rs[:, j, 1:2])\
                   .then_inc(row_normed, 1)

        @block.tensor
        def _(pe):
            def passes(ps, pairs, last):
                n = len(pairs)
                for k, (wh, wl, xh, xl) in enumerate(pairs):
                    for j, (w, x) in enumerate(((wl, xh), (wh, xl), (wh, xh))):
                        for h in range(2):
                            mm = pe.matmul(ps[:, h, :], w, x[:, h * HALF:(h + 1) * HALF],
                                           start=(k == 0 and j == 0), stop=(last and k == n - 1 and j == 2))
                return mm

            def unit(u, s, xs, ps_slot, first=True, last=True, n0=0, ready=None):
                pe.wait_ge(w_lo_ready, u + 1)
                n = len(xs)
                for k, (xh, xl) in enumerate(xs):
                    if ready:
                        pe.wait_ge(ready, n0 + k + 1)
                    for j, (w, x) in enumerate(((w_lo, xh), (w_hi, xl), (w_hi, xh))):
                        for h in range(2):
                            mm = pe.matmul(slot(ps_slot)[:, h, :], w[s][:, k, :],
                                           x[:, h * HALF:(h + 1) * HALF],
                                           start=(first and k == 0 and j == 0),
                                           stop=(last and k == n - 1 and j == 2))
                mm.then_inc(unit_done, 1)

            pe.wait_ge(ident_ready, 1)
            pe.wait_ge(x_landed[4], 16)
            for k in range(KD):
                mm = pe.transpose(aux[:, 3, k * 32:k * 32 + 32], xs_tok[:, k * P:k * P + P],
                                  ident[0:32, 0:32])
            mm.then_inc(turned, 1)
            for j in range(SEQ // P):
                pe.wait_ge(x_landed[j], 16)
                for k in range(KD):
                    if j == 0 and k == KD - 1:
                        pe.wait_ge(x_lo_ready, 1)
                    bank = (main, aux)[k // 4]
                    mm = pe.transpose(bank[:, k % 4, j * P:j * P + P], x_tok[:, j, k * P:k * P + P],
                                      ident[:, :])
                    if j == SEQ // P - 1:
                        mm.then_inc(turned, 1)

            x_in = [(x_hi[:, k, :], x_lo[:, k, :]) for k in range(KD)]

            def in_tile(idx, c):
                pe.wait_ge(tile_out[idx % 2], c * 4 + (idx // 2 + 1))
                unit(c * 8 + idx, idx % RING, x_in, idx % 2)

            pe.wait_ge(x_lo_ready, 3)
            unit(0, 0, x_in, 0, ready=x_lo_ready, n0=1)
            pe.wait_ge(small_landed, 16 * N_SMALL)
            pe.wait_ge(x_lo_ready, KD + 1)
            for c in range(KW):
                pe.transpose(aux[:, 0, c * M_ROWS:(c + 1) * M_ROWS], misc_tok[:, c * P:c * P + P],
                             ident[0:M_ROWS, 0:M_ROWS])
            pe.transpose(aux[:, 0, KW * M_ROWS:KW * M_ROWS + 32], ln_tok[:, :], ident[0:32, 0:32])\
              .then_inc(turned, 1)
            for g in range(2):
                for c in range(2):
                    for half in range(2):
                        mm = pe.transpose(aux[:, 1 + g, c * 240 + half * 120:c * 240 + half * 120 + 120],
                                          conf_tok[:, half, (2 * g + c) * P:(2 * g + c + 1) * P],
                                          ident[0:120, 0:120])
                mm.then_inc(turned, 1)
            for c in range(KW):
                mm = pe.transpose(aux[:, 3, c * 120:c * 120 + 120], pool_tok[:, c * P:c * P + P],
                                  ident[0:120, 0:120])
            mm.then_inc(turned, 1)
            in_tile(1, 0)
            pe.wait_ge(misc_ready, 1)
            pe.wait_ge(tails_out, 1)
            pe.transpose(aux[:, 1, 0:P], ident[:, :], ident[:, :]).then_inc(tails_taken, 1)

            def turn_tails(c):
                pe.wait_ge(ax_used, c + 2)
                pe.wait_ge(tails_out, c + 1)
                for j, (buf, w) in enumerate(((ax_pad, PAD_A), (glu_pad, PAD_B), (cin_pad, PAD_C),
                                              (dch_pad, PAD_D))):
                    pe.transpose(aux[0:30, 1, j * P:j * P + P], buf[:, w + SEQ - 30:w + SEQ], ident[:, :])
                pe.wait_ge(rows_packed, c + 1)
                for j in range(3):
                    pe.transpose(aux[0:120, 0, j * P:j * P + P], packed[:, 120 * j:120 * j + 120], ident[:, :])
                pe.transpose(aux[0:24, 2, 0:P], packed[:, 360:384], ident[:, :])
                pe.transpose(aux[0:16, 2, P:2 * P], packed[:, 384:400], ident[:, :])\
                  .then_inc(tails_taken, 1)

            with pe.Fori(0, KW - 1) as c:
                for idx in range(2, 8):
                    in_tile(idx, c)
                for idx in range(2):
                    in_tile(idx, c + 1)
                turn_tails(c)
            for idx in range(2, 8):
                in_tile(idx, KW - 1)

            def side(j):
                if j == 0:
                    pe.wait_ge(sm_lo_ready, 1)
                if j < KW:
                    c, t, src = j, 2 * KW + j, Y_C
                    pe.wait_ge(yc_made, c + 1)
                else:
                    c = (j - KW) // 2
                    t, src = ((j - KW) % 2) * KW + c, Y_A
                    pe.wait_ge(ax_used, c + 2)
                if j >= 2:
                    pe.wait_ge(side_out, j - 1)
                passes(aslot(j % 2), [(sm_hi[:, t, :], sm_lo[:, t, :], src[:, c, :], src[:, KW + c, :])],
                       True).then_inc(side_done, 1)

            def b_sums():
                pe.wait_ge(bsq_summed, 1)
                for s, src in ((0, bsq[:, 1, :]), (1, bsq[:, 0, :])):
                    pe.wait_ge(side_out, 3 * KW - 1 + s)
                    for h in range(2):
                        mm = pe.matmul(aslot(s)[:, h, :], ones[:, :], src[:, h * HALF:(h + 1) * HALF],
                                       start=True, stop=True)
                    mm.then_inc(side_done, 1)

            def pairs(q, i, xs, branch_ready, tails=False, jobs=False, deviation=False):
                for mm_ in range(2):
                    u = i * 4 + (U_MIX + 16 * q + 2 * mm_)
                    t2_ = i * 2 + ((U_MIX + 16 * q) // 2 + mm_ + 1)
                    pe.wait_ge(tile_out[0], t2_)
                    unit(u, 2 * mm_, x_in, 0)
                    if deviation and mm_ == 0:
                        b_sums()
                    if jobs:
                        side(4 * (i - 1) + 2 * mm_)
                    pe.wait_ge(tile_out[1], t2_)
                    pe.wait_ge(branch_ready, KW)
                    unit(u + 1, 2 * mm_ + 1, xs, 1)
                    if tails and mm_ == 0:
                        turn_tails(KW - 1)
                    if jobs:
                        side(4 * (i - 1) + 2 * mm_ + 1)

            for q in range(4):
                yq = (Y_D, Y_C, Y_A, Y_D)[q]
                xs = [(yq[:, k, :], yq[:, KW + k, :]) for k in range(KW)]
                if q == 3:
                    for c in range(KW):
                        mm = pe.transpose(aux[0:1 + B, 0, c * P:c * P + P], h_last[:, c, :], ident[:, :])
                    mm.then_inc(h_turned, 1)
                branch_ready = (yd_ready, yc_split, ya_ready, yb_ready)[q]
                if q == 0:
                    for i in range(KD // 2):
                        pairs(0, i, xs, branch_ready, tails=(i == 0), jobs=(i > 0))
                    continue
                if q == 1:
                    pairs(1, 0, xs, branch_ready, deviation=True)
                with pe.Fori(1 if q == 1 else 0, KD // 2) as i:
                    pairs(q, i, xs, branch_ready)

            def half_unit(hi_w, lo_w, xs, bank, h, ready=None, n0=0, first=True, last=True):
                cols = slice(h * HALF, (h + 1) * HALF)
                for k, (xh, xl) in enumerate(xs):
                    if ready:
                        pe.wait_ge(ready, n0 + k + 1)
                    for j, (w, x) in enumerate(((lo_w, xh), (hi_w, xl), (hi_w, xh))):
                        mm = pe.matmul(bank, w[:, k, :], x[:, cols], start=(first and k == 0 and j == 0),
                                       stop=(last and k == len(xs) - 1 and j == 2))
                return mm

            def sums(h):
                pe.wait_ge(acc_ready, h + 1)
                pe.wait_ge(sq_summed, (h + 1) * (KD - 2))
                b0, b1 = aux[:, 2 * h, 0:HALF], aux[:, 2 * h + 1, 0:HALF]
                pe.matmul(b0, ones[:, :], acc_r[:, :], start=True, stop=False)
                pe.matmul(b1, ones[:, :], acc_q[:, :], start=True, stop=False)
                pe.wait_ge(r_ready, (h + 1) * KD)
                pe.matmul(b0, ones[:, :], merged[:, KD - 1, h * HALF:(h + 1) * HALF], start=False, stop=True)
                pe.wait_ge(rsq_ready, (h + 1) * KD)
                pe.matmul(b1, ones[:, :], rsq[(KD - 1) % 2][:, :], start=False, stop=True)\
                  .then_inc(stat_done, 1)

            xs = [(Y_C[:, k, :], Y_A[:, k, :]) for k in range(KD)]
            for slot_ in range(2):
                pe.wait_ge(tile_out[slot_], U_OUT // 2 + 1)
            for h in range(2):
                for m in range(KD):
                    step = h * KD + m
                    if step >= 4:
                        pe.wait_ge(half_out, step - 3)
                    if h == 0:
                        pe.wait_ge(w_lo_ready, U_OUT + m + 1)
                    w = (w_hi[m], w_lo[m]) if m < RING else (wx_hi[m - RING], wx_lo[m - RING])
                    half_unit(*w, xs, main[:, step % 4, 0:HALF], h,
                              ready=merged_ready if step == 0 else None)\
                        .then_inc((half_done, unit_done)[h], 1)
                    if step == KD:
                        sums(0)
            for h in range(2):
                for j in range(4):
                    if h == 0:
                        pe.wait_ge(w_lo_ready, U_FF + j + 1)
                        if j < 2:
                            pe.wait_ge(half_out, 2 * KD - 3 + 2 * j)
                    elif j < 2:
                        pe.wait_ge(half_out, 2 * KD - 2 + 2 * j)
                    if j >= 2:
                        pe.wait_ge(var_ready, 1 if j == 2 else 2)
                    bank = (main, aux)[j // 2][:, 2 * (j % 2) + h, 0:HALF]
                    mm = half_unit(w_hi[j], w_lo[j], x_in, bank, h,
                                   ready=x1_lo_ready if j == 0 else None, n0=h * KD)
                    if h == 1:
                        mm.then_inc(unit_done, 1)
                    if h == 0 and j == 0:
                        sums(1)
            with pe.Fori(0, KF // 2 - 1) as i:
                for j in range(2):
                    t2_ = i * 2 + (T_FF + 3 + j)
                    pe.wait_ge(tile_out[0], t2_)
                    unit(i * 4 + (U_FF + 4 + 2 * j), 2 * j, x_in, 0)
                    pe.wait_ge(tile_out[1], t2_)
                    unit(i * 4 + (U_FF + 5 + 2 * j), 1 + 2 * j, x_in, 1)

            def turn_rows(m):
                pe.wait_ge(r_ready, 2 * KD + m + 1)
                if m >= 2:
                    pe.wait_ge(rows_out, m - 1)
                r = S[m % 2]
                for j in range(NTILE):
                    pe.transpose(aux[:, m % 2, j * P:j * P + P], r[:, j * P:j * P + P], ident[:, :])
                pe.transpose(aux[0:B * T, 2 + m % 2, 0:P], r[:, SEQ:NT], ident[:, :]).then_inc(rows_turned, 1)

            pe.wait_ge(hid_lo_ready, KF - 1)
            for m in range(KD - 1):
                pe.wait_ge(tile_out[m % 2], T_DOWN + m // 2 + 1)
                k = 0
                for part, n in enumerate(DOWN_SPLIT):
                    u = U_DOWN + 3 * m + part
                    if m == 0 and part == 2:
                        pe.wait_ge(hid_lo_ready, KF)
                    unit(u, u % RING, [(h_hi[:, k + j, :], h_lo[:, k + j, :]) for j in range(n)], m % 2,
                         first=(part == 0), last=(part == 2))
                    k += n
                if m >= 1:
                    turn_rows(m - 1)
            pe.wait_ge(tile_out[1], T_DOWN + (KD - 1) // 2 + 1)
            for h in range(2):
                k = 0
                for part, n in enumerate(DOWN_SPLIT):
                    u = U_END - 3 + part
                    if h == 0:
                        pe.wait_ge(w_lo_ready, u + 1)
                    mm = half_unit(w_hi[u % RING], w_lo[u % RING],
                                   [(h_hi[:, k + j, :], h_lo[:, k + j, :]) for j in range(n)],
                                   main[:, 2 + h, 0:HALF], h, first=(part == 0), last=(part == 2))
                    k += n
                    if h == 1:
                        mm.then_inc(unit_done, 1)
                    elif part == 2:
                        mm.then_inc(last_half, 1)
                    if part == 0:
                        if h == 0:
                            turn_rows(KD - 2)
                        else:
                            pe.wait_ge(r_ready, 3 * KD)
                            pe.wait_ge(rows_out, KD - 2)
                            for j in range(2):
                                mm = pe.transpose(aux[:, 1, j * P:j * P + P], S[1][:, j * P:j * P + P],
                                                  ident[:, :])
                            mm.then_inc(rows_turned, 1)
            pe.wait_ge(r_ready, 3 * KD + 1)
            pe.wait_ge(rows_out, KD)
            for j in range(2, NTILE):
                pe.transpose(aux[:, 1, j * P:j * P + P], S[1][:, j * P:j * P + P], ident[:, :])
            pe.transpose(aux[0:B * T, 3, 0:P], S[1][:, SEQ:NT], ident[:, :]).then_inc(rows_turned, 1)

        @block.vector
        def _(ve):
            ch = Chain(ve, dve)
            link, after = ch.link, ch.after

            def vec(c, j):
                return miscT[:, c, j:j + 1]

            ve.wait_ge(x_hi_ready, 1)
            ve.tensor_tensor(x_lo[:, :, SEQ:NT], aux[:, 3, 0:256].rearrange("p (k n) -> p k n", k=KD),
                             x_hi[:, :, SEQ:NT].bitcast(F32), ALU.subtract).then_inc(x_lo_ready, 1)
            for k in range(KD):
                ve.wait_ge(x_hi_ready, k + 2)
                bank = (main, aux)[k // 4]
                ve.tensor_tensor(x_lo[:, k, 0:SEQ], bank[:, k % 4, :], x_hi[:, k, 0:SEQ].bitcast(F32),
                                 ALU.subtract).then_inc(x_lo_ready, 1)
            ve.wait_ge(turned, KD + 2)
            ve.tensor_copy(miscT[:, :, :], aux[:, 0, 0:KW * M_ROWS].rearrange("p (c n) -> p c n", c=KW))\
              .then_inc(misc_ready, 1)
            ve.tensor_copy(lnT[:, :], aux[:, 0, KW * M_ROWS:KW * M_ROWS + 32]).then_inc(tile_out[0], 1)
            ve.wait_ge(misc_ready, 1)
            lam = miscT[:, :, V_LAM:V_LAM + 1].rearrange("p c o -> p (c o)")
            after(link(ve.tensor_scalar(spv[:, 2, :], lam, -1.0, None, ALU.mult)))
            ve.tensor_tensor(spv[:, 0, :], lam, spv[:, 2, :], ALU.min).then_inc(lam_ready, 1)
            after(link(ve.tensor_scalar(spv[:, 3, :], spv[:, 2, :], 0.0, None, ALU.max)))
            ve.wait_ge(z_ready, 1)
            after(link(ve.tensor_scalar(spv[:, 4, :], spv[:, 1, :], 2.0, None, ALU.add)))
            after(link(ve.reciprocal(spv[:, 4, :], spv[:, 4, :])))
            after(link(ve.tensor_tensor(spv[:, 4, :], spv[:, 4, :], spv[:, 1, :], ALU.mult)))
            after(link(ve.tensor_tensor(spv[:, 5, :], spv[:, 4, :], spv[:, 4, :], ALU.mult)))
            after(link(ve.tensor_scalar(spv[:, 6, :], spv[:, 5, :], 1.0 / 17, None, ALU.mult)))
            for n in (15, 13, 11, 9, 7, 5, 3):
                after(link(ve.scalar_tensor_tensor(spv[:, 6, :], spv[:, 6, :], 1.0 / n, spv[:, 5, :],
                                                   ALU.add, ALU.mult)))
            after(link(ve.scalar_tensor_tensor(spv[:, 6, :], spv[:, 6, :], 1.0, spv[:, 4, :],
                                               ALU.add, ALU.mult)))
            after(link(ve.scalar_tensor_tensor(spv[:, 6, :], spv[:, 6, :], 2.0, spv[:, 3, :],
                                               ALU.mult, ALU.add)))
            after(link(ve.tensor_scalar(spv[:, 7, :], spv[:, 6, :], 4.0, None, ALU.mult)))
            ve.wait_ge(conf_ready, 1)
            ve.wait_ge(db_used, 1)

            def filter_taps(taps, src, w, out, out_s, weight, bias, state):
                for t in taps:
                    pin, sin = pr(src, w, t), sa(src, w, t)
                    if t == 0:
                        if bias is None:
                            state[0] = link(ve.tensor_scalar(out, pin, weight(0), None, ALU.mult))
                            state[1] = link(ve.tensor_scalar(out_s, sin, weight(0), None, ALU.mult))
                        else:
                            state[0] = link(ve.tensor_scalar(out, pin, weight(0), bias, ALU.mult, ALU.add))
                            state[1] = link(ve.tensor_scalar(out_s, sin, weight(0), bias, ALU.mult, ALU.add))
                    else:
                        after(state[0])
                        state[0] = link(ve.scalar_tensor_tensor(out, pin, weight(t), out, ALU.mult, ALU.add))
                        after(state[1])
                        state[1] = link(ve.scalar_tensor_tensor(out_s, sin, weight(t), out_s,
                                                                ALU.mult, ALU.add))

            def split(src, hi_ap, lo_ap):
                after(link(ve.tensor_copy(hi_ap, src)))
                return ve.tensor_tensor(lo_ap, src, hi_ap.bitcast(F32), ALU.subtract)

            with ve.Fori(0, KW) as c:
                ch.enter(c, PER_IN)
                ve.wait_ge(tails_taken, c + 1)
                link(ve.tensor_copy(sa(glu_pad, PAD_B, 0, PAD_B), steps(confT[:, c, :])))
                ve.wait_ge(tile_out[1], c * 4 + 2)
                ve.wait_ge(tile_out[0], c * 4 + 2)
                link(ve.tensor_tensor(glu_pad[:, PAD_B:PAD_B + SEQ], b_val[:, 0:SEQ], b_sig[:, 0:SEQ],
                                      ALU.mult))
                ve.tensor_tensor(sa(glu_pad, PAD_B, PAD_B), steps(b_val[:, SEQ:NT]), steps(b_sig[:, SEQ:NT]),
                                 ALU.mult).then_inc(glu_made, 1)
                ve.wait_ge(glu_made, c + 2)
                st_b = [None, None]
                conv_b = (glu_pad, PAD_B, bconv[:, c, 0:SEQ], steps(bconv[:, c, SEQ:NT]),
                          lambda t: vec(c, V_CFW + t), vec(c, V_CFB), st_b)
                filter_taps(range(0, CONF_TAPS_1), *conv_b)

                link(ve.tensor_copy(sa(dch_pad, PAD_D, 0, PAD_D), steps(miscT[:, c, M_SC:M_H])))
                ve.wait_ge(tile_out[0], c * 4 + 3)
                ve.wait_ge(unit_done, c * 8 + 4)
                dh = slot(1)
                link(ve.tensor_tensor(dch_pad[:, PAD_D:PAD_D + HALF], dh[:, 0, :], d_c[:, 0:HALF], ALU.mult))
                link(ve.tensor_tensor(dch_pad[:, PAD_D + HALF:PAD_D + SEQ], dh[:, 1, 0:SEQ - HALF],
                                      d_c[:, HALF:SEQ], ALU.mult))
                ve.tensor_tensor(sa(dch_pad, PAD_D, PAD_D), steps(dh[:, 1, SEQ - HALF:HALF]),
                                 steps(d_c[:, SEQ:NT]), ALU.mult).then_inc(tile_out[1], 1)
                ve.wait_ge(tile_out[1], c * 4 + 3)
                st_d = [None, None]
                filter_taps(range(SC_TAPS), dch_pad, PAD_D, acc[:, 0:SEQ], steps(acc[:, SEQ:NT]),
                            lambda t: vec(c, V_SCW + t), None, st_d)
                ve.wait_ge(tile_out[0], c * 4 + 4)
                after(st_d[1])
                ve.tensor_tensor(acc[:, :], acc[:, :], d_b[:, :], ALU.mult).then_inc(db_used, 1)
                ve.wait_ge(db_used, c + 2)
                split(acc[:, :], Y_D[:, c, :], Y_D[:, c + KW, :]).then_inc(yd_ready, 1)

                filter_taps(range(CONF_TAPS_1, CONF_TAPS_2), *conv_b)

                link(ve.tensor_copy(sa(ax_pad, PAD_A, 0, PAD_A), steps(miscT[:, c, M_CONV:M_SC])))
                ve.wait_ge(tile_out[0], c * 4 + 5)
                ve.wait_ge(yd_ready, c + 1)
                after(ch.base + ch.local)
                st_a = [None, None]
                filter_taps(range(RG_TAPS), ax_pad, PAD_A, xc[:, c, 0:SEQ], steps(xc[:, c, SEQ:NT]),
                            lambda t: vec(c, V_RGW + t), vec(c, V_RGB), st_a)
                after(st_a[1])
                after(link(ve.tensor_copy(Y_A[:, c, :], xc[:, c, :])))
                ve.tensor_tensor(Y_A[:, c + KW, :], xc[:, c, :], Y_A[:, c, :].bitcast(F32), ALU.subtract)\
                  .then_inc(ax_used, 1)
                filter_taps(range(CONF_TAPS_2, CF_TAPS), *conv_b)
                after(st_b[1])
            ch.leave(KW)

            def product(q, i, mm):
                u = i * 4 + (U_MIX + 16 * q + 2 * mm)
                ve.wait_ge(tile_out[0], i * 2 + ((U_MIX + 16 * q) // 2 + mm + 2))
                ve.wait_ge(unit_done, u + 2)
                m = i * 2 + mm
                if q == 0:
                    ve.tensor_tensor(halves(merged[:, m, :]), slot(1), halves(sig[mm][:, :]), ALU.mult)\
                      .then_inc(tile_out[1], 1)
                    return
                ve.tensor_tensor(halves(prod[:, :]), slot(1), halves(sig[mm][:, :]), ALU.mult)\
                  .then_inc(tile_out[1], 1)
                ve.wait_ge(tile_out[1], i * 2 + ((U_MIX + 16 * q) // 2 + mm + 2))
                v = link(ve.tensor_tensor(merged[:, m, :], merged[:, m, :], prod[:, :], ALU.add))
                after(v)
                if q == 3:
                    split(merged[:, m, :], Y_C[:, m, :], Y_A[:, m, :]).then_inc(merged_ready, 1)

            def recurrence(c):
                s_d, s_a, s_b, s_x = S
                after(link(ve.tensor_scalar(s_d[:, :], th[:, c, :], 1.0, None, ALU.add)))
                after(link(ve.reciprocal(s_d[:, :], s_d[:, :])))
                link(ve.tensor_scalar(s_a[:, :], s_d[:, :], 2.0, -1.0, ALU.mult, ALU.add))
                link(ve.tensor_tensor(s_b[:, :], sq_th[:, c, :], s_d[:, :], ALU.mult))
                after(link(ve.scalar_tensor_tensor(s_x[:, :], igate[:, c, :], 2.0, xc[:, c, :],
                                                   ALU.mult, ALU.mult)))
                after(link(ve.tensor_tensor(s_b[:, :], s_b[:, :], s_x[:, :], ALU.mult)))
                a0 = steps(s_a[:, SEQ:NT])[:, :, 0:1].rearrange("p b o -> p (b o)")
                b0 = steps(s_b[:, SEQ:NT])[:, :, 0:1].rearrange("p b o -> p (b o)")
                after(link(ve.tensor_tensor(s_x[:, 0:B], a0, miscT[:, c, M_H:M_H + B], ALU.mult)))
                link(ve.tensor_tensor(b0, b0, s_x[:, 0:B], ALU.add))
                after(link(ve.tensor_scalar(a0, a0, 0.0, None, ALU.mult)))
                after(link(ve.tensor_tensor_scan(s_x[:, :], s_a[:, :], s_b[:, :], 0.0, ALU.mult, ALU.add)))
                link(ve.tensor_copy(h_last[:, c, 0:1], s_x[:, SEQ - 1:SEQ]))
                link(ve.tensor_copy(h_last[:, c, 1:1 + B],
                                    steps(s_x[:, SEQ:NT])[:, :, T - 1:T].rearrange("p b o -> p (b o)")))
                after(link(ve.tensor_tensor(s_b[:, :], s_x[:, :], agate[:, c, :], ALU.mult)))
                after(link(ve.tensor_scalar(Y_A[:, c, :], s_b[:, :], 1.0, None, ALU.mult)))
                ve.tensor_tensor(Y_A[:, c + KW, :], s_b[:, :], Y_A[:, c, :].bitcast(F32), ALU.subtract)\
                    .then_inc(ya_ready, 1)
                ve.wait_ge(ya_ready, c + 1)

            def statistics(n, mean, var, prod2, sem_out):
                link(ve.tensor_scalar(halves(mean[:, :]), aslot(0), 1.0 / n, None, ALU.mult))
                after(ch.base + ch.local)
                after(link(ve.tensor_tensor(prod2[:, :], mean[:, :], mean[:, :], ALU.mult)))
                after(link(ve.scalar_tensor_tensor(halves(var[:, :]), aslot(1), 1.0 / n, halves(prod2[:, :]),
                                                   ALU.mult, ALU.subtract)))
                ve.tensor_scalar(var[:, :], var[:, :], 0.0, EPS, ALU.max, ALU.add).then_inc(sem_out, 1)

            ve.wait_ge(tails_taken, KW + 1)
            ve.wait_ge(yc_made, KW)
            for i in range(KD // 2):
                for mm in range(2):
                    product(0, i, mm)
                if i == 1:
                    for c in range(KW):
                        ve.wait_ge(yc_ready, c + 1)
                        ve.tensor_tensor(Y_C[:, c + KW, :], pool_t[:, c, :], Y_C[:, c, :].bitcast(F32),
                                         ALU.subtract).then_inc(yc_split, 1)
            for q in range(1, 4):
                if q == 1:
                    ve.wait_ge(side_done, 3 * KW + 2)
                    statistics(W, b_mean, b_std, b_tmp, bvar_ready)
                if q == 2:
                    ve.wait_ge(bstd_ready, 1)
                    after(link(ve.reciprocal(b_std[:, :], b_std[:, :])))
                ch.flush()
                with ve.Fori(0, KD // 2) as i:
                    ch.enter(i, (0, 2 + PER_REC, 2 + PER_B, 4)[q])
                    if q == 2:
                        t = bconv[:, i, :]
                        after(link(ve.tensor_tensor(t, t, b_mean[:, :], ALU.subtract)))
                        after(link(ve.tensor_tensor(t, t, b_std[:, :], ALU.mult)))
                        ve.tensor_scalar(S[2][:, :], t, vec(i, V_CFG), vec(i, V_CFLB), ALU.mult, ALU.add)\
                          .then_inc(bnorm_ready, 1)
                    product(q, i, 0)
                    if q == 1:
                        ve.wait_ge(sqrt_ready, 1)
                        ve.wait_ge(gelu_ready, 1)
                        recurrence(i)
                    product(q, i, 1)
                    if q == 2:
                        ve.wait_ge(bsig_ready, i + 1)
                        after(link(ve.tensor_tensor(bconv[:, i, :], S[2][:, :], S[3][:, :], ALU.mult)))
                        split(bconv[:, i, :], Y_D[:, i, :], Y_D[:, i + KW, :]).then_inc(yb_ready, 1)
                ch.leave(KD // 2)

            def residual(m, u_done, t_val, n0, out):
                ve.wait_ge(unit_done, u_done)
                ve.scalar_tensor_tensor(halves(S[2][:, :]), halves(x_lo[:, m, :].bitcast(F32)), ALPHA,
                                        slot(m % 2), ALU.mult, ALU.add).then_inc(tile_out[m % 2], 1)
                ve.wait_ge(tile_out[m % 2], t_val)
                ve.scalar_tensor_tensor(out, x_hi[:, m, :].bitcast(F32), ALPHA, S[2][:, :],
                                        ALU.mult, ALU.add).then_inc(r_ready, 1)
                ve.wait_ge(r_ready, n0 + m + 1)

            def residual_half(h, m):
                step, cols = h * KD + m, slice(h * HALF, (h + 1) * HALF)
                ve.wait_ge((half_done, unit_done)[h], (0, U_OUT)[h] + m + 1)
                ve.scalar_tensor_tensor(r_tmp[:, :], x_lo[:, m, cols].bitcast(F32), ALPHA,
                                        main[:, step % 4, 0:HALF], ALU.mult, ALU.add).then_inc(half_out, 1)
                ve.wait_ge(half_out, step + 1)
                ve.scalar_tensor_tensor(merged[:, m, cols], x_hi[:, m, cols].bitcast(F32), ALPHA, r_tmp[:, :],
                                        ALU.mult, ALU.add).then_inc(r_ready, 1)
                ve.wait_ge(r_ready, step + 1)
                if 1 <= m < KD - 1:
                    if h == 1 and m == 1:
                        ve.wait_ge(stat_done, 1)
                    before = merged[:, 0, cols] if m == 1 else acc_r[:, :]
                    ins = ve.tensor_tensor(acc_r[:, :], before, merged[:, m, cols], ALU.add)
                    if m == KD - 2:
                        ins.then_inc(acc_ready, 1)
                    else:
                        after(link(ins))

            def half_statistics(h):
                ve.wait_ge(stat_done, h + 1)
                b0, b1 = aux[:, 2 * h, 0:HALF], aux[:, 2 * h + 1, 0:HALF]
                after(link(ve.tensor_scalar(mean_h[:, :], b0, 1.0 / D, None, ALU.mult)))
                after(link(ve.tensor_tensor(tmp_h[:, :], mean_h[:, :], mean_h[:, :], ALU.mult)))
                after(link(ve.scalar_tensor_tensor(std_h[:, :], b1, 1.0 / D, tmp_h[:, :],
                                                   ALU.mult, ALU.subtract)))
                ve.tensor_scalar(std_h[:, :], std_h[:, :], 0.0, EPS, ALU.max, ALU.add).then_inc(var_ready, 1)

            def inverse(h):
                ve.wait_ge(std_ready, h + 1)
                after(link(ve.reciprocal(std_h[:, :], std_h[:, :])))

            def normalise(h, chunks):
                def part(k):
                    return merged[:, k, h * HALF:(h + 1) * HALF]

                centred = link(ve.tensor_tensor(part(chunks[0]), part(chunks[0]), mean_h[:, :], ALU.subtract))
                for k in chunks:
                    now = centred
                    if k != chunks[-1]:
                        centred = link(ve.tensor_tensor(part(k + 1), part(k + 1), mean_h[:, :], ALU.subtract))
                    after(now)
                    ve.tensor_tensor(part(k), part(k), std_h[:, :], ALU.mult).then_inc(norm_ready, 1)

            for m in range(KD):
                residual_half(0, m)
            for m in range(KD):
                residual_half(1, m)
                if m == 0:
                    half_statistics(0)
                elif m <= 4:
                    if m == 1:
                        inverse(0)
                    normalise(0, (2 * m - 2, 2 * m - 1))
            half_statistics(1)
            inverse(1)
            normalise(1, range(KD))
            ve.wait_ge(norm_ready, 2 * KD)
            ch.flush()

            def ff_product(i, mm, up_slot):
                f = i * 2 + mm
                ve.wait_ge(tile_out[0], i * 2 + (T_FF + mm + 2))
                ve.wait_ge(unit_done, i * 4 + (U_FF + 2 * mm + 2))
                ve.tensor_tensor(halves(S[2 + mm][:, :]), up_slot, halves(S[mm][:, :]), ALU.mult)\
                  .then_inc(tile_out[1], 1)
                ve.wait_ge(tile_out[1], i * 2 + (T_FF + mm + 2))
                ve.wait_ge(hid_hi_ready, f + 1)
                ve.tensor_tensor(h_lo[:, f, :], S[2 + mm][:, :], h_hi[:, f, :].bitcast(F32), ALU.subtract)\
                  .then_inc(hid_lo_ready, 1)
                ve.wait_ge(hid_lo_ready, f + 1)

            for mm in range(2):
                ff_product(0, mm, (slot, aslot)[mm](1))
            with ve.Fori(1, KF // 2) as i:
                for mm in range(2):
                    ff_product(i, mm, slot(1))

            def row_statistics(m):
                ve.wait_ge(rows_out, m + 1)
                for j in range(NTILE):
                    link(ve.bn_stats(bn[:, j, m, :], r_tok[:, j, m * P:m * P + P]))
                link(ve.bn_stats(bn[0:B * T, NTILE, m, :], rs_tok[:, m * P:m * P + P]))

            for m in range(KD - 1):
                if m >= 2:
                    ve.wait_ge(rows_turned, m - 1)
                residual(m, U_DOWN + 3 * m + 3, T_DOWN + m // 2 + 2, 2 * KD, S[m % 2][:, :])
                if m >= 1:
                    row_statistics(m - 1)

            def residual_last(h):
                cols = slice(h * HALF, (h + 1) * HALF)
                ve.scalar_tensor_tensor(S[2][:, cols], x_lo[:, KD - 1, cols].bitcast(F32), ALPHA,
                                        main[:, 2 + h, 0:HALF], ALU.mult, ALU.add).then_inc(last_out, 1)
                ve.wait_ge(last_out, h + 1)
                ve.scalar_tensor_tensor(S[1][:, cols], x_hi[:, KD - 1, cols].bitcast(F32), ALPHA, S[2][:, cols],
                                        ALU.mult, ALU.add).then_inc(r_ready, 1)

            def last_statistics(h, j0, j1):
                ve.wait_ge(rows_out, KD + h)
                for j in range(j0, j1):
                    q = P if j < NTILE else B * T
                    t = r_tok[:, j, D - P:D] if j < NTILE else rs_tok[:, D - P:D]
                    link(ve.bn_stats(bn[0:q, j, KD - 1, :], t))
                after(ch.base + ch.local)
                for j in range(j0, j1):
                    q = P if j < NTILE else B * T
                    ins = ve.bn_aggr(bn_mv[0:q, j, :], bn[0:q, j, :, :].rearrange("p k s -> p (k s)"))
                    if j < j1 - 1:
                        link(ins)
                ins.then_inc(bn_var, 1)
                ve.wait_ge(bn_std, h + 1)
                after(link(ve.reciprocal(bn_rs[:, j0:j1, 0:1], bn_rs[:, j0:j1, 0:1])))
                ve.scalar_tensor_tensor(bn_rs[:, j0:j1, 1:2], bn_mv[:, j0:j1, 0:1], -1.0,
                                        bn_rs[:, j0:j1, 0:1], ALU.mult, ALU.mult).then_inc(bn_scale, 1)
                ve.wait_ge(bn_scale, h + 1)

            def finish(t, q, j, cols):
                after(link(ve.scalar_tensor_tensor(t, t, bn_mv[0:q, j, 0:1], g_row[0:q, cols],
                                                   ALU.subtract, ALU.mult)))
                ve.scalar_tensor_tensor(t, t, bn_rs[0:q, j, 0:1], b_row[0:q, cols], ALU.mult, ALU.add)\
                  .then_inc(rows_ready, 1)

            ve.wait_ge(rows_turned, KD - 2)
            ve.wait_ge(last_half, 1)
            residual_last(0)
            row_statistics(KD - 2)
            ve.wait_ge(bn_zero, 1)
            last_statistics(0, 0, 2)
            ve.wait_ge(row_vecs, 32)
            finish(r_tok[:, 0, :], P, 0, slice(0, D))
            ve.wait_ge(unit_done, U_END)
            residual_last(1)
            last_statistics(1, 2, NTILE + 1)
            finish(r_tok[:, 2, :], P, 2, slice(0, D))
            finish(rs_tok[:, :], B * T, NTILE, slice(0, D))
            finish(r_tok[:, 3, 0:D // 2], P, 3, slice(0, D // 2))


N_SMALL = 21
PER_IN = 84
PER_REC = 14
PER_B = 4

_INS = ["x_prompt", "x_sample", "state_rglru_h", "state_rglru_conv", "state_conformer_conv", "state_pool",
        "state_shortconv", "w_in", "rg_conv_w", "rg_conv_b", "rg_w_a", "rg_b_a", "rg_w_x", "rg_b_x",
        "rg_lambda", "cf_conv_w", "cf_conv_b", "cf_ln_g", "cf_ln_b", "pool_w", "pool_scale", "sc_conv_w",
        "w_branch", "w_out", "ln1_g", "ln1_b", "w_ff_gate", "w_ff_up", "w_ff_down", "ln2_g", "ln2_b"]
_OUTS = [("y_prompt", (1, SEQ, D)), ("y_sample", (B, T, D)),
         ("prompt_h", (1, 1, W)), ("prompt_rgc", (1, 1, 3, W)), ("prompt_cf", (1, 1, 30, W)),
         ("prompt_pool", (1, 1, 15, W)), ("prompt_sc", (1, 1, 2, W)),
         ("sample_h", (1, B, W)), ("sample_rgc", (1, B, 3, W)), ("sample_cf", (1, B, 30, W)),
         ("sample_pool", (1, B, 15, W)), ("sample_sc", (1, B, 2, W))]


def kernel(**inputs):
    import numpy as _np
    import concourse.bacc as _bacc
    from concourse.bass_utils import run_bass_kernel_spmd as _run

    nc = _bacc.Bacc("TRN2", target_bir_lowering=False, num_devices=1, dynamic_dma_scratch_size=1024)
    arrays, ins, outs = {}, {}, {}
    for name in _INS:
        a = _np.ascontiguousarray(inputs[name])
        arrays[f"in_{name}"] = a
        ins[name] = nc.dram_tensor(f"in_{name}", a.shape, mybir.dt.from_np(a.dtype), kind="ExternalInput").ap()
    for name, shape in _OUTS:
        outs[name] = nc.dram_tensor(f"out_{name}", shape, F32, kind="ExternalOutput").ap()
    build(nc, ins, outs)
    r = _run(nc, [arrays], core_ids=[0])
    return tuple(r.results[0][f"out_{name}"] for name, _ in _OUTS)
```
